# Optimizing a Trainium2 kernel written in Bass

```python
import jax, jax.numpy as jnp
from jax import lax
import numpy as np

D_MODEL = 1024
BATCH = 1
SEQ = 512
DEPTH = 1

CHUNK = 64
CONV_WIDTH = 512
CONV_KERNEL = 31
RWKV_WIDTH = 512
RWKV_HEAD = 64
RWKV_HEADS = RWKV_WIDTH // RWKV_HEAD
LORA_W = 64
LORA_A = 64
LORA_G = 128
N_EXPERTS = 64
TOP_K = 8
N_GROUPS = 8
TOPK_GROUPS = 4
D_EXPERT = 256
D_SHARED = 256
ROUTED_SCALE = 2.5
EXPERT_BLOCK = 256
RMS_EPS = 1e-6
LN_EPS = 1e-5
GN_EPS = 64e-5

COL_CONV = 2 * CONV_WIDTH
COL_RWKV = 3 * RWKV_WIDTH + LORA_W + LORA_A + LORA_G
COL_GATE = 2 * D_MODEL
D_IN = COL_CONV + COL_RWKV + COL_GATE

kernel_name = 'hybrid_conv_rwkv7_moe_stream_encoder'

def rmsnorm(x, g):
    x32 = x.astype(jnp.float32)
    y = x32 * lax.rsqrt(jnp.mean(x32 * x32, axis=-1, keepdims=True) + RMS_EPS)
    return (y * g.astype(jnp.float32)).astype(x.dtype)

def layernorm(x, g, b):
    x32 = x.astype(jnp.float32)
    mu = jnp.mean(x32, axis=-1, keepdims=True)
    var = jnp.mean(jnp.square(x32 - mu), axis=-1, keepdims=True)
    y = (x32 - mu) * lax.rsqrt(var + LN_EPS) * g.astype(jnp.float32) + b.astype(jnp.float32)
    return y.astype(x.dtype)

def conformer_conv(zc, conv_w, conv_b, ln_g, ln_b, p_conv):
    u = zc[..., :CONV_WIDTH] * jax.nn.sigmoid(zc[..., CONV_WIDTH:])
    u = lax.conv_general_dilated(
        u, conv_w[:, None, :], window_strides=(1,),
        padding=[(CONV_KERNEL - 1, 0)],
        dimension_numbers=('NWC', 'WIO', 'NWC'),
        feature_group_count=CONV_WIDTH) + conv_b
    u = jax.nn.silu(layernorm(u, ln_g, ln_b))
    return u @ p_conv

def rwkv7_time_mix(zr, mu, w0, w2, a0, a2, g2, k_k, k_a, r_k, gn_g, gn_b, p_rwkv):
    B, S, _ = zr.shape
    f32 = jnp.float32
    prev = jnp.pad(zr, ((0, 0), (1, 0), (0, 0)))[:, :S]
    zr = zr + (prev - zr) * mu
    RW = RWKV_WIDTH
    r, k, v, wd, ad, gd = jnp.split(
        zr, [RW, 2 * RW, 3 * RW, 3 * RW + LORA_W, 3 * RW + LORA_W + LORA_A], axis=-1)
    w = -jax.nn.softplus(-(w0 + jnp.tanh(wd) @ w2)) - 0.5
    decay = jnp.exp(-jnp.exp(w.astype(f32)))
    a = jax.nn.sigmoid(a0 + ad @ a2)
    g = jax.nn.sigmoid(gd) @ g2
    kk = k * k_k
    k = k * (1.0 + (a - 1.0) * k_a)

    def heads(t):
        return t.astype(f32).reshape(B, S, RWKV_HEADS, RWKV_HEAD)

    r, k, v, kk, a, decay = (heads(t) for t in (r, k, v, kk, a, decay))
    kk = kk * lax.rsqrt(jnp.maximum(jnp.sum(kk * kk, axis=-1, keepdims=True), 1e-24))

    def step(state, inp):
        r_t, w_t, k_t, v_t, kk_t, a_t = inp
        sa = jnp.einsum('bhvk,bhk->bhv', state, -kk_t)
        state = (state * w_t[:, :, None, :]
                 + sa[..., None] * (kk_t * a_t)[:, :, None, :]
                 + v_t[..., None] * k_t[:, :, None, :])
        y_t = jnp.einsum('bhvk,bhk->bhv', state, r_t)
        return state, y_t

    xs = tuple(jnp.moveaxis(t, 1, 0) for t in (r, decay, k, v, kk, a))
    state0 = jnp.zeros((B, RWKV_HEADS, RWKV_HEAD, RWKV_HEAD), f32)
    _, y = lax.scan(step, state0, xs)
    y = jnp.moveaxis(y, 0, 1)
    mu_y = jnp.mean(y, axis=-1, keepdims=True)
    var_y = jnp.mean(jnp.square(y - mu_y), axis=-1, keepdims=True)
    y = ((y - mu_y) * lax.rsqrt(var_y + GN_EPS)).reshape(B, S, RW)
    y = y * gn_g.astype(f32) + gn_b.astype(f32)
    y = y + (jnp.sum(r * k * r_k.astype(f32), axis=-1, keepdims=True) * v).reshape(B, S, RW)
    return (y.astype(zr.dtype) * g) @ p_rwkv

def mixing_sublayer(h, w_in, mu_shift, conv_w, conv_b, conv_ln_g, conv_ln_b, p_conv,
                    w0, w2, a0, a2, g2, k_k, k_a, r_k, gn_g, gn_b, p_rwkv, w_o):
    z = h @ w_in
    zc, zr, zg = jnp.split(z, [COL_CONV, COL_CONV + COL_RWKV], axis=-1)
    y_conv = conformer_conv(zc, conv_w, conv_b, conv_ln_g, conv_ln_b, p_conv)
    y_rwkv = rwkv7_time_mix(zr, mu_shift, w0, w2, a0, a2, g2, k_k, k_a, r_k, gn_g, gn_b, p_rwkv)
    g_conv, g_rwkv = jnp.split(jax.nn.sigmoid(zg), 2, axis=-1)
    return (g_conv * y_conv + g_rwkv * y_rwkv) @ w_o

def moe_ffn(h, w_router, b_router, we_gate, we_up, we_down, ws_gate, ws_up, ws_down):
    B, S, D = h.shape
    t = h.reshape(-1, D)
    n = t.shape[0]
    f32 = jnp.float32
    per_grp = N_EXPERTS // N_GROUPS
    scores = jax.nn.sigmoid((t @ w_router).astype(f32))
    biased = scores + b_router.astype(f32)
    grp_score = lax.top_k(biased.reshape(n, N_GROUPS, per_grp), 2)[0].sum(-1)
    _, top_grp = lax.top_k(grp_score, TOPK_GROUPS)
    grp_mask = jnp.any(top_grp[:, :, None] == jnp.arange(N_GROUPS), axis=1)
    masked = jnp.where(jnp.repeat(grp_mask, per_grp, axis=1), biased, -jnp.inf)
    _, idx = lax.top_k(masked, TOP_K)
    sel = jnp.take_along_axis(scores, idx, axis=1)
    gate = sel / jnp.sum(sel, axis=-1, keepdims=True) * ROUTED_SCALE

    n_assign = n * TOP_K
    flat_e = idx.reshape(-1)
    order = jnp.argsort(flat_e)
    e_sorted = flat_e[order]
    tok = order // TOP_K
    counts = jnp.bincount(flat_e, length=N_EXPERTS)
    padded = (counts + EXPERT_BLOCK - 1) // EXPERT_BLOCK * EXPERT_BLOCK
    pad_end = jnp.cumsum(padded)
    pad_start = pad_end - padded
    start = jnp.cumsum(counts) - counts
    dest = pad_start[e_sorted] + jnp.arange(n_assign) - start[e_sorted]
    n_blocks = -(-n_assign // EXPERT_BLOCK) + N_EXPERTS
    buf = jnp.zeros((n_blocks * EXPERT_BLOCK, D), t.dtype).at[dest].set(t[tok])
    blk_expert = jnp.minimum(
        jnp.searchsorted(pad_end, jnp.arange(n_blocks) * EXPERT_BLOCK, side='right'),
        N_EXPERTS - 1)

    def expert_block(args):
        xb, e = args
        return (jax.nn.silu(xb @ we_gate[e]) * (xb @ we_up[e])) @ we_down[e]

    yb = lax.map(expert_block, (buf.reshape(n_blocks, EXPERT_BLOCK, D), blk_expert))
    y = yb.reshape(-1, D)[dest] * gate.reshape(-1)[order][:, None].astype(t.dtype)
    routed = jax.ops.segment_sum(y, tok, num_segments=n)
    shared = (jax.nn.silu(t @ ws_gate) * (t @ ws_up)) @ ws_down
    return (routed + shared).reshape(B, S, D)

def setup_inputs(seed: int = 0) -> dict:
    key = jax.random.key(seed)
    keys = jax.random.split(key, 40)
    counter = [0]

    def nk():
        k = keys[counter[0]]
        counter[0] += 1
        return k

    def nrm(shape, scale):
        return jax.random.normal(nk(), shape, jnp.float32) * scale

    def gain(shape):
        return 1.0 + nrm(shape, 0.05)

    L, D, CW, RW = DEPTH, D_MODEL, CONV_WIDTH, RWKV_WIDTH
    return {
        'x': nrm((BATCH, SEQ, D), 1.0),
        'c': nrm((BATCH, D), 1.0),
        'w_ada': nrm((L, D, 6 * D), 0.5 * D ** -0.5),
        'b_ada': nrm((L, 6 * D), 0.02),
        'norm_mix_pre': gain((L, D)),
        'norm_mix_post': gain((L, D)),
        'norm_ffn_pre': gain((L, D)),
        'norm_ffn_post': gain((L, D)),
        'w_in': nrm((L, D, D_IN), D ** -0.5),
        'mu_shift': jax.random.uniform(nk(), (L, COL_RWKV), jnp.float32),
        'conv_w': nrm((L, CONV_KERNEL, CW), CONV_KERNEL ** -0.5),
        'conv_b': nrm((L, CW), 0.02),
        'conv_ln_g': gain((L, CW)),
        'conv_ln_b': nrm((L, CW), 0.02),
        'p_conv': nrm((L, CW, D), CW ** -0.5),
        'w0': nrm((L, RW), 1.0) - 1.5,
        'w2': nrm((L, LORA_W, RW), LORA_W ** -0.5),
        'a0': nrm((L, RW), 0.5),
        'a2': nrm((L, LORA_A, RW), 0.5 * LORA_A ** -0.5),
        'g2': nrm((L, LORA_G, RW), LORA_G ** -0.5),
        'k_k': 0.85 + nrm((L, RW), 0.05),
        'k_a': gain((L, RW)),
        'r_k': nrm((L, RWKV_HEADS, RWKV_HEAD), 0.1),
        'gn_g': gain((L, RW)),
        'gn_b': nrm((L, RW), 0.02),
        'p_rwkv': nrm((L, RW, D), RW ** -0.5),
        'w_o': nrm((L, D, D), D ** -0.5),
        'w_router': nrm((L, D, N_EXPERTS), D ** -0.5),
        'b_router': nrm((L, N_EXPERTS), 0.01),
        'we_gate': nrm((L, N_EXPERTS, D, D_EXPERT), D ** -0.5),
        'we_up': nrm((L, N_EXPERTS, D, D_EXPERT), D ** -0.5),
        'we_down': nrm((L, N_EXPERTS, D_EXPERT, D), D_EXPERT ** -0.5),
        'ws_gate': nrm((L, D, D_SHARED), D ** -0.5),
        'ws_up': nrm((L, D, D_SHARED), D ** -0.5),
        'ws_down': nrm((L, D_SHARED, D), D_SHARED ** -0.5),
    }

def reference(x, c, w_ada, b_ada, norm_mix_pre, norm_mix_post, norm_ffn_pre, norm_ffn_post,
              w_in, mu_shift, conv_w, conv_b, conv_ln_g, conv_ln_b, p_conv,
              w0, w2, a0, a2, g2, k_k, k_a, r_k, gn_g, gn_b, p_rwkv, w_o,
              w_router, b_router, we_gate, we_up, we_down, ws_gate, ws_up, ws_down):
    for l in range(DEPTH):
        mod = jax.nn.silu(c) @ w_ada[l] + b_ada[l]
        sh1, sc1, gt1, sh2, sc2, gt2 = (m[:, None, :] for m in jnp.split(mod, 6, axis=-1))
        h = rmsnorm(x, norm_mix_pre[l]) * (1.0 + sc1) + sh1
        y = mixing_sublayer(h, w_in[l], mu_shift[l], conv_w[l], conv_b[l], conv_ln_g[l],
                            conv_ln_b[l], p_conv[l], w0[l], w2[l], a0[l], a2[l], g2[l],
                            k_k[l], k_a[l], r_k[l], gn_g[l], gn_b[l], p_rwkv[l], w_o[l])
        x = x + gt1 * rmsnorm(y, norm_mix_post[l])
        h = rmsnorm(x, norm_ffn_pre[l]) * (1.0 + sc2) + sh2
        y = moe_ffn(h, w_router[l], b_router[l], we_gate[l], we_up[l], we_down[l],
                    ws_gate[l], ws_up[l], ws_down[l])
        x = x + gt2 * rmsnorm(y, norm_ffn_post[l])
    return x


_drawn_inputs = setup_inputs


def setup_inputs(seed=0):
    import zlib

    import numpy as np

    out = dict(_drawn_inputs(seed))
    spreads = {}
    factors = {'norm_ffn_post': 4.123, 'conv_b': 2.874, 'conv_ln_b': 3.646, 'k_k': 3.247, 'gn_b': 5.184}
    for name, (base, spread) in spreads.items():
        noise = np.random.default_rng([zlib.crc32(name.encode()), seed]).standard_normal(out[name].shape)
        drawn = base * np.exp(spread * noise) if base else spread * noise
        out[name] = __import__('jax').numpy.asarray(drawn.astype(out[name].dtype))
    for name, factor in factors.items():
        out[name] = (out[name] * factor).astype(out[name].dtype)
    return out
```

```python
from contextlib import ExitStack

import concourse.bass as bass
from concourse import mybir

F32 = mybir.dt.float32
I32 = mybir.dt.int32
U32 = mybir.dt.uint32
ALU = mybir.AluOpType
ACT = mybir.ActivationFunctionType
AX = mybir.AxisListType

P = 128
D = 1024
S = 512
KD = D // P
NT = S // P
CW = 512
CK = 31
RW = 512
RT_ = RW // P
HEADS, HD = 8, 64
LORA_W, LORA_A, LORA_G = 64, 64, 128
COL_CONV = 2 * CW
COL_RWKV = 3 * RW + LORA_W + LORA_A + LORA_G
COL_GATE = 2 * D
NE, NG, PER, TOPK, TOPG = 64, 8, 8, 8, 4
DE = 256
SCALE = 2.5
RMS_EPS, LN_EPS, GN_EPS = 1e-6, 1e-5, 64e-5
DECAY = float(0.6065306597126334)
N = 512


class Link:

    def __init__(self, engine, semaphore):
        self.engine, self.semaphore, self.count = engine, semaphore, 0

    def sign(self, instruction):
        self.count += 1
        instruction.then_inc(self.semaphore, 1)
        return self.count

    def wait(self, count=None):
        self.engine.wait_ge(self.semaphore, self.count if count is None else count)

    def __call__(self, instruction):
        self.sign(instruction)
        self.wait()


class Memory:

    def __init__(self, nc, stack):
        self.nc, self.stack, self.semaphores = nc, stack, []

    def sb(self, name, shape, dtype=F32):
        return self.stack.enter_context(self.nc.sbuf_tensor(name, shape, dtype))

    def bank(self, name, shape=None):
        return self.stack.enter_context(self.nc.psum_tensor(name, shape or [P, N], F32))

    def sem(self, name):
        self.semaphores.append(self.nc.alloc_semaphore(name=name))
        return self.semaphores[-1]

    def reset_semaphores(self):
        self.nc.clear_and_free_semaphores(self.semaphores)
        self.nc.all_engine_barrier()




VEC_ROWS = [("mu_shift", COL_RWKV // P), ("conv_b", 4), ("conv_ln_g", 4), ("conv_ln_b", 4), ("w0", 4),
            ("a0", 4), ("k_k", 4), ("k_a", 4), ("r_k", 4), ("gn_g", 4), ("gn_b", 4), ("c", KD)]
VEC_AT = {}
_row = 0
for _name, _count in VEC_ROWS:
    VEC_AT[_name] = _row
    _row += _count
N_VEC = _row
N_TAP = CK * (CW // P)
GAINS = ["norm_mix_pre", "norm_mix_post", "norm_ffn_pre", "norm_ffn_post"]
ADA = 6 * D // N
N_WIDE = ADA + 2 * len(GAINS)

IN_SLICES = ([(COL_CONV + o, min(N, COL_RWKV - o)) for o in range(0, COL_RWKV, N)]
             + [(o, N) for o in range(0, COL_CONV, N)]
             + [(COL_CONV + COL_RWKV + o, N) for o in range(0, COL_GATE, N)])
STREAM = [("ada", i) for i in range(4)]
_ada = 4
for _i in range(len(IN_SLICES)):
    STREAM.append(("in", _i))
    if _i >= 1 and _ada < ADA:
        STREAM.append(("ada", _ada))
        _ada += 1
while _ada < ADA:
    STREAM.append(("ada", _ada))
    _ada += 1
STREAM_AT = {item: n for n, item in enumerate(STREAM)}
RING1 = 4
Z_TILES = [(s, t) for s, (_, w) in enumerate(IN_SLICES) for t in range(w // P)]
NZ_RWKV, NZ_CONV, NZ_GATE = COL_RWKV // P, COL_CONV // P, COL_GATE // P


def project(nc, w, keep, mix):
    with ExitStack() as stack:
        m = Memory(nc, stack)
        ring = m.sb("ring1", [P, RING1, KD, N])
        x = m.sb("x1", [P, NT, D])
        hT = m.sb("hT", [P, KD, S])
        upad = m.sb("upad", [P, RT_, CK - 1 + S])
        acc = m.sb("ada_acc", [P, 2, N])
        vrows = m.sb("vrows", [N_VEC, P])
        trows = m.sb("trows", [N_TAP, P])
        wide = m.sb("wide", [N_WIDE, N])
        mean_sq = m.sb("mean_sq", [P, NT])
        rstd = m.sb("rstd1", [P, NT])
        sums = m.sb("sums1", [P, NT])
        pz = [m.bank(f"pz{i}") for i in range(3)]
        pt = [m.bank(f"pt{i}") for i in range(2)]
        pm, pg = m.bank("pm"), m.bank("pg")
        glu = x[:, 0, :].rearrange("p (b n) -> p b n", b=2)
        vec, taps = keep.vec, mix.taps

        s_const = m.sem("p1_const")
        s_vrows = m.sem("p1_vrows_in")
        s_x = m.sem("p1_x_in")
        s_slot = [m.sem(f"p1_slot{i}_in") for i in range(RING1)]
        s_vecT = m.sem("p1_vec_turned")
        s_vec = m.sem("p1_vec_ready")
        s_silu = m.sem("p1_c_ready")
        s_sq = m.sem("p1_squares")
        s_rstd = m.sem("p1_rstd")
        s_ada = m.sem("p1_ada_partial")
        s_adam = m.sem("p1_ada_summed")
        s_adag = m.sem("p1_gain_copied")
        s_mod = m.sem("p1_mod_row")
        s_h = m.sem("p1_h_rows")
        s_ht = m.sem("p1_h_turned")
        s_hA = m.sem("p1_hT_by_scalar")
        s_hV = m.sem("p1_hT_by_vector")
        s_z = m.sem("p1_z")
        s_zA = m.sem("p1_z_taken_by_scalar")
        s_zV = m.sem("p1_z_taken_by_vector")
        s_v = m.sem("p1_vector_chain")
        s_a = m.sem("p1_scalar_chain")
        s_glu = m.sem("p1_glu")
        block = stack.enter_context(nc.Block())

        def vcol(name, i=0):
            return vec[:, VEC_AT[name] + i:VEC_AT[name] + i + 1]

        def slot_wait(engine, item):
            n = STREAM_AT[item]
            engine.wait_ge(s_slot[n % RING1], 16 * (n // RING1 + 1))

        z_end, total = [], 0
        for _, width in IN_SLICES:
            total += width // P
            z_end.append(total)

        def free_wait(engine, item):
            kind, i = item
            if kind == "ada":
                engine.wait_ge(s_ada, i + 1)
            else:
                engine.wait_ge(s_z, z_end[i])

        @block.sync
        def _(sp):
            for n, (kind, i) in enumerate(STREAM):
                if n == 2:
                    sp.dma_start(x[:, :, :], w["x"][0].rearrange("(t p) d -> p t d", p=P)).then_inc(s_x, 16)
                if n >= RING1:
                    free_wait(sp, STREAM[n - RING1])
                if kind == "ada":
                    at, width, source = i * N, N, w["w_ada"][0]
                else:
                    (at, width), source = IN_SLICES[i], w["w_in"][0]
                sp.dma_start(ring[:, n % RING1, :, 0:width],
                             source[:, at:at + width].rearrange("(k p) n -> p k n", p=P)).then_inc(
                                 s_slot[n % RING1], 16)

        @block.gpsimd
        def _(pool):
            pool.memset(keep.ident[:, :], 0.0).then_inc(s_const, 1)
            pool.memset(keep.ones[:, :], 1.0).then_inc(s_const, 1)
            pool.memset(keep.power[:, :], -0.5).then_inc(s_const, 1)
            pool.memset(upad[:, :, 0:CK - 1], 0.0).then_inc(s_const, 1)
            pool.wait_ge(s_const, 4)
            pool.affine_select(out=keep.ident[:, :], in_=keep.ident[:, :], compare_op=ALU.not_equal, fill=1.0,
                               base=0, pattern=[[-1, P]], channel_multiplier=1).then_inc(s_const, 1)
            pool.wait_ge(s_sq, 1)
            pool.tensor_tensor(rstd[:, :], mean_sq[:, :], keep.power[:, 0:NT], ALU.pow).then_inc(s_rstd, 1)

        @block.scalar
        def _(act):
            link = Link(act, s_a)
            for name, count in VEC_ROWS:
                r = VEC_AT[name]
                src = w[name] if name == "c" else w[name][0]
                if name == "r_k":
                    src = src.rearrange("h d -> (h d)")
                elif name == "c":
                    src = src[0]
                act.dma_start(vrows[r:r + count, :], src.rearrange("(r n) -> r n", n=P)).then_inc(s_vrows, 16)
            act.dma_start(trows[:, :], w["conv_w"][0].rearrange("k (r n) -> (k r) n", n=P)).then_inc(s_vrows, 16)
            act.dma_start(wide[0:ADA, :], w["b_ada"][0].rearrange("(r n) -> r n", n=N)).then_inc(s_vrows, 16)
            for g, name in enumerate(GAINS):
                act.dma_start(wide[ADA + 2 * g:ADA + 2 * g + 2, :],
                              w[name][0].rearrange("(r n) -> r n", n=N)).then_inc(s_vrows, 16)
            act.wait_ge(s_vec, 1)
            cc = vec[:, VEC_AT["c"]:VEC_AT["c"] + KD]
            act.activation(keep.silu_c[:, :], cc, ACT.Sigmoid).then_inc(s_silu, 1)
            act.wait_ge(s_x, 16)
            for t in range(NT):
                sq = act.activation(hT[:, 2 * t:2 * t + 2, :], x[:, t, :].rearrange("p (a b) -> p a b", b=S), ACT.Square, accum_out=sums[:, t:t + 1])
                link.sign(sq)
            link.wait()
            act.activation(mean_sq[:, :], sums[:, :], ACT.Copy, scale=1.0 / D, bias=RMS_EPS).then_inc(s_sq, 1)

            def gain_copy(i):
                if (i // 2) % 3:
                    act.wait_ge(s_adam, i + 1)
                    act.activation(keep.mod[:, i * N:i * N + N], pg[:, :], ACT.Copy).then_inc(s_adag, 1)

            for i in range(4):
                gain_copy(i)
            for b in range(NT * 2):
                if b % 2 == 0:
                    act.wait_ge(s_ht, b + 1)
                    t, half = b // 2, b % 2
                    act.activation(hT[:, half * 4:half * 4 + 4, t * P:(t + 1) * P],
                                   pt[0][:, :].rearrange("p (k s) -> p k s", k=4), ACT.Copy).then_inc(s_hA, 1)
            act.wait_ge(s_vec, 2)
            for n, (s, t) in enumerate(Z_TILES):
                act.wait_ge(s_z, n + 1)
                z = pz[n % 3]
                if n < NZ_RWKV:
                    act.activation(mix.zr[:, n, :], z[:, :], ACT.Copy,
                                   scale=keep.one_minus_mu[:, n:n + 1]).then_inc(s_zA, 1)
                elif n < NZ_RWKV + RT_:
                    act.activation(upad[:, n - NZ_RWKV, CK - 1:], z[:, :], ACT.Copy).then_inc(s_zA, 1)
                elif n < NZ_RWKV + NZ_CONV:
                    j = n - NZ_RWKV - RT_
                    if j >= 2:
                        act.wait_ge(s_glu, j - 1)
                    act.activation(glu[:, j % 2, :], z[:, :], ACT.Sigmoid).then_inc(s_zA, 1)
                else:
                    act.activation(mix.gates[:, n - NZ_RWKV - NZ_CONV, :], z[:, :], ACT.Sigmoid).then_inc(s_zA, 1)
                if t == 0 and s >= 2:
                    gain_copy(s + 2)

        @block.tensor
        def _(pe):
            pe.wait_ge(s_const, 5)
            pe.wait_ge(s_vrows, 16 * (len(VEC_ROWS) + 2 + len(GAINS)))
            pe.transpose(pt[0][:, 0:N_VEC], vrows[:, :], keep.ident[0:N_VEC, 0:N_VEC])
            pe.transpose(pt[0][:, P:P + N_TAP], trows[:, :], keep.ident[0:N_TAP, 0:N_TAP]).then_inc(s_vecT, 1)

            def ada_sum(i):
                pe.wait_ge(s_ada, i + 1)
                if i:
                    pe.wait_ge(s_mod, i)
                pe.matmul(pm[:, :], keep.ones[:, :], acc[:, i % 2, :], start=True, stop=False)
                last = pe.matmul(pm[:, :], keep.ident[0:N_WIDE, i:i + 1].to_broadcast([N_WIDE, P]), wide[:, :],
                                 start=False, stop=True)
                if (i // 2) % 3:
                    row = ADA + 2 * {1: 0, 2: 1, 4: 2, 5: 3}[i // 2] + i % 2
                    last = pe.matmul(pg[:, :], keep.ident[0:N_WIDE, row:row + 1].to_broadcast([N_WIDE, P]),
                                     wide[:, :], start=True, stop=True)
                last.then_inc(s_adam, 1)

            for i in range(4):
                ada_sum(i)
            for b in range(NT * 2):
                t, half = b // 2, b % 2
                pe.wait_ge(s_h, t + 1)
                if half == 0:
                    pe.wait_ge(s_vec, 1)
                    if t:
                        pe.wait_ge(s_hA, t)
                elif t:
                    pe.wait_ge(s_hV, t)
                for k in range(4):
                    c0 = (half * 4 + k) * P
                    last = pe.transpose(pt[half][:, k * P:(k + 1) * P], x[:, t, c0:c0 + P], keep.ident[:, :])
                last.then_inc(s_ht, 1)
            pe.wait_ge(s_hA, NT)
            pe.wait_ge(s_hV, NT)
            for n, (s, t) in enumerate(Z_TILES):
                if t == 0:
                    slot_wait(pe, ("in", s))
                if n >= 3:
                    pe.wait_ge(s_zA, n - 2)
                    if n - 3 < NZ_RWKV:
                        pe.wait_ge(s_zV, n - 2)
                slot = STREAM_AT[("in", s)] % RING1
                for k in range(KD):
                    last = pe.matmul(pz[n % 3][:, :], ring[:, slot, k, t * P:(t + 1) * P], hT[:, k, :],
                                     start=(k == 0), stop=(k == KD - 1))
                last.then_inc(s_z, 1)
                if t == 0 and s >= 2:
                    ada_sum(s + 2)

        @block.vector
        def _(dve):
            link = Link(dve, s_v)
            dve.wait_ge(s_vecT, 1)
            nc.vector.tensor_copy(taps[:, :], pt[0][:, P:P + N_TAP])
            nc.vector.tensor_copy(vec[:, :], pt[0][:, 0:N_VEC]).then_inc(s_vec, 1)
            dve.wait_ge(s_vec, 1)
            nc.vector.tensor_scalar(keep.one_minus_mu[:, :], vec[:, 0:NZ_RWKV], -1.0, 1.0, ALU.mult,
                                    ALU.add).then_inc(s_vec, 1)
            dve.wait_ge(s_silu, 1)
            cc = vec[:, VEC_AT["c"]:VEC_AT["c"] + KD]
            link(nc.vector.tensor_tensor(keep.silu_c[:, :], keep.silu_c[:, :], cc, ALU.mult))

            def ada_partial(i):
                slot_wait(dve, ("ada", i))
                if i >= 2:
                    dve.wait_ge(s_adam, i - 1)
                slot = STREAM_AT[("ada", i)] % RING1
                for k in range(KD):
                    c_k = keep.silu_c[:, k:k + 1]
                    if k == 0:
                        last = nc.vector.tensor_scalar(acc[:, i % 2, :], ring[:, slot, k, :], c_k, None, ALU.mult)
                    else:
                        last = nc.vector.scalar_tensor_tensor(out=acc[:, i % 2, :], in0=ring[:, slot, k, :], scalar=c_k,
                                                              in1=acc[:, i % 2, :], op0=ALU.mult, op1=ALU.add)
                    if k < KD - 1:
                        link(last)
                last.then_inc(s_ada, 1)

            def mod_row(i):
                dve.wait_ge(s_adam, i + 1)
                row = keep.mod[:, i * N:i * N + N]
                kind = (i // 2) % 3
                if kind == 0:
                    nc.vector.tensor_copy(row, pm[:, :]).then_inc(s_mod, 1)
                    return
                dve.wait_ge(s_adag, (i // 6) * 4 + i % 6 - 1)
                nc.vector.scalar_tensor_tensor(out=row, in0=pm[:, :], scalar=1.0 if kind == 1 else 0.0, in1=row,
                                               op0=ALU.add, op1=ALU.mult).then_inc(s_mod, 1)

            for i in range(4):
                ada_partial(i)
                mod_row(i)
            dve.wait_ge(s_rstd, 1)
            dve.wait_ge(s_mod, 4)
            scaled = [link.sign(nc.vector.scalar_tensor_tensor(
                out=x[:, t, :], in0=x[:, t, :], scalar=rstd[:, t:t + 1], in1=keep.mod[:, D:2 * D],
                op0=ALU.mult, op1=ALU.mult)) for t in range(NT)]
            for t in range(NT):
                link.wait(scaled[t])
                nc.vector.tensor_tensor(x[:, t, :], x[:, t, :], keep.mod[:, 0:D], ALU.add).then_inc(s_h, 1)
            for b in range(1, NT * 2, 2):
                dve.wait_ge(s_ht, b + 1)
                t = b // 2
                nc.vector.tensor_copy(hT[:, 4:8, t * P:(t + 1) * P],
                                      pt[1][:, :].rearrange("p (k s) -> p k s", k=4)).then_inc(s_hV, 1)

            def ada_steps(s):
                if s >= 2:
                    mod_row(s + 2)
                if 1 <= s <= ADA - 4:
                    ada_partial(s + 3)

            for n, (s, t) in enumerate(Z_TILES[:NZ_RWKV]):
                dve.wait_ge(s_zA, n + 1)
                nc.vector.scalar_tensor_tensor(out=mix.zr[:, n, 1:], in0=pz[n % 3][:, 0:S - 1], scalar=vec[:, n:n + 1],
                                               in1=mix.zr[:, n, 1:], op0=ALU.mult, op1=ALU.add).then_inc(s_zV, 1)
                if t == 1:
                    ada_steps(s)
            ada_steps(4)
            for j in range(RT_):
                dve.wait_ge(s_zA, NZ_RWKV + RT_ + j + 1)
                nc.vector.tensor_tensor(upad[:, j, CK - 1:], upad[:, j, CK - 1:], glu[:, j % 2, :],
                                        ALU.mult).then_inc(s_glu, 1)
                if j == 1:
                    ada_steps(5)
            dve.wait_ge(s_const, 5)
            dve.wait_ge(s_glu, RT_)
            done = {}
            for k in range(CK):
                if k % 8 == 0:
                    ada_steps(6 + k // 8)
                for r in range(RT_):
                    tap = taps[:, k * RT_ + r:k * RT_ + r + 1]
                    u = upad[:, r, k:k + S]
                    if k == 0:
                        done[r] = link.sign(nc.vector.tensor_scalar(mix.co[:, r, :], u, tap, vcol("conv_b", r),
                                                                    ALU.mult, ALU.add))
                    else:
                        link.wait(done[r])
                        done[r] = link.sign(nc.vector.scalar_tensor_tensor(
                            out=mix.co[:, r, :], in0=u, scalar=tap, in1=mix.co[:, r, :], op0=ALU.mult, op1=ALU.add))


def rwkv(nc, w, keep, mix):
    with ExitStack() as stack:
        m = Memory(nc, stack)
        T4 = [P, RT_, S]
        cum, sg, aB, A = m.sb("cum", T4), m.sb("sg", T4), m.sb("aB", T4), m.sb("A_T", T4)
        ep = m.sb("ep", [P, 2, S])
        reset = m.sb("reset", [P, S])
        loras = m.sb("loras", [P, RW])
        g2 = m.sb("g2", [P, RW])
        headones = m.sb("headones", [P, P])
        ka1 = m.sb("one_minus_ka", [P, RT_])
        mid = m.sb("mid", [P, RT_, NT])
        last = m.sb("last", [P, RT_, NT])
        mid_e = m.sb("mid_e", [P, RT_, NT])
        hop = m.sb("hop", [P, RT_, NT])
        LV = 7
        masks = m.sb("level_masks", [P, LV, P])
        low1 = m.sb("low1", [P, P])
        tri = m.sb("tri", [P, 2, P])
        col_i, row_i = m.sb("col_i", [P, P], I32), m.sb("row_i", [P, P], I32)
        colf, rowf, xorf, ge = m.sb("colf", [P, P]), m.sb("rowf", [P, P]), m.sb("xorf", [P, 2, P]), m.sb("ge", [P, 2, P])
        tok = m.sb("tok", [P, 3, RW])
        AB = m.sb("AB", [P, HEADS, 2 * P])
        AK = m.sb("AK", [P, HEADS, 2 * P])
        X, XT = m.sb("X", [P, HEADS, P]), m.sb("XT", [P, HEADS, P])
        Z = sg[:, 0:2, :].rearrange("p a (h t) -> p (a h) t", t=P)
        TM = cum[:, :, :].rearrange("p (b a) (h t) -> p b (a h) t", b=2, t=P)
        G, U = m.sb("G", [P, 2, RT_, HD]), m.sb("U", [P, RT_, 2, HD])
        M = m.sb("M", [P, RT_, HD])
        bank = [m.bank(f"b{i}") for i in range(8)]
        zr, vec, gate_r, bonus = mix.zr, keep.vec, mix.gate_r, mix.bonus
        r_, k_, v_ = zr[:, 0:4, :], zr[:, 4:8, :], zr[:, 8:12, :]

        s_w = m.sem("p2_weights_in")
        s_io = m.sem("p2_iotas")
        s_mask = m.sem("p2_masks")
        s_act = m.sem("p2_lora_activated")
        s_lora = m.sem("p2_lora_products")
        s_loraA = m.sem("p2_lora_taken")
        s_kk = m.sem("p2_kk")
        s_kksq = m.sem("p2_kk_squared")
        s_kksum = m.sem("p2_kk_sums")
        s_kkmax = m.sem("p2_kk_max")
        s_kksqrt = m.sem("p2_kk_root")
        s_rk = m.sem("p2_rk")
        s_rksum = m.sem("p2_rk_sums")
        s_bonus = m.sem("p2_bonus")
        s_cc = m.sem("p2_centred")
        s_e1, s_e2, s_e3 = m.sem("p2_exp_plus"), m.sem("p2_exp_minus"), m.sem("p2_exp_before")
        s_epfree = m.sem("p2_exp_plus_used")
        s_oper = m.sem("p2_operands")
        s_mid = m.sem("p2_mid_exp")
        s_v, s_a, s_g = m.sem("p2_vector_chain"), m.sem("p2_scalar_chain"), m.sem("p2_pool_chain")
        s_tokp, s_tok = m.sem("p2_tok_turned"), m.sem("p2_tok_ready")
        s_pair, s_pairV = m.sem("p2_pair_products"), m.sem("p2_pair_masked")
        s_x2, s_x2p = m.sem("p2_x_start"), m.sem("p2_xt_start")
        s_tm = m.sem("p2_level_T")
        s_z, s_zA = m.sem("p2_Z"), m.sem("p2_Z_taken")
        s_xz, s_xzV = m.sem("p2_XZ"), m.sem("p2_XZ_added")
        s_G, s_GA = m.sem("p2_G"), m.sem("p2_G_taken")
        s_U, s_UV = m.sem("p2_U"), m.sem("p2_U_taken")
        s_M, s_MV = m.sem("p2_M"), m.sem("p2_M_taken")
        s_Y, s_YA = m.sem("p2_Y"), m.sem("p2_Y_taken")
        block = stack.enter_context(nc.Block())
        STEPS = LV - 1
        LAST_C = NT - 1

        def vcol(name, i=0):
            return vec[:, VEC_AT[name] + i:VEC_AT[name] + i + 1]

        def wide(ap, shape):
            return ap.to_broadcast(shape)

        def at(h):
            return h // 2, slice(HD * (h % 2), HD * (h % 2) + HD)

        @block.sync
        def _(sp):
            sp.dma_start(loras[0:LORA_W, :], w["w2"][0]).then_inc(s_w, 16)
            sp.dma_start(loras[LORA_W:P, :], w["a2"][0]).then_inc(s_w, 16)
            sp.dma_start(g2[:, :], w["g2"][0]).then_inc(s_w, 16)

        @block.gpsimd
        def _(pool):
            link = Link(pool, s_g)
            link.sign(pool.memset(headones[:, :], 0.0))
            link.sign(pool.memset(reset[:, :], 1.0))
            pool.iota(col_i[:, :], [[1, P]], base=0, channel_multiplier=0).then_inc(s_io, 1)
            pool.iota(row_i[:, :], [[0, P]], base=0, channel_multiplier=1).then_inc(s_io, 1)
            link.wait()
            for q in range(2):
                pool.wait_ge(s_io, 2 + q)
                pool.memset(headones[HD * q:HD * q + HD, HD * q:HD * q + HD], 1.0).then_inc(s_io, 1)
            pool.wait_ge(s_io, 4)
            pool.memset(reset[:, :].rearrange("p (c t) -> p c t", c=NT)[:, :, 0:1], 0.0).then_inc(s_io, 1)
            pool.wait_ge(s_mask, 1)
            for c in range(NT):
                pool.wait_ge(s_pairV, 4 * c + 4)
                if c:
                    pool.wait_ge(s_U, c)
                link(pool.tensor_tensor(XT[:, :, :], AB[:, :, 0:P], wide(masks[:, 0:1, :], [P, HEADS, P]), ALU.mult))
                pool.tensor_tensor(XT[:, :, :], XT[:, :, :], wide(keep.ident[:, :].unsqueeze(1), [P, HEADS, P]),
                                   ALU.add).then_inc(s_x2p, 1)
                for lv in range(STEPS):
                    n = c * STEPS + lv
                    if n >= 2:
                        pool.wait_ge(s_z, 2 * (n - 1))
                    pool.tensor_tensor(TM[:, n % 2, :, :], AB[:, :, 0:P], wide(masks[:, lv + 1:lv + 2, :], [P, HEADS, P]),
                                       ALU.mult).then_inc(s_tm, 1)

        @block.scalar
        def _(act):
            act.activation(zr[0:LORA_W, 12, :], zr[0:LORA_W, 12, :], ACT.Tanh).then_inc(s_act, 1)
            act.activation(zr[:, 13, :], zr[:, 13, :], ACT.Sigmoid).then_inc(s_act, 1)
            for r in range(RT_):
                for j, (dst, bias) in enumerate(((sg, "w0"), (aB, "a0"), (gate_r, None))):
                    n = 3 * r + j
                    act.wait_ge(s_lora, n + 1)
                    if bias:
                        act.activation(dst[:, r, :], bank[n % 4][:, :], ACT.Sigmoid, bias=vcol(bias, r)).then_inc(s_loraA, 1)
                    else:
                        act.activation(dst[:, r, :], bank[n % 4][:, :], ACT.Copy).then_inc(s_loraA, 1)
            for r in range(RT_):
                act.wait_ge(s_kk, r + 1)
                act.activation(bonus[:, r, :], A[:, r, :], ACT.Square).then_inc(s_kksq, 1)
            for r in range(RT_):
                act.wait_ge(s_kkmax, r + 1)
                act.activation(bonus[:, r, :], bonus[:, r, :], ACT.Sqrt).then_inc(s_kksqrt, 1)
            for r in range(RT_):
                act.wait_ge(s_cc, r + 1)
                if r == 0:
                    act.activation(mid_e[:, :, :], mid[:, :, :], ACT.Exp, scale=-DECAY).then_inc(s_mid, 1)
                if r >= 2:
                    act.wait_ge(s_epfree, r - 1)
                act.activation(ep[:, r % 2, :], cum[:, r, :], ACT.Exp, scale=-DECAY).then_inc(s_e1, 1)
                act.activation(sg[:, r, :], sg[:, r, :], ACT.Exp, scale=-DECAY).then_inc(s_e3, 1)
                act.wait_ge(s_e1, r + 1)
                act.activation(cum[:, r, :], cum[:, r, :], ACT.Exp, scale=DECAY).then_inc(s_e2, 1)
            for c in range(NT):
                for i in range(3):
                    act.wait_ge(s_tokp, 3 * c + i + 1)
                    if c and i == 0:
                        act.wait_ge(s_M, c)
                    act.activation(tok[:, i, :], bank[(6, 7, 6)[i]][:, :], ACT.Copy).then_inc(s_tok, 1)
                for lv in range(STEPS):
                    for g in range(2):
                        n = (c * STEPS + lv) * 2 + g
                        act.wait_ge(s_z, n + 1)
                        if n >= 2:
                            act.wait_ge(s_xz, n - 1)
                        act.activation(Z[:, 4 * g:4 * g + 4, :], bank[g][:, :].rearrange("p (h t) -> p h t", h=4),
                                       ACT.Copy).then_inc(s_zA, 1)
                act.wait_ge(s_G, c + 1)
                for q in range(2):
                    act.activation(G[:, q, :, :], bank[6 + q][:, 0:RT_ * HD].rearrange("p (r v) -> p r v", r=RT_),
                                   ACT.Copy).then_inc(s_GA, 1)
                act.wait_ge(s_Y, c + 1)
                for q in range(2):
                    act.activation(zr[HD * q:HD * q + HD, 0:4, c * P:(c + 1) * P],
                                   bank[2 + q][HD * q:HD * q + HD, :].rearrange("p (r t) -> p r t", r=RT_),
                                   ACT.Copy).then_inc(s_YA, 1)

        @block.tensor
        def _(pe):
            pe.wait_ge(s_w, 48)
            pe.wait_ge(s_act, 2)
            for r in range(RT_):
                for j in range(3):
                    n = 3 * r + j
                    if n >= 4:
                        pe.wait_ge(s_loraA, n - 3)
                    cols = slice(r * P, (r + 1) * P)
                    if j == 0:
                        mm = pe.matmul(bank[n % 4][:, :], loras[0:LORA_W, cols], zr[0:LORA_W, 12, :], start=True, stop=True)
                    elif j == 1:
                        mm = pe.matmul(bank[n % 4][:, :], loras[LORA_W:P, cols], zr[LORA_W:P, 12, :], start=True, stop=True)
                    else:
                        mm = pe.matmul(bank[n % 4][:, :], g2[:, cols], zr[:, 13, :], start=True, stop=True)
                    mm.then_inc(s_lora, 1)
            pe.wait_ge(s_io, 5)
            for r in range(RT_):
                pe.wait_ge(s_kksq, r + 1)
                pe.matmul(bank[4 + r][:, :], headones[:, :], bonus[:, r, :], start=True, stop=True).then_inc(s_kksum, 1)
            pe.wait_ge(s_kkmax, RT_)
            for r in range(RT_):
                pe.wait_ge(s_rk, r + 1)
                pe.matmul(bank[4 + r][:, :], headones[:, :], bonus[:, r, :], start=True, stop=True).then_inc(s_rksum, 1)
            pe.wait_ge(s_bonus, RT_)
            pe.wait_ge(s_oper, RT_)
            for c in range(NT):
                ts = slice(c * P, (c + 1) * P)
                if c:
                    pe.wait_ge(s_GA, 2 * c)
                for i, src in enumerate((aB, k_, v_)):
                    if i == 2:
                        pe.wait_ge(s_tok, 3 * c + 1)
                    b = bank[(6, 7, 6)[i]]
                    for r in range(RT_):
                        mm = pe.transpose(b[:, r * P:(r + 1) * P], src[:, r, ts], keep.ident[:, :])
                    mm.then_inc(s_tokp, 1)
                for g in range(2):
                    if c or g:
                        pe.wait_ge(s_pairV, 4 * c + 2 * g)
                        pe.wait_ge(s_x2, 2 * c + g)
                    if c and g == 0:
                        pe.wait_ge(s_UV, c)
                        pe.wait_ge(s_YA, 2 * c)
                        pe.wait_ge(s_MV, c)
                    for h in range(4 * g, 4 * g + 4):
                        r, ps = at(h)
                        q, j = h % 2, (h % 4) // 2
                        cs = slice(j * 2 * P, (j + 1) * 2 * P)
                        for dst, lhs in ((bank[q], aB), (bank[2 + q], k_)):
                            pe.matmul(dst[:, j * 2 * P:j * 2 * P + P], lhs[ps, r, ts], A[ps, r, ts], start=True, stop=True)
                            pe.matmul(dst[:, j * 2 * P + P:(j + 1) * 2 * P], lhs[ps, r, ts], r_[ps, r, ts],
                                      start=True, stop=True)
                        mm = pe.matmul(bank[4 + q][:, j * P:(j + 1) * P], A[ps, r, ts], aB[ps, r, ts], start=True, stop=True)
                    mm.then_inc(s_pair, 1)
                pe.wait_ge(s_x2, 2 * c + 2)
                pe.wait_ge(s_x2p, c + 1)
                pe.wait_ge(s_pairV, 4 * c + 4)
                for lv in range(STEPS):
                    n = c * STEPS + lv
                    pe.wait_ge(s_tm, n + 1)
                    for g in range(2):
                        if lv:
                            pe.wait_ge(s_xzV, 2 * (n - 1) + g + 1)
                        for h in range(4 * g, 4 * g + 4):
                            mm = pe.matmul(bank[g][:, (h % 4) * P:(h % 4 + 1) * P], TM[:, n % 2, h, :], X[:, h, :],
                                           start=True, stop=True)
                        mm.then_inc(s_z, 1)
                    for g in range(2):
                        pe.wait_ge(s_zA, 2 * n + g + 1)
                        for h in range(4 * g, 4 * g + 4):
                            cs = slice((h % 4) * P, (h % 4 + 1) * P)
                            if lv < STEPS - 1:
                                pe.matmul(bank[2 + g][:, cs], XT[:, h, :], Z[:, h, :], start=True, stop=True)
                            mm = pe.matmul(bank[4 + g][:, cs], Z[:, h, :], XT[:, h, :], start=True, stop=True)
                        mm.then_inc(s_xz, 1)
                pe.wait_ge(s_tok, 3 * c + 3)
                for h in range(HEADS):
                    r, ps = at(h)
                    dst = bank[6 + h % 2][:, r * HD:(r + 1) * HD]
                    if c:
                        pe.matmul(dst, A[ps, r, ts], M[ps, r, :], start=True, stop=False)
                    mm = pe.matmul(dst, AK[:, h, 0:P], tok[:, 2, h * HD:(h + 1) * HD], start=(c == 0), stop=True)
                mm.then_inc(s_G, 1)
                pe.wait_ge(s_xzV, 2 * STEPS * (c + 1))
                pe.wait_ge(s_GA, 2 * c + 2)
                for h in range(HEADS):
                    mm = pe.matmul(bank[4][:, h * HD:(h + 1) * HD], XT[:, h, :], G[:, h % 2, h // 2, :], start=True, stop=True)
                mm.then_inc(s_U, 1)
                pe.wait_ge(s_UV, c + 1)
                for r in range(RT_):
                    cs = slice(r * P, (r + 1) * P)
                    pe.matmul(bank[5][:, cs], tok[:, 0, cs], U[:, r, :, :].rearrange("p q v -> p (q v)"), start=True, stop=False)
                    mm = pe.matmul(bank[5][:, cs], tok[:, 1, cs], tok[:, 2, cs], start=False, stop=True)
                mm.then_inc(s_M, 1)
                for h in range(HEADS):
                    r, ps = at(h)
                    dst = bank[2 + h % 2][ps, r * P:(r + 1) * P]
                    if c:
                        pe.matmul(dst, M[ps, r, :], r_[ps, r, ts], start=True, stop=False)
                    pe.matmul(dst, U[:, r, h % 2, :], AB[:, h, P:2 * P], start=(c == 0), stop=False)
                    mm = pe.matmul(dst, tok[:, 2, h * HD:(h + 1) * HD], AK[:, h, P:2 * P], start=False, stop=True)
                mm.then_inc(s_Y, 1)

        @block.vector
        def _(dve):
            link = Link(dve, s_v)
            V = nc.vector
            dve.wait_ge(s_io, 2)
            a = link.sign(V.tensor_copy(colf[:, :], col_i[:, :]))
            b = link.sign(V.tensor_copy(rowf[:, :], row_i[:, :]))
            link(V.tensor_tensor(col_i[:, :], col_i[:, :], row_i[:, :], ALU.bitwise_xor))
            link(V.tensor_copy(xorf[:, 0, :], col_i[:, :]))
            link.sign(V.tensor_tensor(tri[:, 1, :], colf[:, :], rowf[:, :], ALU.is_ge))
            link.sign(V.tensor_tensor(ge[:, 0, :], colf[:, :], rowf[:, :], ALU.is_lt))
            link(V.tensor_tensor(tri[:, 0, :], colf[:, :], rowf[:, :], ALU.is_gt))
            link.sign(V.tensor_tensor(xorf[:, 1, :], xorf[:, 0, :], ge[:, 0, :], ALU.mult))
            link(V.tensor_tensor(xorf[:, 0, :], xorf[:, 0, :], tri[:, 0, :], ALU.mult))
            link.sign(V.tensor_scalar(low1[:, :], xorf[:, 1, :], 1.0, None, ALU.is_equal))
            for lv in range(LV):
                link(V.tensor_scalar(ge[:, 0, :], xorf[:, 0, :], float(2 ** lv), None, ALU.is_ge))
                link(V.tensor_scalar(ge[:, 1, :], xorf[:, 0, :], float(2 ** (lv + 1)), None, ALU.is_lt))
                link(V.tensor_tensor(masks[:, lv, :], ge[:, 0, :], ge[:, 1, :], ALU.mult))
            V.tensor_scalar(ka1[:, :], vec[:, VEC_AT["k_a"]:VEC_AT["k_a"] + RT_], -1.0, 1.0, ALU.mult,
                            ALU.add).then_inc(s_mask, 1)
            for r in range(RT_):
                V.tensor_scalar(A[:, r, :], k_[:, r, :], vcol("k_k", r), None, ALU.mult).then_inc(s_kk, 1)
            dve.wait_ge(s_io, 5)
            done = []
            for r in range(RT_):
                dve.wait_ge(s_loraA, 3 * r + 1)
                done.append(link.sign(V.tensor_tensor_scan(cum[:, r, :], reset[:, :], sg[:, r, :], 0.0, ALU.mult, ALU.add)))
            for r in range(RT_):
                link.wait(done[r])
                done[r] = link.sign(V.tensor_copy(mid[:, r, :], cum[:, r, P // 2 - 1::P]))
            for r in range(RT_):
                link.wait(done[r])
                chunks = cum[:, r, :].rearrange("p (c t) -> p c t", c=NT)
                done[r] = link.sign(V.tensor_tensor(chunks, chunks, wide(mid[:, r, :].unsqueeze(2), [P, NT, P]), ALU.subtract))
            for r in range(RT_):
                link.wait(done[r])
                V.tensor_tensor(sg[:, r, :], cum[:, r, :], sg[:, r, :], ALU.subtract).then_inc(s_cc, 1)
            for r in range(RT_):
                dve.wait_ge(s_kksum, r + 1)
                V.tensor_scalar(bonus[:, r, :], bank[4 + r][:, :], 1e-24, None, ALU.max).then_inc(s_kkmax, 1)
            for r in range(RT_):
                dve.wait_ge(s_kksqrt, r + 1)
                done[r] = link.sign(V.reciprocal(bonus[:, r, :], bonus[:, r, :]))
            for r in range(RT_):
                link.wait(done[r])
                done[r] = link.sign(V.tensor_tensor(A[:, r, :], A[:, r, :], bonus[:, r, :], ALU.mult))
            dve.wait_ge(s_mask, 1)
            for r in range(RT_):
                dve.wait_ge(s_loraA, 3 * r + 2)
                link.wait(done[r])
                done[r] = link.sign(V.tensor_scalar(bonus[:, r, :], aB[:, r, :], vcol("k_a", r), ka1[:, r:r + 1], ALU.mult, ALU.add))
            for r in range(RT_):
                link.wait(done[r])
                dve.wait_ge(s_kk, r + 1)
                done[r] = link.sign(V.tensor_tensor(k_[:, r, :], k_[:, r, :], bonus[:, r, :], ALU.mult))
                link.sign(V.tensor_tensor(aB[:, r, :], aB[:, r, :], A[:, r, :], ALU.mult))
            for r in range(RT_):
                link.wait(done[r])
                V.scalar_tensor_tensor(out=bonus[:, r, :], in0=k_[:, r, :], scalar=vcol("r_k", r), in1=r_[:, r, :],
                                       op0=ALU.mult, op1=ALU.mult).then_inc(s_rk, 1)
            link.wait()
            dve.wait_ge(s_rk, RT_)
            for r in range(RT_):
                dve.wait_ge(s_e1, r + 1)
                n = link.sign(V.tensor_tensor(r_[:, r, :], r_[:, r, :], ep[:, r % 2, :], ALU.mult))
                link.sign(V.tensor_copy(last[:, r, :], ep[:, r % 2, P - 1::P]))
                link.wait()
                dve.wait_ge(s_e2, r + 1)
                link.sign(V.tensor_tensor(aB[:, r, :], aB[:, r, :], cum[:, r, :], ALU.mult))
                V.tensor_tensor(k_[:, r, :], k_[:, r, :], cum[:, r, :], ALU.mult).then_inc(s_epfree, 1)
                dve.wait_ge(s_e3, r + 1)
                link(V.scalar_tensor_tensor(out=A[:, r, :], in0=A[:, r, :], scalar=-1.0, in1=sg[:, r, :], op0=ALU.mult, op1=ALU.mult))
                dve.wait_ge(s_epfree, r + 1)
                dve.wait_ge(s_rksum, r + 1)
                V.tensor_tensor(bonus[:, r, :], bank[4 + r][:, :], v_[:, r, :], ALU.mult).then_inc(s_bonus, 1)
                dve.wait_ge(s_bonus, r + 1)
                dve.sem_inc(s_oper, 1)
            dve.wait_ge(s_mid, 1)
            link(V.tensor_tensor(hop[:, :, 0:NT - 1], last[:, :, 0:NT - 1], mid_e[:, :, 1:NT], ALU.mult))
            for c in range(NT):
                for g in range(2):
                    dve.wait_ge(s_pair, 2 * c + g + 1)
                    if c and g == 0:
                        dve.wait_ge(s_Y, c)
                    for q in range(2):
                        h0 = 4 * g + q
                        m2 = wide(tri[:, :, :].rearrange("p a t -> p (a t)").unsqueeze(1), [P, 2, 2 * P])
                        V.tensor_tensor(AB[:, h0:h0 + 3:2, :], bank[q][:, :].rearrange("p (h t) -> p h t", h=2), m2,
                                        ALU.mult)
                        V.tensor_tensor(AK[:, h0:h0 + 3:2, :], bank[2 + q][:, :].rearrange("p (h t) -> p h t", h=2),
                                        m2, ALU.mult).then_inc(s_pairV, 1)
                        link.sign(V.tensor_tensor(X[:, h0:h0 + 3:2, :],
                                                  bank[4 + q][:, 0:2 * P].rearrange("p (h t) -> p h t", h=2),
                                                  wide(low1[:, :].unsqueeze(1), [P, 2, P]), ALU.mult))
                    link.wait()
                    V.tensor_tensor(X[:, 4 * g:4 * g + 4, :], X[:, 4 * g:4 * g + 4, :],
                                    wide(keep.ident[:, :].unsqueeze(1), [P, 4, P]), ALU.add).then_inc(s_x2, 1)
                for lv in range(STEPS):
                    for g in range(2):
                        n = (c * STEPS + lv) * 2 + g
                        dve.wait_ge(s_xz, n + 1)
                        if lv == 0:
                            dve.wait_ge(s_x2p, c + 1)
                            dve.wait_ge(s_x2, 2 * c + 2)
                        hs = slice(4 * g, 4 * g + 4)
                        if n >= 2:
                            dve.wait_ge(s_xzV, n - 1)
                        if lv < STEPS - 1:
                            V.tensor_tensor(X[:, hs, :], X[:, hs, :], bank[2 + g][:, :].rearrange("p (h t) -> p h t", h=4), ALU.add)
                        V.tensor_tensor(XT[:, hs, :], XT[:, hs, :], bank[4 + g][:, :].rearrange("p (h t) -> p h t", h=4),
                                        ALU.add).then_inc(s_xzV, 1)
                dve.wait_ge(s_U, c + 1)
                V.tensor_copy(U[:, :, :, :].rearrange("p r q v -> p (r q v)"), bank[4][:, :]).then_inc(s_UV, 1)
                if c == LAST_C:
                    continue
                dve.wait_ge(s_M, c + 1)
                if c:
                    dve.wait_ge(s_Y, c + 1)
                for q in range(2):
                    ps = slice(HD * q, HD * q + HD)
                    new = bank[5][ps, :].rearrange("p (r v) -> p r v", r=RT_)[:, :, HD * q:HD * q + HD]
                    if c:
                        link.sign(V.tensor_tensor(M[ps, :, :], M[ps, :, :], new, ALU.add))
                    else:
                        link.sign(V.tensor_copy(M[ps, :, :], new))
                link.wait()
                V.tensor_tensor(M[:, :, :], M[:, :, :], wide(hop[:, :, c:c + 1], [P, RT_, HD]), ALU.mult).then_inc(s_MV, 1)

    m.reset_semaphores()


def merge(nc, w, keep, mix):
    with ExitStack() as stack:
        m = Memory(nc, stack)
        p_conv, p_rwkv = m.sb("p_conv", [P, RT_, D]), m.sb("p_rwkv", [P, RT_, D])
        w_o = m.sb("w_o", [P, KD, D])
        x = m.sb("x3", [P, NT, D])
        sq = m.sb("sq3", [P, RT_, S])
        stat = m.sb("stat3", [P, S])
        headones = m.sb("headones3", [P, P])
        sums = m.sb("sums3", [P, 2, NT, 2])
        mean_sq, rstd = m.sb("mean_sq3", [P, 2, NT]), m.sb("rstd3", [P, 2, NT])
        bank = [m.bank(f"c{i}") for i in range(8)]
        co, y, gates, vec = mix.co, mix.zr[:, 0:4, :], mix.gates, keep.vec

        s_pc, s_pr, s_wo, s_x = (m.sem(f"p3_{n}_in") for n in ("p_conv", "p_rwkv", "w_o", "x"))
        s_g = m.sem("p3_head_ones")
        s_mu = m.sem("p3_sums")
        s_d = m.sem("p3_centred")
        s_sq = m.sem("p3_squared")
        s_var = m.sem("p3_square_sums")
        s_varV = m.sem("p3_variance")
        s_root = m.sem("p3_root")
        s_n = m.sem("p3_conv_normed")
        s_sig = m.sem("p3_conv_sigmoid")
        s_u = m.sem("p3_conv_out")
        s_y = m.sem("p3_rwkv_out")
        s_p = m.sem("p3_projected")
        s_pV = m.sem("p3_projected_taken")
        s_o = m.sem("p3_out_projected")
        s_oA = m.sem("p3_out_squares")
        s_r = m.sem("p3_rstd")
        s_x1 = m.sem("p3_x1")
        s_x1A = m.sem("p3_x1_squares")
        s_h2 = m.sem("p3_h2")
        s_st = m.sem("p3_stored")
        s_v, s_a = m.sem("p3_vector_chain"), m.sem("p3_scalar_chain")
        block = stack.enter_context(nc.Block())

        def h2(t):
            return p_conv[:, t, :]

        def vcol(name, i=0):
            return vec[:, VEC_AT[name] + i:VEC_AT[name] + i + 1]

        @block.sync
        def _(sp):
            sp.dma_start(p_conv[:, :, :], w["p_conv"][0].rearrange("(k p) n -> p k n", p=P)).then_inc(s_pc, 16)
            sp.dma_start(p_rwkv[:, :, :], w["p_rwkv"][0].rearrange("(k p) n -> p k n", p=P)).then_inc(s_pr, 16)
            sp.dma_start(w_o[:, :, :], w["w_o"][0].rearrange("(k p) n -> p k n", p=P)).then_inc(s_wo, 16)
            sp.dma_start(x[:, :, :], w["x"][0].rearrange("(t p) d -> p t d", p=P)).then_inc(s_x, 16)
            for t in range(NT):
                sp.wait_ge(s_x1, t + 1)
                sp.dma_start(keep.x1_dram[t * P:(t + 1) * P, :], x[:, t, :]).then_inc(s_st, 16)
            for t in range(NT):
                sp.wait_ge(s_h2, t + 1)
                sp.dma_start(keep.h2_dram[t * P:(t + 1) * P, :], h2(t)).then_inc(s_st, 16)
            sp.wait_ge(s_st, 16 * 2 * NT)

        @block.gpsimd
        def _(pool):
            pool.memset(headones[:, :], 0.0).then_inc(s_g, 1)
            for q in range(2):
                pool.wait_ge(s_g, 1 + q)
                pool.memset(headones[HD * q:HD * q + HD, HD * q:HD * q + HD], 1.0).then_inc(s_g, 1)
            pool.wait_ge(s_g, 3)
            for j in range(2 * NT):
                kind, t = j % 2, j // 2
                pool.wait_ge(s_oA, j + 1)
                pool.tensor_tensor(rstd[:, kind, t:t + 1], mean_sq[:, kind, t:t + 1], keep.power[:, 0:1],
                                   ALU.pow).then_inc(s_r, 1)

        @block.scalar
        def _(act):
            link = Link(act, s_a)
            for r in range(RT_):
                act.wait_ge(s_d, r + 1)
                act.activation(sq[:, r, :], co[:, r, :], ACT.Square).then_inc(s_sq, 1)
            act.wait_ge(s_varV, 1)
            act.activation(stat[:, :], stat[:, :], ACT.Sqrt).then_inc(s_root, 1)
            for r in range(RT_):
                act.wait_ge(s_d, RT_ + r + 1)
                act.activation(sq[:, r, :], y[:, r, :], ACT.Square).then_inc(s_sq, 1)
            for r in range(RT_):
                act.wait_ge(s_varV, 2 + r)
                act.activation(sq[:, r, :], sq[:, r, :], ACT.Sqrt).then_inc(s_root, 1)
            for r in range(RT_):
                act.wait_ge(s_n, r + 1)
                if r >= 1:
                    act.wait_ge(s_u, r)
                act.activation(stat[:, :], co[:, r, :], ACT.Sigmoid, bias=vcol("conv_ln_b", r),
                               scale=vcol("conv_ln_g", r)).then_inc(s_sig, 1)
            for t in range(NT):
                act.wait_ge(s_o, 2 * t + 2)
                for half in range(2):
                    act.wait_ge(s_y, RT_)
                    if t or half:
                        link.wait()
                    link.sign(act.activation(stat[:, :], bank[(2 * t + half) % 4][:, :], ACT.Square,
                                             accum_out=sums[:, 0, t, half:half + 1]))
                link.wait()
                link(act.activation(mean_sq[:, 0, t:t + 1], sums[:, 0, t, 0:1], ACT.Identity, bias=sums[:, 0, t, 1:2]))
                act.activation(mean_sq[:, 0, t:t + 1], mean_sq[:, 0, t:t + 1], ACT.Copy, scale=1.0 / D,
                               bias=RMS_EPS).then_inc(s_oA, 1)
                act.wait_ge(s_x1, t + 1)
                for half in range(2):
                    link.sign(act.activation(stat[:, :], x[:, t, half * N:half * N + N], ACT.Square,
                                             accum_out=sums[:, 1, t, half:half + 1]))
                    link.wait()
                link(act.activation(mean_sq[:, 1, t:t + 1], sums[:, 1, t, 0:1], ACT.Identity, bias=sums[:, 1, t, 1:2]))
                act.activation(mean_sq[:, 1, t:t + 1], mean_sq[:, 1, t:t + 1], ACT.Copy, scale=1.0 / D,
                               bias=RMS_EPS).then_inc(s_oA, 1)

        @block.tensor
        def _(pe):
            for r in range(RT_):
                mm = pe.matmul(bank[0][:, :], keep.ones[:, :], co[:, r, :], start=(r == 0), stop=(r == RT_ - 1))
            mm.then_inc(s_mu, 1)
            pe.wait_ge(s_g, 3)
            for r in range(RT_):
                pe.matmul(bank[1 + r][:, :], headones[:, :], y[:, r, :], start=True, stop=True).then_inc(s_mu, 1)
            pe.wait_ge(s_sq, RT_)
            for r in range(RT_):
                mm = pe.matmul(bank[5][:, :], keep.ones[:, :], sq[:, r, :], start=(r == 0), stop=(r == RT_ - 1))
            mm.then_inc(s_var, 1)
            for r in range(RT_):
                pe.wait_ge(s_sq, RT_ + r + 1)
                pe.matmul(bank[1 + r][:, :], headones[:, :], sq[:, r, :], start=True, stop=True).then_inc(s_var, 1)
            for j, (p_w, src, s_in, s_ready) in enumerate(((p_conv, co, s_pc, s_u), (p_rwkv, y, s_pr, s_y))):
                pe.wait_ge(s_in, 16)
                pe.wait_ge(s_ready, RT_)
                for dt in range(KD):
                    n = j * KD + dt
                    if n < 3:
                        pe.wait_ge(s_varV, 1 + RT_)
                    else:
                        pe.wait_ge(s_pV, n - 2)
                    for r in range(RT_):
                        mm = pe.matmul(bank[5 + n % 3][:, :], p_w[:, r, dt * P:(dt + 1) * P], src[:, r, :],
                                       start=(r == 0), stop=(r == RT_ - 1))
                    mm.then_inc(s_p, 1)
            pe.wait_ge(s_wo, 16)
            pe.wait_ge(s_pV, 2 * KD)
            for t in range(NT):
                for half in range(2):
                    if t >= 2:
                        pe.wait_ge(s_x1, t - 1)
                    for k in range(KD):
                        mm = pe.matmul(bank[(2 * t + half) % 4][:, :], gates[:, k, t * P:(t + 1) * P],
                                       w_o[:, k, half * N:half * N + N], start=(k == 0), stop=(k == KD - 1))
                    mm.then_inc(s_o, 1)

        @block.vector
        def _(dve):
            link = Link(dve, s_v)
            V = nc.vector
            dve.wait_ge(s_mu, 1)
            link(V.tensor_scalar(stat[:, :], bank[0][:, :], 1.0 / CW, None, ALU.mult))
            for r in range(RT_):
                V.tensor_tensor(co[:, r, :], co[:, r, :], stat[:, :], ALU.subtract).then_inc(s_d, 1)
            for r in range(RT_):
                dve.wait_ge(s_mu, 2 + r)
                V.scalar_tensor_tensor(out=y[:, r, :], in0=bank[1 + r][:, :], scalar=-1.0 / HD, in1=y[:, r, :],
                                       op0=ALU.mult, op1=ALU.add).then_inc(s_d, 1)
            dve.wait_ge(s_var, 1)
            dve.wait_ge(s_d, RT_)
            V.tensor_scalar(stat[:, :], bank[5][:, :], 1.0 / CW, LN_EPS, ALU.mult, ALU.add).then_inc(s_varV, 1)
            dve.wait_ge(s_root, 1)
            link(V.reciprocal(stat[:, :], stat[:, :]))
            for r in range(RT_):
                V.tensor_tensor(co[:, r, :], co[:, r, :], stat[:, :], ALU.mult).then_inc(s_n, 1)
            for r in range(RT_):
                dve.wait_ge(s_var, 2 + r)
                V.tensor_scalar(sq[:, r, :], bank[1 + r][:, :], 1.0 / HD, GN_EPS, ALU.mult, ALU.add).then_inc(s_varV, 1)
            dve.wait_ge(s_n, RT_)
            for r in range(RT_):
                dve.wait_ge(s_sig, r + 1)
                link(V.tensor_scalar(co[:, r, :], co[:, r, :], vcol("conv_ln_g", r), vcol("conv_ln_b", r), ALU.mult, ALU.add))
                V.tensor_tensor(co[:, r, :], co[:, r, :], stat[:, :], ALU.mult).then_inc(s_u, 1)
            for r in range(RT_):
                dve.wait_ge(s_root, 2 + r)
                link(V.reciprocal(sq[:, r, :], sq[:, r, :]))
                link(V.tensor_tensor(y[:, r, :], y[:, r, :], sq[:, r, :], ALU.mult))
                link(V.tensor_scalar(y[:, r, :], y[:, r, :], vcol("gn_g", r), vcol("gn_b", r), ALU.mult, ALU.add))
                link(V.tensor_tensor(y[:, r, :], y[:, r, :], mix.bonus[:, r, :], ALU.add))
                V.tensor_tensor(y[:, r, :], y[:, r, :], mix.gate_r[:, r, :], ALU.mult).then_inc(s_y, 1)
            for n in range(2 * KD):
                dve.wait_ge(s_p, n + 1)
                gated = V.tensor_tensor(gates[:, n, :], gates[:, n, :], bank[5 + n % 3][:, :], ALU.mult)
                if n < KD:
                    gated.then_inc(s_pV, 1)
                else:
                    link(gated)
                    dve.wait_ge(s_pV, n - KD + 1)
                    V.tensor_tensor(gates[:, n - KD, :], gates[:, n - KD, :], gates[:, n, :], ALU.add).then_inc(s_pV, 1)
            dve.wait_ge(s_x, 16)
            for t in range(NT):
                dve.wait_ge(s_r, 2 * t + 1)
                gt, g2row, shift = keep.mod[:, 2 * D:3 * D], keep.mod[:, 4 * D:5 * D], keep.mod[:, 3 * D:4 * D]
                for half in range(2):
                    cs = slice(half * N, half * N + N)
                    link.sign(V.scalar_tensor_tensor(out=h2(t)[:, cs], in0=bank[(2 * t + half) % 4][:, :],
                                                     scalar=rstd[:, 0, t:t + 1], in1=gt[:, cs], op0=ALU.mult, op1=ALU.mult))
                link.wait()
                V.tensor_tensor(x[:, t, :], x[:, t, :], h2(t), ALU.add).then_inc(s_x1, 1)
                dve.wait_ge(s_r, 2 * t + 2)
                dve.wait_ge(s_x1, t + 1)
                link(V.scalar_tensor_tensor(out=h2(t), in0=x[:, t, :], scalar=rstd[:, 1, t:t + 1], in1=g2row,
                                            op0=ALU.mult, op1=ALU.mult))
                V.tensor_tensor(h2(t), h2(t), shift, ALU.add).then_inc(s_h2, 1)


MAXB = NE + S * TOPK // P - 1
NO_TOKEN, NO_ROW = 8 * S, 16 * S * TOPK
BIG = 1e30


def route(nc, w, keep, moe):
    with ExitStack() as stack:
        m = Memory(nc, stack)
        spare = [0]

        def old(*shape):
            size = 1
            for n in shape:
                size *= n
            spare[0] += size
            assert spare[0] <= 5 * D
            flat = keep.mod[:, spare[0] - size:spare[0]]
            names = "abc"[:len(shape)]
            if len(shape) == 1:
                return flat
            return flat.rearrange("p (%s) -> p %s" % (" ".join(names), " ".join(names)), **dict(zip(names, shape)))

        h2 = moe.xg
        h2T = m.sb("h2T", [P, KD, S])
        br = m.sb("b_router", [P, NE])
        ws = m.sb("ws", [P, 2, KD, DE])
        sig, gu = m.sb("sig4", [P, 2, DE]), m.sb("gu4", [P, 2, DE])
        hT = m.sb("hT4", [P, 2, 2, P])
        E = [P, NT, NE]
        wsd, wr, g8 = old(2, D), old(KD, NE), old(NT, NG, 8)
        scores, biased, sel, gated, left, rank, resets = (old(NT, NE) for _ in range(7))
        gs, top4, top8 = (m.sb(n, [P, NT, 8]) for n in ("gs", "top4", "top8"))
        gi = m.sb("gi", [P, NT, 8], U32)
        gif = m.sb("gif", [P, NT, 8])
        eq = m.sb("eq", [P, NT, NG, TOPG])
        gmask = m.sb("gmask", [P, NT, NG])
        total, over = m.sb("total", [P, NT]), m.sb("over", [P, NT])
        iota8i, iota8 = m.sb("iota8i", [P, NG, TOPG], I32), m.sb("iota8", [P, NG, TOPG])
        toki, tokf, pi, pf = m.sb("toki", [P, NT], I32), m.sb("tokf", [P, 3, NT]), m.sb("pi", [P, 1], I32), m.sb("pf", [P, 1])
        iota_i = m.sb("iota_i", [P, S], I32)
        colf, before = m.sb("colf4", [P, P]), m.sb("before", [P, P])
        cnt, more, ends, done_, part = (m.sb(n, [P, NE]) for n in ("cnt", "more", "ends", "done_", "part"))
        bf = m.sb("bf", [P, 4])
        bank = [m.bank(f"d{i}") for i in range(8)]
        table = moe.table

        s_h, s_wr, s_ws = [m.sem(f"p4_h2_{t}_in") for t in range(NT)], m.sem("p4_router_in"), m.sem("p4_shared_in")
        s_io = m.sem("p4_iotas")
        s_t, s_tA, s_tV = m.sem("p4_h2_turned"), m.sem("p4_h2T_by_scalar"), m.sem("p4_h2T_by_vector")
        s_lg, s_sc = m.sem("p4_logits"), m.sem("p4_scores")
        s_sel, s_tri = m.sem("p4_selected"), m.sem("p4_before_mask")
        s_pos, s_blk, s_blkp = m.sem("p4_places"), m.sem("p4_blocks"), m.sem("p4_blocks_turned")
        s_s, s_sA, s_sV = m.sem("p4_shared_up"), m.sem("p4_shared_sigmoid"), m.sem("p4_shared_hidden")
        s_ht, s_htA = m.sem("p4_hidden_turned"), m.sem("p4_hiddenT")
        s_dn, s_dnA = m.sem("p4_shared_down"), m.sem("p4_shared_out")
        s_v = m.sem("p4_vector_chain")
        block = stack.enter_context(nc.Block())

        @block.sync
        def _(sp):
            for t in range(NT):
                sp.dma_start(h2[:, t, :], keep.h2_dram[t * P:(t + 1) * P, :]).then_inc(s_h[t], 16)
            sp.dma_start(wr[:, :, :], w["w_router"][0].rearrange("(k p) n -> p k n", p=P)).then_inc(s_wr, 16)
            sp.dma_start(br[:, :], w["b_router"][0].rearrange("(a n) -> a n", a=1).to_broadcast([P, NE])).then_inc(s_wr, 16)
            for j, name in enumerate(("ws_gate", "ws_up")):
                sp.dma_start(ws[:, j, :, :], w[name][0].rearrange("(k p) n -> p k n", p=P)).then_inc(s_ws, 16)
            sp.dma_start(wsd[:, :, :], w["ws_down"][0].rearrange("(k p) n -> p k n", p=P)).then_inc(s_ws, 16)
            for b in range(moe.RING):
                moe.load(sp, b, b)

        @block.gpsimd
        def _(pool):
            pool.iota(iota8i[:, :, :], [[1, NG], [0, TOPG]], base=0, channel_multiplier=0).then_inc(s_io, 1)
            pool.iota(toki[:, :], [[P, NT]], base=0, channel_multiplier=1).then_inc(s_io, 1)
            pool.iota(pi[:, :], [[0, 1]], base=0, channel_multiplier=1).then_inc(s_io, 1)
            pool.iota(iota_i[:, :], [[1, S]], base=0, channel_multiplier=0).then_inc(s_io, 1)
            pool.memset(resets[:, :, :], 1.0).then_inc(s_io, 1)
            pool.memset(moe.offsets[:, 0:1], float(NO_TOKEN)).then_inc(s_io, 1)
            pool.memset(moe.offsets[:, 1:2], float(NO_ROW)).then_inc(s_io, 1)
            pool.wait_ge(s_io, 7)
            pool.memset(resets[:, :, 0:1], 0.0).then_inc(s_io, 1)

        @block.scalar
        def _(act):
            for t in range(NT):
                act.wait_ge(s_t, 2 * t + 1)
                act.activation(h2T[:, 0:4, t * P:(t + 1) * P], bank[0][:, :].rearrange("p (k s) -> p k s", k=4),
                               ACT.Copy).then_inc(s_tA, 1)
            act.wait_ge(s_lg, 1)
            act.activation(scores[:, :, :], bank[2][:, 0:NT * NE].rearrange("p (t e) -> p t e", t=NT),
                           ACT.Sigmoid).then_inc(s_sc, 1)
            for t in range(NT):
                act.wait_ge(s_s, t + 1)
                if t >= 2:
                    act.wait_ge(s_sV, t - 1)
                act.activation(sig[:, t % 2, :], bank[4 + t % 2][:, 0:DE], ACT.Sigmoid).then_inc(s_sA, 1)
                act.wait_ge(s_ht, t + 1)
                if t >= 2:
                    act.wait_ge(s_dn, t - 1)
                act.activation(hT[:, t % 2, :, :], bank[3][:, 0:2 * P].rearrange("p (k s) -> p k s", k=2),
                               ACT.Copy).then_inc(s_htA, 1)
                act.wait_ge(s_dn, t + 1)
                for half in range(2):
                    act.activation(moe.shared[:, t, half * N:half * N + N], bank[6 + half][:, :], ACT.Copy).then_inc(s_dnA, 1)

        @block.tensor
        def _(pe):
            for t in range(NT):
                pe.wait_ge(s_h[t], 16)
                for half in range(2):
                    if t:
                        pe.wait_ge((s_tA, s_tV)[half], t)
                    for k in range(4):
                        c0 = (half * 4 + k) * P
                        mm = pe.transpose(bank[half][:, k * P:(k + 1) * P], h2[:, t, c0:c0 + P], keep.ident[:, :])
                    mm.then_inc(s_t, 1)
            pe.wait_ge(s_wr, 32)
            pe.wait_ge(s_tA, NT)
            pe.wait_ge(s_tV, NT)
            for t in range(NT):
                for k in range(KD):
                    mm = pe.matmul(bank[2][:, t * NE:(t + 1) * NE], h2T[:, k, t * P:(t + 1) * P], wr[:, k, :],
                                   start=(k == 0), stop=(k == KD - 1))
            mm.then_inc(s_lg, 1)
            pe.wait_ge(s_ws, 48)

            def shared_up(t):
                if t >= 2:
                    pe.wait_ge(s_sV, t - 1)
                for k in range(KD):
                    mm = pe.matmul(bank[4 + t % 2][:, :], h2T[:, k, t * P:(t + 1) * P], ws[:, :, k, :],
                                   start=(k == 0), stop=(k == KD - 1))
                mm.then_inc(s_s, 1)

            def shared_down(t):
                pe.wait_ge(s_sV, t + 1)
                if t:
                    pe.wait_ge(s_htA, t)
                for k in range(2):
                    mm = pe.transpose(bank[3][:, k * P:(k + 1) * P], gu[:, t % 2, k * P:(k + 1) * P], keep.ident[:, :])
                mm.then_inc(s_ht, 1)
                pe.wait_ge(s_htA, t + 1)
                if t:
                    pe.wait_ge(s_dnA, 2 * t)
                for half in range(2):
                    for k in range(2):
                        mm = pe.matmul(bank[6 + half][:, :], hT[:, t % 2, k, :], wsd[:, k, half * N:half * N + N],
                                       start=(k == 0), stop=(k == 1))
                mm.then_inc(s_dn, 1)

            shared_up(0)
            for t in range(NT):
                if t < NT - 1:
                    shared_up(t + 1)
                shared_down(t)
            pe.wait_ge(s_sel, 1)
            pe.wait_ge(s_tri, 1)
            for t in range(NT):
                for u in range(t + 1):
                    pe.matmul(bank[0][:, t * NE:(t + 1) * NE], before[:, :] if u == t else keep.ones[:, :], sel[:, u, :],
                              start=(u == 0), stop=(u == t))
            for u in range(NT):
                mm = pe.matmul(bank[1][:, 0:NE], keep.ones[:, :], sel[:, u, :], start=(u == 0), stop=(u == NT - 1))
            mm.then_inc(s_pos, 1)
            pe.wait_ge(s_blk, 1)
            for j in range(2):
                mm = pe.matmul(bank[2][0:1, j * P:(j + 1) * P], bf[:, j:j + 1], keep.ident[:, :], start=True, stop=True)
            mm.then_inc(s_blkp, 1)

        @block.vector
        def _(dve):
            link = Link(dve, s_v)
            V = nc.vector

            def hidden(t):
                dve.wait_ge(s_sA, t + 1)
                link(V.tensor_tensor(sig[:, t % 2, :], sig[:, t % 2, :], bank[4 + t % 2][:, 0:DE], ALU.mult))
                if t >= 2:
                    dve.wait_ge(s_ht, t - 1)
                V.tensor_tensor(gu[:, t % 2, :], sig[:, t % 2, :], bank[4 + t % 2][:, DE:2 * DE], ALU.mult).then_inc(s_sV, 1)

            dve.wait_ge(s_io, 8)
            link.sign(V.tensor_copy(iota8[:, :, :], iota8i[:, :, :]))
            link.sign(V.tensor_copy(tokf[:, 0, :], toki[:, :]))
            link.sign(V.tensor_copy(pf[:, :], pi[:, :]))
            link.sign(V.tensor_copy(moe.iota[:, :], iota_i[:, :]))
            link(V.tensor_copy(colf[:, :], iota_i[:, 0:P]))
            V.tensor_scalar(before[:, :], colf[:, :], pf[:, 0:1], None, ALU.is_gt).then_inc(s_tri, 1)
            link.sign(V.tensor_scalar(tokf[:, 1, :], tokf[:, 0, :], float(-NO_TOKEN), None, ALU.add))
            link.sign(V.tensor_scalar(tokf[:, 2, :], tokf[:, 0, :], float(TOPK), float(-NO_ROW), ALU.mult, ALU.add))
            for t in range(NT):
                dve.wait_ge(s_t, 2 * t + 2)
                V.tensor_copy(h2T[:, 4:8, t * P:(t + 1) * P],
                              bank[1][:, :].rearrange("p (k s) -> p k s", k=4)).then_inc(s_tV, 1)
            dve.wait_ge(s_sc, 1)
            dve.wait_ge(s_wr, 32)
            link(V.tensor_tensor(biased[:, :, :], scores[:, :, :], br[:, :].unsqueeze(1).to_broadcast(E), ALU.add))
            hidden(0)
            for t in range(NT):
                for g in range(NG):
                    link.sign(V.max(g8[:, t, g, :], biased[:, t, g * PER:(g + 1) * PER]))
            link.wait()
            link(V.tensor_tensor(gs[:, :, :], g8[:, :, :, 0], g8[:, :, :, 1], ALU.add))
            hidden(1)
            for t in range(NT):
                link.sign(V.max(top4[:, t, :], gs[:, t, :]))
            link.wait()
            for t in range(NT):
                link.sign(V.max_index(gi[:, t, :], top4[:, t, :], gs[:, t, :]))
            link.wait()
            link(V.tensor_copy(gif[:, :, :], gi[:, :, :]))
            for t in range(NT):
                link.sign(V.tensor_tensor(eq[:, t, :, :], iota8[:, :, :],
                                          gif[:, t, 0:TOPG].unsqueeze(1).to_broadcast([P, NG, TOPG]), ALU.is_equal))
            link.wait()
            link(V.tensor_reduce(gmask[:, :, :], eq[:, :, :, :], AX.X, ALU.add))
            link(V.tensor_scalar(gmask[:, :, :], gmask[:, :, :], -1.0, BIG, ALU.add, ALU.mult))
            hidden(2)
            for t in range(NT):
                link.sign(V.tensor_tensor(biased[:, t, :].rearrange("p (g m) -> p g m", g=NG),
                                          biased[:, t, :].rearrange("p (g m) -> p g m", g=NG),
                                          gmask[:, t, :].unsqueeze(2).to_broadcast([P, NG, PER]), ALU.add))
            link.wait()
            for t in range(NT):
                link.sign(V.max(top8[:, t, :], biased[:, t, :]))
            link.wait()
            hidden(3)
            for t in range(NT):
                link.sign(V.match_replace(out=left[:, t, :], in_to_replace=top8[:, t, :], in_values=biased[:, t, :],
                                          imm_value=-2.0 * BIG))
            link.wait()
            V.tensor_tensor(sel[:, :, :], left[:, :, :], biased[:, :, :], ALU.is_lt).then_inc(s_sel, 1)
            dve.wait_ge(s_sel, 1)
            link(V.tensor_tensor(gated[:, :, :], scores[:, :, :], sel[:, :, :], ALU.mult))
            link(V.tensor_reduce(total[:, :], gated[:, :, :], AX.X, ALU.add))
            link(V.reciprocal(over[:, :], total[:, :]))
            for t in range(NT):
                link.sign(V.tensor_scalar(table[:, t, :, 0], gated[:, t, :], over[:, t:t + 1], SCALE, ALU.mult, ALU.mult))
                link.sign(V.tensor_scalar(table[:, t, :, 1], sel[:, t, :], 0.0, tokf[:, 1, t:t + 1], ALU.mult, ALU.add))
            link(V.tensor_tensor_scan(rank[:, :, :].rearrange("p t e -> p (t e)"), resets[:, :, :].rearrange("p t e -> p (t e)"),
                                      sel[:, :, :].rearrange("p t e -> p (t e)"), 0.0, ALU.mult, ALU.add))
            link(V.tensor_tensor(rank[:, :, :], rank[:, :, :], sel[:, :, :], ALU.subtract))
            for t in range(NT):
                link.sign(V.tensor_scalar(table[:, t, :, 2], rank[:, t, :], tokf[:, 2, t:t + 1], None, ALU.add))
            dve.wait_ge(s_pos, 1)
            link(V.tensor_scalar(left[:, :, :], sel[:, :, :], -1.0, 4.0 * S, ALU.add, ALU.mult))
            link.sign(V.tensor_tensor(table[:, :, :, 3], left[:, :, :],
                                      bank[0][:, 0:NT * NE].rearrange("p (t e) -> p t e", t=NT), ALU.add))
            link(V.tensor_copy(cnt[:, :], bank[1][:, 0:NE]))
            link(V.tensor_scalar(more[:, :], cnt[:, :], float(P), None, ALU.is_gt))
            for j in range(2, NT):
                link(V.tensor_scalar(part[:, :], cnt[:, :], float(j * P), None, ALU.is_gt))
                link(V.tensor_tensor(more[:, :], more[:, :], part[:, :], ALU.add))
            link(V.tensor_tensor_scan(ends[:, :], keep.ones[:, 0:NE], more[:, :], float(NE), ALU.mult, ALU.add))
            link(V.tensor_copy(moe.n_blocks[0:1, :], ends[0:1, NE - 1:NE]))
            link(V.tensor_scalar(done_[:, :], ends[:, :], pf[:, 0:1], None, ALU.is_le))
            link(V.tensor_tensor(part[:, :], done_[:, :], more[:, :], ALU.mult))
            link(V.tensor_reduce(bf[:, 2:3], done_[:, :], AX.X, ALU.add))
            link(V.tensor_reduce(bf[:, 3:4], part[:, :], AX.X, ALU.add))
            link(V.tensor_scalar(bf[:, 3:4], bf[:, 3:4], -1.0, pf[:, 0:1], ALU.mult, ALU.add))
            link(V.tensor_scalar(bf[:, 3:4], bf[:, 3:4], float(1 - NE), float(P), ALU.add, ALU.mult))
            link(V.tensor_scalar(bf[:, 2:3], bf[:, 2:3], float(NE - 1), None, ALU.min))
            link(V.tensor_scalar(part[:, 0:1], pf[:, :], float(NE), None, ALU.is_lt))
            link(V.tensor_scalar(bf[:, 3:4], bf[:, 3:4], 0.0, float(S - P), ALU.max, ALU.min))
            link(V.tensor_scalar(part[:, 1:2], part[:, 0:1], -1.0, 1.0, ALU.mult, ALU.add))
            link(V.tensor_tensor(bf[:, 1:2], bf[:, 3:4], part[:, 1:2], ALU.mult))
            link(V.tensor_tensor(bf[:, 2:3], bf[:, 2:3], part[:, 1:2], ALU.mult))
            link(V.tensor_tensor(part[:, 2:3], pf[:, :], part[:, 0:1], ALU.mult))
            V.tensor_tensor(bf[:, 0:1], bf[:, 2:3], part[:, 2:3], ALU.add).then_inc(s_blk, 1)
            dve.wait_ge(s_blkp, 1)
            link(V.tensor_copy(moe.blocks[0:1, :, :].rearrange("p a b -> p (a b)"), bank[2][0:1, 0:2 * P]))


def plan_experts(nc, m, w, keep, moe):
    moe.RING = 4
    moe.ring = m.sb("expert_ring", [P, moe.RING, 3 * KD * DE])
    moe.table = m.sb("table", [P, NT, NE, 4])
    moe.iota = m.sb("iota", [P, S])
    moe.xg = m.sb("xg", [P, 4, D])
    moe.blocks = m.sb("blocks", [1, 2, P], I32)
    moe.n_blocks = m.sb("n_blocks", [1, 1], I32)
    moe.offsets = m.sb("offsets", [P, 2])
    moe.s_ring = [m.sem(f"expert_slot{i}_in") for i in range(moe.RING)]
    moe.rows = nc.dram_tensor("expert_rows", (S * TOPK, D), F32, kind="Internal").ap()
    width = KD * DE
    parts = [w["we_gate"][0].rearrange("e (p k) n -> e p (k n)", k=KD),
             w["we_up"][0].rearrange("e (p k) n -> e p (k n)", k=KD),
             w["we_down"][0].rearrange("e (p k) n -> e p (k n)", k=2)]

    def load(engine, expert, slot):
        for j, part in enumerate(parts):
            source = part[expert] if isinstance(expert, int) else part[bass.ds(expert, 1)].rearrange("a p n -> (a p) n")
            engine.dma_start(moe.ring[:, slot, j * width:(j + 1) * width], source).then_inc(moe.s_ring[slot], 16)

    moe.load = load


def experts(nc, w, keep, moe):
    with ExitStack() as stack:
        m = Memory(nc, stack)
        RING = moe.RING
        hot = m.sb("hot", [P, 2, NT, P])
        column = m.sb("column", [P, 2, NT, 4])
        gate = m.sb("gate", [P, 4, 1])
        ids = m.sb("ids", [P, 4, 2], U32)
        xT = m.sb("xT", [P, 2, KD, P])
        sig = m.sb("sig5", [P, 2, DE])
        hid = m.sb("hid", [P, 2, DE])
        hT = m.sb("hT5", [P, 2, 2, P])
        y = m.sb("y5", [P, 2, D])
        px = [m.bank(f"px{i}") for i in range(2)]
        pgu = [m.bank(f"pgu{i}") for i in range(2)]
        py = [m.bank(f"py{i}") for i in range(2)]
        ph, pid = m.bank("ph"), m.bank("pid")
        carrier = m.sb("carrier", [1, 2])

        s_gather, s_scatter = m.sem("p5_gather_may_start"), m.sem("p5_scatter_may_start")
        s_col = m.sem("p5_column")
        s_hot = m.sem("p5_one_hot")
        s_id = m.sem("p5_ids_product")
        s_ids = m.sem("p5_ids")
        s_xg = [m.sem(f"p5_gathered{i}") for i in range(4)]
        s_x = m.sem("p5_x_turned")
        s_xA, s_xV = m.sem("p5_xT_by_scalar"), m.sem("p5_xT_by_vector")
        s_gu = m.sem("p5_up")
        s_sig, s_t, s_hid = m.sem("p5_sigmoid"), m.sem("p5_silu"), m.sem("p5_hidden")
        s_h, s_hA = m.sem("p5_hidden_turned"), m.sem("p5_hiddenT")
        s_y, s_yA, s_yV = m.sem("p5_down"), m.sem("p5_y_by_scalar"), m.sem("p5_y_by_vector")
        s_out = [m.sem(f"p5_scattered{i}") for i in range(2)]
        block = stack.enter_context(nc.Block())
        MAIN = NE - 4
        STEPS = (MAXB + 3) // 4 * 4

        def steps(engine, stages, last=None):
            most = max(lead for lead, _ in stages)
            for i in range(-most, 4):
                for lead, code in stages:
                    if i + lead >= 0 and (i >= 0 or i + lead < lead):
                        code(i + lead, i + lead)
            with engine.Fori(1, MAIN // 4) as turn:
                for u in range(4):
                    for lead, code in stages:
                        code(4 * turn + (u + lead), u + lead)
            count = engine.value_load(moe.n_blocks[0:1, 0:1], min_val=NE, max_val=MAXB)
            with engine.Fori(MAIN // 4, STEPS // 4) as turn:
                for u in range(4):
                    for lead, code in stages:
                        with engine.If(4 * turn + (u + lead) < count):
                            code(4 * turn + (u + lead), u + lead)
                            if last is not None and lead == 0:
                                last(4 * turn + u, u)

        def taken(engine, semaphore, b, back, per=1):
            if isinstance(b, int) and b < back:
                return
            engine.wait_ge(semaphore, per * (b - back + 1))

        def left(engine, b, u, back):
            if isinstance(b, int) and b < back:
                return
            engine.wait_ge(s_out[u % 2], 8 * b + (16 - 8 * (u % 2) - 8 * back))

        @block.sync
        def _(sp):
            with sp.Fori(1, NE // RING) as turn:
                for u in range(RING):
                    sp.wait_ge(s_y, RING * turn + (u - RING + 1))
                    moe.load(sp, RING * turn + u, u)
            count = sp.value_load(moe.n_blocks[0:1, 0:1], min_val=NE, max_val=MAXB)
            with sp.Fori(NE // RING, STEPS // RING) as turn:
                for u in range(RING):
                    with sp.If(RING * turn + u < count):
                        sp.wait_ge(s_y, RING * turn + (u - RING + 1))
                        expert = sp.value_load(moe.blocks[0:1, 0, bass.ds(RING * turn + u, 1)], min_val=0, max_val=NE - 1)
                        moe.load(sp, expert, u)

        @block.gpsimd
        def _(pool):
            last_token, last_row = pool.to_reg(S - 1), pool.to_reg(S * TOPK - 1)

            def carry_wait(semaphore, b, place):
                taken(pool, semaphore, b, 1)
                nc.gpsimd.tensor_tensor(carrier[0:1, place:place + 1], moe.offsets[0:1, 0:1], moe.offsets[0:1, 0:1],
                                        ALU.add).then_inc(semaphore, 1)

            def gather(b, u):
                pool.wait_ge(s_ids, b + 1)
                taken(pool, s_x, b, 4)
                carry_wait(s_gather, b, 0)
                pool.indirect_dma_start(moe.xg[:, u % 4, :], None, keep.h2_dram,
                                        bass.IndirectOffsetOnAxis(ids[:, u % 4, 0:1], 0),
                                        bounds_check=last_token, oob_is_err=False).then_inc(s_xg[u % 4], 16)

            def scatter(b, u):
                pool.wait_ge(s_yA, b + 1)
                pool.wait_ge(s_yV, b + 1)
                carry_wait(s_scatter, b, 1)
                pool.indirect_dma_start(moe.rows, bass.IndirectOffsetOnAxis(ids[:, u % 4, 1:2], 0), y[:, u % 2, :], None,
                                        bounds_check=last_row, oob_is_err=False).then_inc(s_out[u % 2], 16)

            steps(pool, [(2, gather), (0, scatter)], lambda b, u: left(pool, b, u, 0))

        @block.scalar
        def _(act):
            def xT_half(b, u):
                act.wait_ge(s_x, b + 1)
                taken(act, s_gu, b, 2)
                act.activation(xT[:, u % 2, 0:4, :], px[0][:, :].rearrange("p (k s) -> p k s", k=4), ACT.Copy).then_inc(s_xA, 1)

            def sigmoid(b, u):
                act.wait_ge(s_gu, b + 1)
                taken(act, s_hid, b, 2)
                act.activation(sig[:, u % 2, :], pgu[u % 2][:, 0:DE], ACT.Sigmoid).then_inc(s_sig, 1)

            def down(b, u):
                act.wait_ge(s_h, b + 1)
                taken(act, s_y, b, 2)
                act.activation(hT[:, u % 2, :, :], ph[:, 0:2 * P].rearrange("p (k s) -> p k s", k=2), ACT.Copy).then_inc(s_hA, 1)
                act.wait_ge(s_y, b + 1)
                left(act, b, u, 2)
                act.activation(y[:, u % 2, 0:N], py[0][:, :], ACT.Copy).then_inc(s_yA, 1)

            steps(act, [(1, xT_half), (0, down), (1, sigmoid)])

        @block.tensor
        def _(pe):
            def places(b, u):
                pe.wait_ge(s_hot, b + 1)
                taken(pe, s_ids, b, 1)
                for t in range(NT):
                    mm = pe.matmul(pid[:, 0:4], hot[:, u % 2, t, :], column[:, u % 2, t, :], start=(t == 0), stop=(t == NT - 1))
                mm.then_inc(s_id, 1)

            def up(b, u):
                if isinstance(b, int):
                    pe.wait_ge(s_xg[u % 4], 16 * (b // 4 + 1))
                else:
                    pe.wait_ge(s_xg[u % 4], 4 * b + (16 - 4 * (u % 4)))
                taken(pe, s_xA, b, 1)
                taken(pe, s_xV, b, 1)
                rows = moe.xg[:, u % 4, :].rearrange("p (d k) -> p k d", k=KD)
                for k in range(KD):
                    mm = pe.transpose(px[k // 4][:, (k % 4) * P:(k % 4 + 1) * P], rows[:, k, :], keep.ident[:, :])
                mm.then_inc(s_x, 1)
                if isinstance(b, int):
                    pe.wait_ge(moe.s_ring[u % RING], 48 * (b // RING + 1))
                else:
                    pe.wait_ge(moe.s_ring[u % RING], 12 * b + (48 - 12 * (u % RING)))
                pe.wait_ge(s_xA, b + 1)
                pe.wait_ge(s_xV, b + 1)
                taken(pe, s_hid, b, 2)
                weights = moe.ring[:, u % RING, 0:2 * KD * DE].rearrange("p (j k n) -> p k j n", j=2, k=KD)
                for k in range(KD):
                    mm = pe.matmul(pgu[u % 2][:, :], xT[:, u % 2, k, :], weights[:, k, :, :], start=(k == 0), stop=(k == KD - 1))
                mm.then_inc(s_gu, 1)

            def down(b, u):
                pe.wait_ge(s_hid, b + 1)
                taken(pe, s_hA, b, 1)
                rows = hid[:, u % 2, :].rearrange("p (d k) -> p k d", k=2)
                for k in range(2):
                    mm = pe.transpose(ph[:, k * P:(k + 1) * P], rows[:, k, :], keep.ident[:, :])
                mm.then_inc(s_h, 1)
                pe.wait_ge(s_hA, b + 1)
                taken(pe, s_yA, b, 1)
                taken(pe, s_yV, b, 1)
                weights = moe.ring[:, u % RING, 2 * KD * DE:3 * KD * DE].rearrange("p (k n) -> p k n", k=2)
                for half in range(2):
                    for k in range(2):
                        mm = pe.matmul(py[half][:, :], hT[:, u % 2, k, :], weights[:, k, half * N:half * N + N],
                                       start=(k == 0), stop=(k == 1))
                mm.then_inc(s_y, 1)

            steps(pe, [(2, places), (1, up), (0, down)])

        @block.vector
        def _(dve):
            V = nc.vector

            def places(b, u):
                if isinstance(b, int):
                    expert, first = b, 0
                else:
                    expert = dve.value_load(moe.blocks[0:1, 0, bass.ds(b, 1)], min_val=0, max_val=NE - 1)
                    first = dve.value_load(moe.blocks[0:1, 1, bass.ds(b, 1)], min_val=0, max_val=S - P)
                taken(dve, s_id, b, 2)
                V.tensor_copy(column[:, u % 2, :, :].unsqueeze(2), moe.table[:, :, bass.ds(expert, 1), :]).then_inc(s_col, 1)
                dve.wait_ge(s_col, b + 1)
                for t in range(NT):
                    last = V.tensor_scalar(hot[:, u % 2, t, :], moe.iota[:, bass.ds(first, P)], column[:, u % 2, t, 3:4], None,
                                           ALU.is_equal)
                last.then_inc(s_hot, 1)

            def numbers(b, u):
                dve.wait_ge(s_id, b + 1)
                left(dve, b, u, 4)
                V.tensor_copy(gate[:, u % 4, :], pid[:, 0:1])
                V.tensor_tensor(ids[:, u % 4, :], pid[:, 1:3], moe.offsets[:, :], ALU.add).then_inc(s_ids, 1)

            def xT_half(b, u):
                dve.wait_ge(s_x, b + 1)
                taken(dve, s_gu, b, 2)
                V.tensor_copy(xT[:, u % 2, 4:8, :], px[1][:, :].rearrange("p (k s) -> p k s", k=4)).then_inc(s_xV, 1)

            def hidden(b, u):
                dve.wait_ge(s_sig, b + 1)
                V.scalar_tensor_tensor(out=sig[:, u % 2, :], in0=pgu[u % 2][:, 0:DE], scalar=gate[:, u % 4, :], in1=sig[:, u % 2, :],
                                       op0=ALU.mult, op1=ALU.mult).then_inc(s_t, 1)
                dve.wait_ge(s_t, b + 1)
                taken(dve, s_h, b, 2)
                V.tensor_tensor(hid[:, u % 2, :], sig[:, u % 2, :], pgu[u % 2][:, DE:2 * DE], ALU.mult).then_inc(s_hid, 1)

            def y_half(b, u):
                dve.wait_ge(s_y, b + 1)
                left(dve, b, u, 2)
                V.tensor_copy(y[:, u % 2, N:2 * N], py[1][:, :]).then_inc(s_yV, 1)

            steps(dve, [(2, places), (2, numbers), (1, xT_half), (0, y_half), (1, hidden)])


def combine(nc, w, keep, moe, out):
    with ExitStack() as stack:
        m = Memory(nc, stack)
        rows = m.sb("rows6", [P, 2, TOPK * D])
        x1 = m.sb("x6", [P, NT, D])
        y = m.sb("y6", [P, 2, D])
        sq = m.sb("sq6", [P, D])
        sums, mean_sq, rstd = m.sb("sums6", [P, NT]), m.sb("mean_sq6", [P, NT]), m.sb("rstd6", [P, NT])
        s_in, s_x = m.sem("p6_rows_in"), m.sem("p6_x1_in")
        s_red, s_y, s_sq, s_r, s_o, s_st = (m.sem(f"p6_{n}") for n in ("reduced", "y", "squares", "rstd", "out", "stored"))
        s_v, s_a = m.sem("p6_vector_chain"), m.sem("p6_scalar_chain")
        s_in = [m.sem(f"p6_rows{i}_in") for i in range(2)]
        block = stack.enter_context(nc.Block())
        expert_rows = moe.rows.rearrange("(t p j) d -> t p (j d)", p=P, j=TOPK)

        @block.sync
        def _(sp):
            for t in range(NT):
                if t >= 2:
                    sp.wait_ge(s_red, t - 1)
                sp.dma_start(rows[:, t % 2, :], expert_rows[t]).then_inc(s_in[t % 2], 16)
                if t == 0:
                    sp.dma_start(x1[:, :, :], keep.x1_dram.rearrange("(t p) d -> p t d", p=P)).then_inc(s_x, 16)
            for t in range(NT):
                sp.wait_ge(s_o, t + 1)
                sp.dma_start(out[0, t * P:(t + 1) * P, :], x1[:, t, :]).then_inc(s_st, 16)
            sp.wait_ge(s_st, 16 * NT)

        @block.gpsimd
        def _(pool):
            for t in range(NT):
                pool.wait_ge(s_sq, t + 1)
                pool.tensor_tensor(rstd[:, t:t + 1], mean_sq[:, t:t + 1], keep.power[:, 0:1], ALU.pow).then_inc(s_r, 1)

        @block.scalar
        def _(act):
            link = Link(act, s_a)
            for t in range(NT):
                act.wait_ge(s_y, t + 1)
                link(act.activation(sq[:, :], y[:, t % 2, :], ACT.Square, accum_out=sums[:, t:t + 1]))
                act.activation(mean_sq[:, t:t + 1], sums[:, t:t + 1], ACT.Copy, scale=1.0 / D, bias=RMS_EPS).then_inc(s_sq, 1)

        @block.vector
        def _(dve):
            link = Link(dve, s_v)
            V = nc.vector
            gt = keep.mod[:, 5 * D:6 * D]

            def finish(t):
                dve.wait_ge(s_r, t + 1)
                dve.wait_ge(s_x, 16)
                link(V.scalar_tensor_tensor(out=y[:, t % 2, :], in0=y[:, t % 2, :], scalar=rstd[:, t:t + 1], in1=gt,
                                            op0=ALU.mult, op1=ALU.mult))
                V.tensor_tensor(x1[:, t, :], x1[:, t, :], y[:, t % 2, :], ALU.add).then_inc(s_o, 1)

            for t in range(NT):
                dve.wait_ge(s_in[t % 2], 16 * (t // 2 + 1))
                if t >= 2:
                    dve.wait_ge(s_o, t - 1)
                V.tensor_reduce(y[:, t % 2, :], rows[:, t % 2, :].rearrange("p (j d) -> p d j", j=TOPK), AX.X,
                                ALU.add).then_inc(s_red, 1)
                dve.wait_ge(s_red, t + 1)
                V.tensor_tensor(y[:, t % 2, :], y[:, t % 2, :], moe.shared[:, t, :], ALU.add).then_inc(s_y, 1)
                if t:
                    finish(t - 1)
            finish(NT - 1)


class Names:
    pass


def layer(nc, w, out):
    with ExitStack() as stack:
        m = Memory(nc, stack)
        keep = Names()
        keep.mod = m.sb("mod", [P, 6 * D])
        keep.ident = m.sb("ident", [P, P])
        keep.ones = m.sb("ones", [P, P])
        keep.power = m.sb("power", [P, 8])
        keep.vec = m.sb("vec", [P, N_VEC])
        keep.one_minus_mu = m.sb("one_minus_mu", [P, NZ_RWKV])
        keep.silu_c = m.sb("silu_c", [P, KD])
        keep.x1_dram = nc.dram_tensor("x1_rows", (S, D), F32, kind="Internal").ap()
        keep.h2_dram = nc.dram_tensor("h2_rows", (S, D), F32, kind="Internal").ap()
        with ExitStack() as mix_stack:
            mm = Memory(nc, mix_stack)
            mix = Names()
            mix.gates = mm.sb("gates", [P, NZ_GATE, S])
            mix.zr = mm.sb("zr", [P, NZ_RWKV, S])
            mix.co = mm.sb("co", [P, RT_, S])
            mix.taps = mm.sb("taps", [P, N_TAP])
            project(nc, w, keep, mix)
            mix.gate_r = mm.sb("gate_r", [P, RT_, S])
            mix.bonus = mm.sb("bonus", [P, RT_, S])
            rwkv(nc, w, keep, mix)
            merge(nc, w, keep, mix)
        moe = Names()
        moe.shared = m.sb("shared", [P, NT, D])
        with ExitStack() as moe_stack:
            me = Memory(nc, moe_stack)
            plan_experts(nc, me, w, keep, moe)
            route(nc, w, keep, moe)
            experts(nc, w, keep, moe)
        combine(nc, w, keep, moe, out)


_INS = ["x", "c", "w_ada", "b_ada", "norm_mix_pre", "norm_mix_post", "norm_ffn_pre", "norm_ffn_post", "w_in",
        "mu_shift", "conv_w", "conv_b", "conv_ln_g", "conv_ln_b", "p_conv", "w0", "w2", "a0", "a2", "g2", "k_k",
        "k_a", "r_k", "gn_g", "gn_b", "p_rwkv", "w_o", "w_router", "b_router", "we_gate", "we_up", "we_down",
        "ws_gate", "ws_up", "ws_down"]


def kernel(**inputs):
    import numpy as np
    import concourse.bacc as bacc
    from concourse.bass_utils import run_bass_kernel_spmd

    nc = bacc.Bacc("TRN2", target_bir_lowering=False, num_devices=1)
    arrays, w = {}, {}
    for name in _INS:
        a = np.ascontiguousarray(inputs[name])
        arrays[f"in_{name}"] = a
        w[name] = nc.dram_tensor(f"in_{name}", a.shape, mybir.dt.from_np(a.dtype), kind="ExternalInput").ap()
    out = nc.dram_tensor("out_rows", (1, S, D), F32, kind="ExternalOutput").ap()
    layer(nc, w, out)
    result = run_bass_kernel_spmd(nc, [arrays], core_ids=[0])
    return result.results[0]["out_rows"]
```

```python
from contextlib import ExitStack

import concourse.bass as bass
from concourse import mybir

F32 = mybir.dt.float32
F32R = mybir.dt.float32r
I32 = mybir.dt.int32
U32 = mybir.dt.uint32
ALU = mybir.AluOpType
ACT = mybir.ActivationFunctionType
AX = mybir.AxisListType

P = 128
D = 1024
S = 512
KD = D // P
NT = S // P
CW = 512
CK = 31
RW = 512
RT_ = RW // P
HEADS, HD = 8, 64
LORA_W, LORA_A, LORA_G = 64, 64, 128
COL_CONV = 2 * CW
COL_RWKV = 3 * RW + LORA_W + LORA_A + LORA_G
COL_GATE = 2 * D
NE, NG, PER, TOPK, TOPG = 64, 8, 8, 8, 4
DE = 256
SCALE = 2.5
RMS_EPS, LN_EPS, GN_EPS = 1e-6, 1e-5, 64e-5
DECAY = float(0.6065306597126334)
N = 512


class Link:

    def __init__(self, engine, semaphore):
        self.engine, self.semaphore, self.count = engine, semaphore, 0

    def sign(self, instruction):
        self.count += 1
        instruction.then_inc(self.semaphore, 1)
        return self.count

    def wait(self, count=None):
        self.engine.wait_ge(self.semaphore, self.count if count is None else count)

    def __call__(self, instruction):
        self.sign(instruction)
        self.wait()


class Memory:

    def __init__(self, nc, stack):
        self.nc, self.stack, self.semaphores = nc, stack, []

    def sb(self, name, shape, dtype=F32):
        return self.stack.enter_context(self.nc.sbuf_tensor(name, shape, dtype))

    def bank(self, name, shape=None):
        return self.stack.enter_context(self.nc.psum_tensor(name, shape or [P, N], F32))

    def sem(self, name):
        self.semaphores.append(self.nc.alloc_semaphore(name=name))
        return self.semaphores[-1]

    def reset_semaphores(self):
        self.nc.clear_and_free_semaphores(self.semaphores)
        self.nc.all_engine_barrier()




VEC_ROWS = [("mu_shift", COL_RWKV // P), ("conv_b", 4), ("conv_ln_g", 4), ("conv_ln_b", 4), ("w0", 4),
            ("a0", 4), ("k_k", 4), ("k_a", 4), ("r_k", 4), ("gn_g", 4), ("gn_b", 4)]
VEC_AT = {}
_row = 0
for _name, _count in VEC_ROWS:
    VEC_AT[_name] = _row
    _row += _count
N_VEC = _row
N_TAP = CK * (CW // P)
GAINS = ["norm_mix_pre", "norm_mix_post", "norm_ffn_pre", "norm_ffn_post"]
ADA = 6 * D // N
N_WIDE = ADA + 2 * len(GAINS)

IN_SLICES = ([(COL_CONV + o, min(N, COL_RWKV - o)) for o in range(0, COL_RWKV, N)]
             + [(o, N) for o in range(0, COL_CONV, N)]
             + [(COL_CONV + COL_RWKV + o, N) for o in range(0, COL_GATE, N)])
STREAM = [("ada", i) for i in range(4)]
_ada = 4
for _i in range(len(IN_SLICES)):
    STREAM.append(("in", _i))
    if _i >= 1 and _ada < ADA:
        STREAM.append(("ada", _ada))
        _ada += 1
while _ada < ADA:
    STREAM.append(("ada", _ada))
    _ada += 1
STREAM_AT = {item: n for n, item in enumerate(STREAM)}
RING1 = 3
PAIR = 2 * P
FIRST = 4
DIRECT = 2
Z_TILES = [(s, t) for s, (_, w) in enumerate(IN_SLICES) for t in range(w // P)]
NZ_RWKV, NZ_CONV, NZ_GATE = COL_RWKV // P, COL_CONV // P, COL_GATE // P


def project(nc, w, keep, mix):
    with ExitStack() as stack:
        m = Memory(nc, stack)
        with ExitStack() as first_use:
            mf = Memory(nc, first_use)
            ring = mf.sb("ring1", [P, RING1, KD, N])
            x = mf.sb("x1", [P, NT, D])
            hT = mf.sb("hT", [P, KD, S])
        ring_lo = m.sb("ring_lo", [P, RING1, KD, N], F32R)
        h_hi = m.sb("h_hi", [P, KD, S], F32R)
        h_lo = m.sb("h_lo", [P, KD, S], F32R)
        w_hi = m.sb("w_hi", [P, 2, KD, PAIR], F32R)
        glu = mix.gates[:, NZ_GATE - 2:, :]
        upad = m.sb("upad", [P, RT_, CK - 1 + S])
        acc = m.sb("ada_acc", [P, 2, N])
        crow = m.sb("crow", [KD, P])
        modcol = m.sb("modcol", [P, 2 * KD])
        vrows = m.sb("vrows", [N_VEC, P])
        trows = m.sb("trows", [N_TAP, P])
        wide = m.sb("wide", [N_WIDE, N])
        mean_sq = m.sb("mean_sq", [P, NT])
        rstd = m.sb("rstd1", [P, NT])
        sums = m.sb("sums1", [P, NT])
        pz = [m.bank(f"pz{i}") for i in range(3)]
        pt = [m.bank(f"pt{i}") for i in range(2)]
        pm, pg = [m.bank(f"pm{i}") for i in range(2)], m.bank("pg")
        vec, taps = keep.vec, mix.taps

        s_const = m.sem("p1_const")
        s_crow, s_wide, s_vrows, s_x = m.sem("p1_c_in"), m.sem("p1_wide_in"), m.sem("p1_vrows_in"), m.sem("p1_x_in")
        s_slot = [m.sem(f"p1_slot{i}_in") for i in range(RING1)]
        s_cT, s_sig, s_silu = m.sem("p1_c_turned"), m.sem("p1_c_sigmoid"), m.sem("p1_silu_c")
        s_vecT, s_vec = m.sem("p1_vec_turned"), m.sem("p1_vec_ready")
        s_sq, s_rstd = m.sem("p1_squares"), m.sem("p1_rstd")
        s_xA, s_xV = m.sem("p1_x_scaled_by_scalar"), m.sem("p1_x_scaled_by_vector")
        s_ada, s_adam = m.sem("p1_ada_partial"), m.sem("p1_ada_summed")
        s_gain, s_adag = m.sem("p1_gain_row"), m.sem("p1_gain_copied")
        s_mod = m.sem("p1_mod_row")
        s_col, s_colV = m.sem("p1_mod_columns"), m.sem("p1_mod_columns_taken")
        s_ht, s_hA = m.sem("p1_x_turned"), m.sem("p1_xT_taken")
        s_mod_h, s_hlo = m.sem("p1_hT"), m.sem("p1_h_lo")
        s_whi, s_wlo = m.sem("p1_w_hi"), m.sem("p1_w_lo")
        s_hhi = m.sem("p1_h_hi")
        s_z = m.sem("p1_z")
        s_zA, s_zV = m.sem("p1_z_taken_by_scalar"), m.sem("p1_z_taken_by_vector")
        s_v, s_a = m.sem("p1_vector_chain"), m.sem("p1_scalar_chain")
        s_glu = m.sem("p1_glu")
        block = stack.enter_context(nc.Block())

        def vcol(name, i=0):
            return vec[:, VEC_AT[name] + i:VEC_AT[name] + i + 1]

        def slot_wait(engine, item):
            n = STREAM_AT[item]
            engine.wait_ge(s_slot[n % RING1], 16 * (n // RING1 + 1))

        z_end, total = [], 0
        for _, width in IN_SLICES:
            total += width // P
            z_end.append(total)

        def free_wait(engine, item):
            kind, i = item
            if kind == "ada":
                engine.wait_ge(s_adam, i + 1)
            else:
                engine.wait_ge(s_z, z_end[i])

        def exact(ap):
            return ap.bitcast(F32)

        def pair(buffer, b):
            s, t = Z_TILES[2 * b]
            return buffer[:, STREAM_AT[("in", s)] % RING1, :, t * P:t * P + PAIR]

        def has_gain(i):
            return (i // 2) % 3 > 0

        def gains_to(i):
            return sum(has_gain(j) for j in range(i))

        @block.sync
        def _(sp):
            sp.dma_start(crow[:, :], w["c"][0].rearrange("(r n) -> r n", n=P)).then_inc(s_crow, 16)
            sp.dma_start(wide[0:ADA, :], w["b_ada"][0].rearrange("(r n) -> r n", n=N)).then_inc(s_wide, 16)
            for g, name in enumerate(GAINS):
                sp.dma_start(wide[ADA + 2 * g:ADA + 2 * g + 2, :],
                              w[name][0].rearrange("(r n) -> r n", n=N)).then_inc(s_wide, 16)
            sp.dma_start(x[:, :, :], w["x"][0].rearrange("(t p) d -> p t d", p=P)).then_inc(s_x, 16)
            for n, (kind, i) in enumerate(STREAM):
                if n >= RING1:
                    free_wait(sp, STREAM[n - RING1])
                if kind == "ada":
                    at, width, source = i * N, N, w["w_ada"][0]
                else:
                    (at, width), source = IN_SLICES[i], w["w_in"][0]
                sp.dma_start(ring[:, n % RING1, :, 0:width],
                             source[:, at:at + width].rearrange("(k p) n -> p k n", p=P)).then_inc(
                                 s_slot[n % RING1], 16)

        @block.gpsimd
        def _(pool):
            pool.memset(keep.ident[:, :], 0.0).then_inc(s_const, 1)
            pool.memset(keep.ones[:, :], 1.0).then_inc(s_const, 1)
            pool.memset(keep.power[:, :], -0.5).then_inc(s_const, 1)
            pool.memset(upad[:, :, 0:CK - 1], 0.0).then_inc(s_const, 1)
            pool.wait_ge(s_const, 4)
            pool.affine_select(out=keep.ident[:, :], in_=keep.ident[:, :], compare_op=ALU.not_equal, fill=1.0,
                               base=0, pattern=[[-1, P]], channel_multiplier=1).then_inc(s_const, 1)
            pool.wait_ge(s_sq, 1)
            pool.tensor_tensor(rstd[:, :], mean_sq[:, :], keep.power[:, 0:NT], ALU.pow).then_inc(s_rstd, 1)
            for b in range(len(Z_TILES) // 2):
                pool.wait_ge(s_whi, b + 1)
                pool.tensor_tensor(pair(ring_lo, b), pair(ring, b), exact(w_hi[:, b % 2, :, :]), ALU.subtract).then_inc(s_wlo, 1)

        @block.scalar
        def _(act):
            link = Link(act, s_a)
            for name, count in VEC_ROWS:
                r = VEC_AT[name]
                src = w[name][0]
                if name == "r_k":
                    src = src.rearrange("h d -> (h d)")
                act.dma_start(vrows[r:r + count, :], src.rearrange("(r n) -> r n", n=P)).then_inc(s_vrows, 16)
            act.dma_start(trows[:, :], w["conv_w"][0].rearrange("k (r n) -> (k r) n", n=P)).then_inc(s_vrows, 16)
            act.wait_ge(s_cT, 1)
            act.activation(keep.silu_c[:, :], pg[:, 0:KD], ACT.Sigmoid).then_inc(s_sig, 1)
            act.wait_ge(s_x, 16)
            for t in range(NT):
                sq = act.activation(hT[:, 2 * t:2 * t + 2, :], x[:, t, :].rearrange("p (a b) -> p a b", b=S), ACT.Square, accum_out=sums[:, t:t + 1])
                link.sign(sq)
            link.wait()
            act.activation(mean_sq[:, :], sums[:, :], ACT.Copy, scale=1.0 / D, bias=RMS_EPS).then_inc(s_sq, 1)
            act.wait_ge(s_rstd, 1)
            for t in range(0, NT, 2):
                act.activation(x[:, t, :], x[:, t, :], ACT.Copy, scale=rstd[:, t:t + 1]).then_inc(s_xA, 1)

            def gain_copy(i):
                if has_gain(i):
                    act.wait_ge(s_gain, gains_to(i) + 1)
                    act.activation(keep.mod[:, i * N:i * N + N], pg[:, :], ACT.Copy).then_inc(s_adag, 1)

            for i in range(FIRST):
                gain_copy(i)
                for k in range(2 * i, 2 * i + 2):
                    act.wait_ge(s_ht, k + 1)
                    act.activation(hT[:, k, :], pt[k % 2][:, :], ACT.Copy).then_inc(s_hA, 1)

            def split(b):
                slot_wait(act, ("in", Z_TILES[2 * b][0]))
                if b >= 2:
                    act.wait_ge(s_z, 2 * b - 2)
                act.activation(w_hi[:, b % 2, :, :], pair(ring, b), ACT.Copy).then_inc(s_whi, 1)

            split(0)
            act.wait_ge(s_colV, 1)
            for k in range(KD):
                act.activation(h_hi[:, k, :], hT[:, k, :], ACT.Identity, scale=modcol[:, KD + k:KD + k + 1],
                               bias=modcol[:, k:k + 1]).then_inc(s_hhi, 1)
            split(1)
            act.wait_ge(s_vec, 2)
            for n, (s, t) in enumerate(Z_TILES):
                act.wait_ge(s_z, n + 1)
                z = pz[n % 3]
                if n < NZ_RWKV:
                    act.activation(mix.zr[:, n, :], z[:, :], ACT.Copy,
                                   scale=keep.one_minus_mu[:, n:n + 1]).then_inc(s_zA, 1)
                elif n < NZ_RWKV + RT_:
                    act.activation(upad[:, n - NZ_RWKV, CK - 1:], z[:, :], ACT.Copy).then_inc(s_zA, 1)
                elif n < NZ_RWKV + NZ_CONV:
                    j = n - NZ_RWKV - RT_
                    if j >= 2:
                        act.wait_ge(s_glu, j - 1)
                    act.activation(glu[:, j % 2, :], z[:, :], ACT.Sigmoid).then_inc(s_zA, 1)
                else:
                    if n == len(Z_TILES) - 2:
                        act.wait_ge(s_glu, RT_)
                    act.activation(mix.gates[:, n - NZ_RWKV - NZ_CONV, :], z[:, :], ACT.Sigmoid).then_inc(s_zA, 1)
                if n % 2 and n // 2 + 2 < len(Z_TILES) // 2:
                    split(n // 2 + 2)
                if t == 0 and s >= 2:
                    gain_copy(s + 2)

        @block.tensor
        def _(pe):
            pe.wait_ge(s_const, 5)
            pe.wait_ge(s_crow, 16)
            pe.transpose(pg[:, 0:KD], crow[:, :], keep.ident[0:KD, 0:KD]).then_inc(s_cT, 1)

            def gain_row(i):
                if has_gain(i):
                    if gains_to(i):
                        pe.wait_ge(s_adag, gains_to(i))
                    row = ADA + 2 * {1: 0, 2: 1, 4: 2, 5: 3}[i // 2] + i % 2
                    pe.matmul(pg[:, :], keep.ident[0:N_WIDE, row:row + 1].to_broadcast([N_WIDE, P]),
                              wide[:, :], start=True, stop=True).then_inc(s_gain, 1)

            def ada_direct(i):
                out = pm[i % 2]
                if i >= 2:
                    pe.wait_ge(s_mod, i - 1)
                if i < FIRST:
                    slot_wait(pe, ("ada", i))
                    slot = STREAM_AT[("ada", i)] % RING1
                    for k in range(DIRECT):
                        pe.matmul(out[:, :], keep.silu_c[:, k:k + 1].to_broadcast([P, P]), ring[:, slot, k, :],
                                  start=(k == 0), stop=False)

            def ada_sum(i):
                out = pm[i % 2]
                pe.wait_ge(s_ada, i + 1)
                pe.matmul(out[:, :], keep.ones[:, :], acc[:, i % 2, :], start=(i >= FIRST), stop=False)
                pe.matmul(out[:, :], keep.ident[0:N_WIDE, i:i + 1].to_broadcast([N_WIDE, P]), wide[:, :],
                          start=False, stop=True).then_inc(s_adam, 1)

            def mod_columns(i):
                pe.wait_ge(s_mod, i + 1)
                for j in range(i * N // P, (i + 1) * N // P):
                    last = pe.matmul(pt[1][:, j:j + 1], keep.mod[0:1, j * P:(j + 1) * P], keep.ones[0:1, 0:1],
                                     start=True, stop=True)
                last.then_inc(s_col, 1)

            pe.wait_ge(s_silu, 1)
            pe.wait_ge(s_wide, 16 * (1 + len(GAINS)))
            gain_row(2)
            ada_direct(0)
            pe.wait_ge(s_xA, NT // 2)
            pe.wait_ge(s_xV, NT // 2)
            for k in range(KD):
                if k >= 2:
                    pe.wait_ge(s_hA, k - 1)
                for t in range(NT):
                    last = pe.transpose(pt[k % 2][:, t * P:(t + 1) * P], x[:, t, k * P:(k + 1) * P], keep.ident[:, :])
                last.then_inc(s_ht, 1)
            ada_sum(0)
            gain_row(3)
            ada_direct(1)
            ada_sum(1)
            pe.wait_ge(s_hA, KD)
            mod_columns(0)
            pe.wait_ge(s_vrows, 16 * (len(VEC_ROWS) + 1))
            pe.transpose(pt[0][:, 0:N_VEC], vrows[:, :], keep.ident[0:N_VEC, 0:N_VEC])
            pe.transpose(pt[0][:, P:P + N_TAP], trows[:, :], keep.ident[0:N_TAP, 0:N_TAP]).then_inc(s_vecT, 1)
            mod_columns(1)
            for i in (2, 3):
                ada_direct(i)
                ada_sum(i)
            mod_columns(2)
            mod_columns(3)
            for n, (s, t) in enumerate(Z_TILES):
                if t == 0:
                    slot_wait(pe, ("in", s))
                if n >= 3:
                    pe.wait_ge(s_zA, n - 2)
                    if n - 3 < NZ_RWKV:
                        pe.wait_ge(s_zV, n - 2)
                pe.wait_ge(s_wlo, n // 2 + 1)
                w_lo = pair(ring_lo, n // 2)
                cs = slice(n % 2 * P, n % 2 * P + P)
                for k in range(KD):
                    if n == 0:
                        pe.wait_ge(s_hhi, k + 1)
                        pe.wait_ge(s_hlo, k + 1)
                    for i, (weights, h) in enumerate(((w_hi[:, n // 2 % 2, k, cs], h_hi), (w_hi[:, n // 2 % 2, k, cs], h_lo),
                                                      (w_lo[:, k, cs], h_hi))):
                        last = pe.matmul(pz[n % 3][:, :], weights, h[:, k, :],
                                         start=(k == 0 and i == 0), stop=(k == KD - 1 and i == 2))
                last.then_inc(s_z, 1)
                if t == 0 and s >= 2:
                    gain_row(s + 2)
                    ada_direct(s + 2)
                    ada_sum(s + 2)

        @block.vector
        def _(dve):
            link = Link(dve, s_v)
            dve.wait_ge(s_sig, 1)
            nc.vector.tensor_tensor(keep.silu_c[:, :], keep.silu_c[:, :], pg[:, 0:KD], ALU.mult).then_inc(s_silu, 1)
            dve.wait_ge(s_rstd, 1)
            for t in range(1, NT, 2):
                nc.vector.tensor_scalar(x[:, t, :], x[:, t, :], rstd[:, t:t + 1], None, ALU.mult).then_inc(s_xV, 1)
            dve.wait_ge(s_silu, 1)

            def ada_partial(i):
                slot_wait(dve, ("ada", i))
                if i >= 2:
                    dve.wait_ge(s_adam, i - 1)
                slot = STREAM_AT[("ada", i)] % RING1
                first = DIRECT if i < FIRST else 0
                for k in range(first, KD):
                    c_k = keep.silu_c[:, k:k + 1]
                    if k == first:
                        last = nc.vector.tensor_scalar(acc[:, i % 2, :], ring[:, slot, k, :], c_k, None, ALU.mult)
                    else:
                        last = nc.vector.scalar_tensor_tensor(out=acc[:, i % 2, :], in0=ring[:, slot, k, :], scalar=c_k,
                                                              in1=acc[:, i % 2, :], op0=ALU.mult, op1=ALU.add)
                    if k < KD - 1:
                        link(last)
                last.then_inc(s_ada, 1)

            def mod_row(i):
                dve.wait_ge(s_adam, i + 1)
                row = keep.mod[:, i * N:i * N + N]
                kind = (i // 2) % 3
                if kind == 0:
                    nc.vector.tensor_copy(row, pm[i % 2][:, :]).then_inc(s_mod, 1)
                    return
                dve.wait_ge(s_adag, gains_to(i) + 1)
                nc.vector.scalar_tensor_tensor(out=row, in0=pm[i % 2][:, :], scalar=1.0 if kind == 1 else 0.0, in1=row,
                                               op0=ALU.add, op1=ALU.mult).then_inc(s_mod, 1)

            for i in range(FIRST):
                ada_partial(i)
                if i:
                    mod_row(i - 1)
            dve.wait_ge(s_vecT, 1)
            nc.vector.tensor_copy(taps[:, :], pt[0][:, P:P + N_TAP])
            nc.vector.tensor_copy(vec[:, :], pt[0][:, 0:N_VEC]).then_inc(s_vec, 1)
            dve.wait_ge(s_vec, 1)
            nc.vector.tensor_scalar(keep.one_minus_mu[:, :], vec[:, 0:NZ_RWKV], -1.0, 1.0, ALU.mult,
                                    ALU.add).then_inc(s_vec, 1)
            mod_row(FIRST - 1)
            dve.wait_ge(s_col, FIRST)
            nc.vector.tensor_copy(modcol[:, :], pt[1][:, 0:2 * KD]).then_inc(s_colV, 1)
            dve.wait_ge(s_colV, 1)
            dve.wait_ge(s_hA, KD)
            for k in range(KD):
                dve.wait_ge(s_hhi, k + 1)
                nc.vector.tensor_scalar(hT[:, k, :], hT[:, k, :], modcol[:, KD + k:KD + k + 1], modcol[:, k:k + 1],
                                        ALU.mult, ALU.add).then_inc(s_mod_h, 1)
                dve.wait_ge(s_mod_h, k + 1)
                nc.vector.tensor_tensor(h_lo[:, k, :], hT[:, k, :], exact(h_hi[:, k, :]), ALU.subtract).then_inc(s_hlo, 1)

            def ada_steps(s):
                if s >= 2:
                    mod_row(s + 2)
                if 1 <= s <= ADA - 4:
                    ada_partial(s + 3)

            for n, (s, t) in enumerate(Z_TILES[:NZ_RWKV]):
                dve.wait_ge(s_zA, n + 1)
                nc.vector.scalar_tensor_tensor(out=mix.zr[:, n, 1:], in0=pz[n % 3][:, 0:S - 1], scalar=vec[:, n:n + 1],
                                               in1=mix.zr[:, n, 1:], op0=ALU.mult, op1=ALU.add).then_inc(s_zV, 1)
                if t == 1:
                    ada_steps(s)
            ada_steps(4)
            for j in range(RT_):
                dve.wait_ge(s_zA, NZ_RWKV + RT_ + j + 1)
                nc.vector.tensor_tensor(upad[:, j, CK - 1:], upad[:, j, CK - 1:], glu[:, j % 2, :],
                                        ALU.mult).then_inc(s_glu, 1)
                if j == 1:
                    ada_steps(5)
            dve.wait_ge(s_const, 5)
            dve.wait_ge(s_glu, RT_)
            done = {}
            for k in range(CK):
                if k % 8 == 0:
                    ada_steps(6 + k // 8)
                for r in range(RT_):
                    tap = taps[:, k * RT_ + r:k * RT_ + r + 1]
                    u = upad[:, r, k:k + S]
                    if k == 0:
                        done[r] = link.sign(nc.vector.tensor_scalar(mix.co[:, r, :], u, tap, vcol("conv_b", r),
                                                                    ALU.mult, ALU.add))
                    else:
                        link.wait(done[r])
                        done[r] = link.sign(nc.vector.scalar_tensor_tensor(
                            out=mix.co[:, r, :], in0=u, scalar=tap, in1=mix.co[:, r, :], op0=ALU.mult, op1=ALU.add))


def rwkv(nc, w, keep, mix):
    with ExitStack() as stack:
        m = Memory(nc, stack)
        T4 = [P, RT_, S]
        cum, sg, aB, A = m.sb("cum", T4), m.sb("sg", T4), m.sb("aB", T4), m.sb("A_T", T4)
        reset = m.sb("reset", [P, S])
        loras = m.sb("loras", [P, RW])
        g2 = m.sb("g2", [P, RW])
        headones = m.sb("headones", [P, P])
        ka1 = m.sb("one_minus_ka", [P, RT_])
        mid = m.sb("mid", [P, RT_, NT])
        last = m.sb("last", [P, RT_, NT])
        mid_e = m.sb("mid_e", [P, RT_, NT])
        hop = m.sb("hop", [P, RT_, NT])
        LV = 7
        masks = m.sb("level_masks", [P, LV, P])
        low1 = m.sb("low1", [P, P])
        tri = m.sb("tri", [P, 2, P])
        col_i, row_i = m.sb("col_i", [P, P], I32), m.sb("row_i", [P, P], I32)
        colf, rowf, xorf, ge = m.sb("colf", [P, P]), m.sb("rowf", [P, P]), m.sb("xorf", [P, 2, P]), m.sb("ge", [P, 2, P])
        tok = m.sb("tok", [P, 2, 3, RW])
        AB = m.sb("AB", [P, HEADS, 2 * P])
        AK = m.sb("AK", [P, HEADS, 2 * P])
        factor, ep = (ap[:, :, :].rearrange("p (r h) t -> p r (h t)", r=RT_) for ap in (AB, AK))
        X, XT = m.sb("X", [P, HEADS, P]), m.sb("XT", [P, HEADS, P])
        Z = sg[:, :, :].rearrange("p (b a) (h t) -> p b (a h) t", b=2, t=P)
        TM = cum[:, :, :].rearrange("p (b a) (h t) -> p b (a h) t", b=2, t=P)
        G, U = m.sb("G", [P, 2, RT_, HD]), m.sb("U", [P, RT_, 2, HD])
        M = m.sb("M", [P, RT_, HD])
        bank = [m.bank(f"b{i}") for i in range(8)]
        zr, vec, gate_r, bonus = mix.zr, keep.vec, mix.gate_r, mix.bonus
        r_, k_, v_ = zr[:, 0:4, :], zr[:, 4:8, :], zr[:, 8:12, :]

        s_w = m.sem("p2_weights_in")
        s_io = m.sem("p2_iotas")
        s_mask = m.sem("p2_masks")
        s_act = m.sem("p2_lora_activated")
        s_lora = m.sem("p2_lora_products")
        s_loraA = m.sem("p2_lora_taken")
        s_kk = m.sem("p2_kk")
        s_kksq = m.sem("p2_kk_squared")
        s_kksum = m.sem("p2_kk_sums")
        s_kkmax, s_kkroot = m.sem("p2_kk_max"), m.sem("p2_kk_inverse_norm")
        s_rk = m.sem("p2_rk")
        s_rksum = m.sem("p2_rk_sums")
        s_bonus = m.sem("p2_bonus")
        s_cc = m.sem("p2_centred")
        s_e1, s_e2, s_e3 = m.sem("p2_exp_plus"), m.sem("p2_exp_minus"), m.sem("p2_exp_before")
        s_epfree = m.sem("p2_exp_plus_used")
        s_oper = m.sem("p2_operands")
        s_mid = m.sem("p2_mid_exp")
        s_v, s_a, s_g = m.sem("p2_vector_chain"), m.sem("p2_scalar_chain"), m.sem("p2_pool_chain")
        s_tokp, s_tok = m.sem("p2_tok_turned"), m.sem("p2_tok_ready")
        s_pair, s_pairV = m.sem("p2_pair_products"), m.sem("p2_pair_masked")
        s_x2, s_x2p = m.sem("p2_x_start"), m.sem("p2_xt_start")
        s_tm = m.sem("p2_level_T")
        s_z, s_zA = m.sem("p2_Z"), m.sem("p2_Z_taken")
        s_xz, s_xV, s_xzV = m.sem("p2_XZ"), m.sem("p2_X_added"), m.sem("p2_XT_added")
        s_G, s_GA = m.sem("p2_G"), m.sem("p2_G_taken")
        s_U, s_UV = m.sem("p2_U"), m.sem("p2_U_taken")
        s_M, s_MV = m.sem("p2_M"), m.sem("p2_M_taken")
        s_Y, s_YA = m.sem("p2_Y"), m.sem("p2_Y_taken")
        block = stack.enter_context(nc.Block())
        STEPS = LV - 1
        LAST_C = NT - 1

        def vcol(name, i=0):
            return vec[:, VEC_AT[name] + i:VEC_AT[name] + i + 1]

        def wide(ap, shape):
            return ap.to_broadcast(shape)

        def unit(u):
            g, q = u // 2, u % 2
            return slice(4 * g + q, 4 * g + q + 3, 2), q

        TM_COUNT = 4 + STEPS - 1

        def at(h):
            return h // 2, slice(HD * (h % 2), HD * (h % 2) + HD)

        @block.sync
        def _(sp):
            sp.dma_start(loras[0:LORA_W, :], w["w2"][0]).then_inc(s_w, 16)
            sp.dma_start(loras[LORA_W:P, :], w["a2"][0]).then_inc(s_w, 16)
            sp.dma_start(g2[:, :], w["g2"][0]).then_inc(s_w, 16)

        @block.gpsimd
        def _(pool):
            link = Link(pool, s_g)
            link.sign(pool.memset(headones[:, :], 0.0))
            link.sign(pool.memset(reset[:, :], 1.0))
            pool.iota(col_i[:, :], [[1, P]], base=0, channel_multiplier=0).then_inc(s_io, 1)
            pool.iota(row_i[:, :], [[0, P]], base=0, channel_multiplier=1).then_inc(s_io, 1)
            link.wait()
            for q in range(2):
                pool.wait_ge(s_io, 2 + q)
                pool.memset(headones[HD * q:HD * q + HD, HD * q:HD * q + HD], 1.0).then_inc(s_io, 1)
            pool.wait_ge(s_io, 4)
            pool.memset(reset[:, :].rearrange("p (c t) -> p c t", c=NT)[:, :, 0:1], 0.0).then_inc(s_io, 1)
            pool.wait_ge(s_mask, 1)
            for c in range(NT):
                for u in range(4):
                    heads, _ = unit(u)
                    if c:
                        pool.wait_ge(s_z, 2 * (c * STEPS - 1))
                    pool.wait_ge(s_pairV, 4 * c + u + 1)
                    pool.tensor_tensor(TM[:, (c * STEPS) % 2, heads, :], AB[:, heads, 0:P], wide(masks[:, 1:2, :], [P, 2, P]),
                                       ALU.mult).then_inc(s_tm, 1)
                for lv in range(1, STEPS):
                    n = c * STEPS + lv
                    if n >= 2:
                        pool.wait_ge(s_z, 2 * (n - 1))
                    pool.tensor_tensor(TM[:, n % 2, :, :], AB[:, :, 0:P], wide(masks[:, lv + 1:lv + 2, :], [P, HEADS, P]),
                                       ALU.mult).then_inc(s_tm, 1)

        @block.scalar
        def _(act):
            link = Link(act, s_a)
            act.activation(zr[0:LORA_W, 12, :], zr[0:LORA_W, 12, :], ACT.Tanh).then_inc(s_act, 1)
            act.activation(zr[:, 13, :], zr[:, 13, :], ACT.Sigmoid).then_inc(s_act, 1)
            for r in range(RT_):
                for j, (dst, bias) in enumerate(((sg, "w0"), (aB, "a0"), (gate_r, None))):
                    n = 3 * r + j
                    act.wait_ge(s_lora, n + 1)
                    if bias:
                        act.activation(dst[:, r, :], bank[n % 4][:, :], ACT.Sigmoid, bias=vcol(bias, r)).then_inc(s_loraA, 1)
                    else:
                        act.activation(dst[:, r, :], bank[n % 4][:, :], ACT.Copy).then_inc(s_loraA, 1)
            for r in range(RT_):
                act.wait_ge(s_kk, r + 1)
                act.activation(bonus[:, r, :], A[:, r, :], ACT.Square).then_inc(s_kksq, 1)
            for r in range(RT_):
                act.wait_ge(s_kkmax, r + 1)
                link.sign(act.activation(bonus[:, r, :], bonus[:, r, :], ACT.Ln))
            for r in range(RT_):
                link.wait(r + 1)
                act.activation(bonus[:, r, :], bonus[:, r, :], ACT.Exp, scale=-0.5).then_inc(s_kkroot, 1)
            for r in range(RT_):
                act.wait_ge(s_cc, r + 1)
                if r == 0:
                    act.activation(mid_e[:, :, :], mid[:, :, :], ACT.Exp, scale=-DECAY).then_inc(s_mid, 1)
                act.activation(ep[:, r, :], cum[:, r, :], ACT.Exp, scale=-DECAY).then_inc(s_e1, 1)
                act.activation(sg[:, r, :], sg[:, r, :], ACT.Exp, scale=-DECAY).then_inc(s_e3, 1)
                act.wait_ge(s_e1, r + 1)
                act.activation(cum[:, r, :], cum[:, r, :], ACT.Exp, scale=DECAY).then_inc(s_e2, 1)

            def tokens(c, i):
                act.wait_ge(s_tokp, 3 * c + i + 1)
                if c >= 2:
                    act.wait_ge(s_Y, c - 1)
                act.activation(tok[:, c % 2, i, :], bank[(6, 7, 6)[i]][:, :], ACT.Copy).then_inc(s_tok, 1)

            for i in range(3):
                tokens(0, i)
            for c in range(NT):
                for lv in range(STEPS):
                    for g in range(2):
                        n = (c * STEPS + lv) * 2 + g
                        act.wait_ge(s_z, n + 1)
                        if n >= 2:
                            act.wait_ge(s_xz, n - 1)
                        act.activation(Z[:, lv % 2, 4 * g:4 * g + 4, :], bank[g][:, :].rearrange("p (h t) -> p h t", h=4),
                                       ACT.Copy).then_inc(s_zA, 1)
                        if lv == 0 and g == 0:
                            act.wait_ge(s_G, c + 1)
                            if c:
                                act.wait_ge(s_U, c)
                            for q in range(2):
                                act.activation(G[:, q, :, :], bank[6 + q][:, 0:RT_ * HD].rearrange("p (r v) -> p r v", r=RT_),
                                               ACT.Copy).then_inc(s_GA, 1)
                if c < LAST_C:
                    for i in range(2):
                        tokens(c + 1, i)
                act.wait_ge(s_Y, c + 1)
                for q in range(2):
                    act.activation(zr[HD * q:HD * q + HD, 0:4, c * P:(c + 1) * P],
                                   bank[2 + q][HD * q:HD * q + HD, :].rearrange("p (r t) -> p r t", r=RT_),
                                   ACT.Copy).then_inc(s_YA, 1)
                if c < LAST_C:
                    tokens(c + 1, 2)

        @block.tensor
        def _(pe):
            pe.wait_ge(s_w, 48)
            pe.wait_ge(s_act, 2)
            for r in range(RT_):
                for j in range(3):
                    n = 3 * r + j
                    if n >= 4:
                        pe.wait_ge(s_loraA, n - 3)
                    cols = slice(r * P, (r + 1) * P)
                    if j == 0:
                        mm = pe.matmul(bank[n % 4][:, :], loras[0:LORA_W, cols], zr[0:LORA_W, 12, :], start=True, stop=True)
                    elif j == 1:
                        mm = pe.matmul(bank[n % 4][:, :], loras[LORA_W:P, cols], zr[LORA_W:P, 12, :], start=True, stop=True)
                    else:
                        mm = pe.matmul(bank[n % 4][:, :], g2[:, cols], zr[:, 13, :], start=True, stop=True)
                    mm.then_inc(s_lora, 1)
            pe.wait_ge(s_io, 5)
            for r in range(RT_):
                pe.wait_ge(s_kksq, r + 1)
                pe.matmul(bank[4 + r][:, :], headones[:, :], bonus[:, r, :], start=True, stop=True).then_inc(s_kksum, 1)
            pe.wait_ge(s_kkmax, RT_)
            for r in range(RT_):
                pe.wait_ge(s_rk, r + 1)
                pe.matmul(bank[4 + r][:, :], headones[:, :], bonus[:, r, :], start=True, stop=True).then_inc(s_rksum, 1)
            pe.wait_ge(s_bonus, RT_)
            pe.wait_ge(s_oper, RT_)

            def turn(c, i):
                if c and i == 0:
                    pe.wait_ge(s_GA, 2 * c)
                if i == 2:
                    pe.wait_ge(s_tok, 3 * c + 1)
                for r in range(RT_):
                    mm = pe.transpose(bank[(6, 7, 6)[i]][:, r * P:(r + 1) * P], (aB, k_, v_)[i][:, r, c * P:(c + 1) * P],
                                      keep.ident[:, :])
                mm.then_inc(s_tokp, 1)

            def start_values(c):
                pe.wait_ge(s_tok, 3 * c + 3)
                pe.wait_ge(s_pairV, 4 * c + 4)
                if c:
                    pe.wait_ge(s_MV, c)
                for h in range(HEADS):
                    r, ps = at(h)
                    dst = bank[6 + h % 2][:, r * HD:(r + 1) * HD]
                    if c:
                        pe.matmul(dst, A[ps, r, c * P:(c + 1) * P], M[ps, r, :], start=True, stop=False)
                    mm = pe.matmul(dst, AK[:, h, 0:P], tok[:, c % 2, 2, h * HD:(h + 1) * HD], start=(c == 0), stop=True)
                mm.then_inc(s_G, 1)

            for i in range(3):
                turn(0, i)
            for c in range(NT):
                ts = slice(c * P, (c + 1) * P)
                B_tok, K_tok, V_tok = (tok[:, c % 2, i, :] for i in range(3))
                for u in range(4):
                    _, q = unit(u)
                    if u >= 2:
                        pe.wait_ge(s_pairV, 4 * c + u - 1)
                        pe.wait_ge(s_x2, 4 * c + u - 1)
                    elif c:
                        pe.wait_ge(s_YA, 2 * c - 1 + q)
                        if q == 0:
                            pe.wait_ge(s_UV, c)
                        else:
                            pe.wait_ge(s_MV, c)
                    for j in range(2):
                        r, ps = at(4 * (u // 2) + 2 * j + q)
                        for dst, lhs in ((bank[q], aB), (bank[2 + q], k_)):
                            pe.matmul(dst[:, j * 2 * P:j * 2 * P + P], lhs[ps, r, ts], A[ps, r, ts], start=True, stop=True)
                            pe.matmul(dst[:, j * 2 * P + P:(j + 1) * 2 * P], lhs[ps, r, ts], r_[ps, r, ts],
                                      start=True, stop=True)
                        mm = pe.matmul(bank[4 + q][:, j * P:(j + 1) * P], A[ps, r, ts], aB[ps, r, ts], start=True, stop=True)
                    mm.then_inc(s_pair, 1)
                for lv in range(STEPS):
                    n = c * STEPS + lv
                    for g in range(2):
                        if lv:
                            pe.wait_ge(s_tm, TM_COUNT * c + 4 + lv)
                            pe.wait_ge(s_xV, 2 * (c * (STEPS - 1) + lv - 1) + g + 1)
                        else:
                            pe.wait_ge(s_tm, TM_COUNT * c + 2 * g + 2)
                            pe.wait_ge(s_x2, 4 * c + 2 * g + 2)
                            pe.wait_ge(s_pairV, 4 * c + 3 + g)
                        for h in range(4 * g, 4 * g + 4):
                            cs = slice((h % 4) * P, (h % 4 + 1) * P)
                            mm = pe.matmul(bank[g][:, cs], TM[:, n % 2, h, :], X[:, h, :], start=True, stop=True)
                        mm.then_inc(s_z, 1)
                        if lv == 0 and g == 0:
                            start_values(c)
                    for g in range(2):
                        pe.wait_ge(s_zA, 2 * n + g + 1)
                        if lv:
                            pe.wait_ge(s_xzV, 2 * (n - 1) + g + 1)
                        if lv == 0:
                            pe.wait_ge(s_x2, 4 * c + 3 + g)
                            pe.wait_ge(s_x2p, 4 * c + 2 * g + 2)
                        for h in range(4 * g, 4 * g + 4):
                            cs = slice((h % 4) * P, (h % 4 + 1) * P)
                            if lv < STEPS - 1:
                                pe.matmul(bank[2 + g][:, cs], XT[:, h, :], Z[:, lv % 2, h, :], start=True, stop=True)
                            mm = pe.matmul(bank[4 + g][:, cs], Z[:, lv % 2, h, :], XT[:, h, :], start=True, stop=True)
                        mm.then_inc(s_xz, 1)
                pe.wait_ge(s_xzV, 2 * STEPS * (c + 1))
                pe.wait_ge(s_GA, 2 * c + 2)
                for h in range(HEADS):
                    mm = pe.matmul(bank[4][:, h * HD:(h + 1) * HD], XT[:, h, :], G[:, h % 2, h // 2, :], start=True, stop=True)
                mm.then_inc(s_U, 1)
                if c < LAST_C:
                    turn(c + 1, 0)
                    turn(c + 1, 1)
                pe.wait_ge(s_UV, c + 1)
                if c < LAST_C:
                    for r in range(RT_):
                        cs = slice(r * P, (r + 1) * P)
                        pe.matmul(bank[5][:, cs], B_tok[:, cs], U[:, r, :, :].rearrange("p q v -> p (q v)"), start=True, stop=False)
                        mm = pe.matmul(bank[5][:, cs], K_tok[:, cs], V_tok[:, cs], start=False, stop=True)
                    mm.then_inc(s_M, 1)
                for h in range(HEADS):
                    r, ps = at(h)
                    dst = bank[2 + h % 2][ps, r * P:(r + 1) * P]
                    if c:
                        pe.matmul(dst, M[ps, r, :], r_[ps, r, ts], start=True, stop=False)
                    pe.matmul(dst, U[:, r, h % 2, :], AB[:, h, P:2 * P], start=(c == 0), stop=False)
                    mm = pe.matmul(dst, V_tok[:, h * HD:(h + 1) * HD], AK[:, h, P:2 * P], start=False, stop=True)
                mm.then_inc(s_Y, 1)
                if c < LAST_C:
                    turn(c + 1, 2)

        @block.vector
        def _(dve):
            link = Link(dve, s_v)
            V = nc.vector
            dve.wait_ge(s_io, 2)
            a = link.sign(V.tensor_copy(colf[:, :], col_i[:, :]))
            b = link.sign(V.tensor_copy(rowf[:, :], row_i[:, :]))
            link(V.tensor_tensor(col_i[:, :], col_i[:, :], row_i[:, :], ALU.bitwise_xor))
            link(V.tensor_copy(xorf[:, 0, :], col_i[:, :]))
            link.sign(V.tensor_tensor(tri[:, 1, :], colf[:, :], rowf[:, :], ALU.is_ge))
            link.sign(V.tensor_tensor(ge[:, 0, :], colf[:, :], rowf[:, :], ALU.is_lt))
            link(V.tensor_tensor(tri[:, 0, :], colf[:, :], rowf[:, :], ALU.is_gt))
            link.sign(V.tensor_tensor(xorf[:, 1, :], xorf[:, 0, :], ge[:, 0, :], ALU.mult))
            link(V.tensor_tensor(xorf[:, 0, :], xorf[:, 0, :], tri[:, 0, :], ALU.mult))
            link.sign(V.tensor_scalar(low1[:, :], xorf[:, 1, :], 1.0, None, ALU.is_equal))
            for lv in range(LV):
                link(V.tensor_scalar(ge[:, 0, :], xorf[:, 0, :], float(2 ** lv), None, ALU.is_ge))
                link(V.tensor_scalar(ge[:, 1, :], xorf[:, 0, :], float(2 ** (lv + 1)), None, ALU.is_lt))
                link(V.tensor_tensor(masks[:, lv, :], ge[:, 0, :], ge[:, 1, :], ALU.mult))
            V.tensor_scalar(ka1[:, :], vec[:, VEC_AT["k_a"]:VEC_AT["k_a"] + RT_], -1.0, 1.0, ALU.mult,
                            ALU.add).then_inc(s_mask, 1)
            for r in range(RT_):
                V.tensor_scalar(A[:, r, :], k_[:, r, :], vcol("k_k", r), None, ALU.mult).then_inc(s_kk, 1)
            dve.wait_ge(s_io, 5)
            done = []
            for r in range(RT_):
                dve.wait_ge(s_loraA, 3 * r + 1)
                done.append(link.sign(V.tensor_tensor_scan(cum[:, r, :], reset[:, :], sg[:, r, :], 0.0, ALU.mult, ALU.add)))
            for r in range(RT_):
                link.wait(done[r])
                done[r] = link.sign(V.tensor_copy(mid[:, r, :], cum[:, r, P // 2 - 1::P]))
            for r in range(RT_):
                link.wait(done[r])
                chunks = cum[:, r, :].rearrange("p (c t) -> p c t", c=NT)
                done[r] = link.sign(V.tensor_tensor(chunks, chunks, wide(mid[:, r, :].unsqueeze(2), [P, NT, P]), ALU.subtract))
            for r in range(RT_):
                link.wait(done[r])
                V.tensor_tensor(sg[:, r, :], cum[:, r, :], sg[:, r, :], ALU.subtract).then_inc(s_cc, 1)
            for r in range(RT_):
                dve.wait_ge(s_kksum, r + 1)
                V.tensor_scalar(bonus[:, r, :], bank[4 + r][:, :], 1e-24, None, ALU.max).then_inc(s_kkmax, 1)
            dve.wait_ge(s_mask, 1)
            for r in range(RT_):
                dve.wait_ge(s_loraA, 3 * r + 2)
                done[r] = link.sign(V.tensor_scalar(factor[:, r, :], aB[:, r, :], vcol("k_a", r), ka1[:, r:r + 1], ALU.mult, ALU.add))
            for r in range(RT_):
                link.wait(done[r])
                dve.wait_ge(s_kk, r + 1)
                done[r] = link.sign(V.tensor_tensor(k_[:, r, :], k_[:, r, :], factor[:, r, :], ALU.mult))
            for r in range(RT_):
                dve.wait_ge(s_kkroot, r + 1)
                done[r] = link.sign(V.tensor_tensor(A[:, r, :], A[:, r, :], bonus[:, r, :], ALU.mult))
            for r in range(RT_):
                link.wait(done[r])
                done[r] = link.sign(V.tensor_tensor(aB[:, r, :], aB[:, r, :], A[:, r, :], ALU.mult))
            for r in range(RT_):
                link.wait(done[r])
                V.scalar_tensor_tensor(out=bonus[:, r, :], in0=k_[:, r, :], scalar=vcol("r_k", r), in1=r_[:, r, :],
                                       op0=ALU.mult, op1=ALU.mult).then_inc(s_rk, 1)
            link.wait()
            dve.wait_ge(s_rk, RT_)
            for r in range(RT_):
                dve.wait_ge(s_e1, r + 1)
                n = link.sign(V.tensor_tensor(r_[:, r, :], r_[:, r, :], ep[:, r, :], ALU.mult))
                link.sign(V.tensor_copy(last[:, r, :], ep[:, r, P - 1::P]))
                link.wait()
                dve.wait_ge(s_e2, r + 1)
                link.sign(V.tensor_tensor(aB[:, r, :], aB[:, r, :], cum[:, r, :], ALU.mult))
                V.tensor_tensor(k_[:, r, :], k_[:, r, :], cum[:, r, :], ALU.mult).then_inc(s_epfree, 1)
                dve.wait_ge(s_e3, r + 1)
                link(V.scalar_tensor_tensor(out=A[:, r, :], in0=A[:, r, :], scalar=-1.0, in1=sg[:, r, :], op0=ALU.mult, op1=ALU.mult))
                dve.wait_ge(s_epfree, r + 1)
                dve.wait_ge(s_rksum, r + 1)
                V.tensor_tensor(bonus[:, r, :], bank[4 + r][:, :], v_[:, r, :], ALU.mult).then_inc(s_bonus, 1)
                dve.wait_ge(s_bonus, r + 1)
                dve.sem_inc(s_oper, 1)
            dve.wait_ge(s_mid, 1)
            link(V.tensor_tensor(hop[:, :, 0:NT - 1], last[:, :, 0:NT - 1], mid_e[:, :, 1:NT], ALU.mult))
            for c in range(NT):
                for u in range(4):
                    heads, q = unit(u)
                    dve.wait_ge(s_pair, 4 * c + u + 1)
                    if c and u == 0:
                        dve.wait_ge(s_Y, c)
                    m2 = wide(tri[:, :, :].rearrange("p a t -> p (a t)").unsqueeze(1), [P, 2, 2 * P])
                    products = bank[q][:, :].rearrange("p (h t) -> p h t", h=2)
                    V.tensor_tensor(AB[:, heads, :], products, m2, ALU.mult)
                    first = link.sign(V.tensor_tensor(X[:, heads, :], bank[4 + q][:, 0:2 * P].rearrange("p (h t) -> p h t", h=2),
                                                      wide(low1[:, :].unsqueeze(1), [P, 2, P]), ALU.mult))
                    second = link.sign(V.tensor_tensor(XT[:, heads, :], products[:, :, 0:P], wide(masks[:, 0:1, :], [P, 2, P]),
                                                       ALU.mult))
                    V.tensor_tensor(AK[:, heads, :], bank[2 + q][:, :].rearrange("p (h t) -> p h t", h=2),
                                    m2, ALU.mult).then_inc(s_pairV, 1)
                    one = wide(keep.ident[:, :].unsqueeze(1), [P, 2, P])
                    link.wait(first)
                    V.tensor_tensor(X[:, heads, :], X[:, heads, :], one, ALU.add).then_inc(s_x2, 1)
                    link.wait(second)
                    V.tensor_tensor(XT[:, heads, :], XT[:, heads, :], one, ALU.add).then_inc(s_x2p, 1)
                for lv in range(STEPS):
                    for g in range(2):
                        n = (c * STEPS + lv) * 2 + g
                        dve.wait_ge(s_xz, n + 1)
                        if lv == 0:
                            dve.wait_ge(s_x2p, 4 * c + 4)
                            dve.wait_ge(s_x2, 4 * c + 4)
                        if n >= 2:
                            dve.wait_ge(s_xzV, n - 1)
                        hs = slice(4 * g, 4 * g + 4)
                        if lv < STEPS - 1:
                            V.tensor_tensor(X[:, hs, :], X[:, hs, :], bank[2 + g][:, :].rearrange("p (h t) -> p h t", h=4),
                                            ALU.add).then_inc(s_xV, 1)
                        V.tensor_tensor(XT[:, hs, :], XT[:, hs, :], bank[4 + g][:, :].rearrange("p (h t) -> p h t", h=4),
                                        ALU.add).then_inc(s_xzV, 1)
                dve.wait_ge(s_U, c + 1)
                V.tensor_copy(U[:, :, :, :].rearrange("p r q v -> p (r q v)"), bank[4][:, :]).then_inc(s_UV, 1)
                if c == LAST_C:
                    continue
                dve.wait_ge(s_M, c + 1)
                if c:
                    dve.wait_ge(s_Y, c + 1)
                for q in range(2):
                    ps = slice(HD * q, HD * q + HD)
                    new = bank[5][ps, :].rearrange("p (r v) -> p r v", r=RT_)[:, :, HD * q:HD * q + HD]
                    if c:
                        link.sign(V.tensor_tensor(M[ps, :, :], M[ps, :, :], new, ALU.add))
                    else:
                        link.sign(V.tensor_copy(M[ps, :, :], new))
                link.wait()
                V.tensor_tensor(M[:, :, :], M[:, :, :], wide(hop[:, :, c:c + 1], [P, RT_, HD]), ALU.mult).then_inc(s_MV, 1)

    m.reset_semaphores()


def merge(nc, w, keep, mix):
    with ExitStack() as stack:
        m = Memory(nc, stack)
        p_conv, p_rwkv = m.sb("p_conv", [P, RT_, D]), m.sb("p_rwkv", [P, RT_, D])
        w_o = m.sb("w_o", [P, KD, D])
        x = m.sb("x3", [P, NT, D])
        sq = m.sb("sq3", [P, RT_, S])
        stat = m.sb("stat3", [P, S])
        sig = m.sb("sig3", [P, 3, S])
        headones = m.sb("headones3", [P, P])
        sums = m.sb("sums3", [P, 2, NT, 2])
        mean_sq, rstd = m.sb("mean_sq3", [P, 2, NT]), m.sb("rstd3", [P, 2, NT])
        bank = [m.bank(f"c{i}") for i in range(8)]
        co, y, gates, vec = mix.co, mix.zr[:, 0:4, :], mix.gates, keep.vec

        s_pc, s_pr, s_wo, s_x = (m.sem(f"p3_{n}_in") for n in ("p_conv", "p_rwkv", "w_o", "x"))
        s_g = m.sem("p3_head_ones")
        s_mu = m.sem("p3_sums")
        s_d = m.sem("p3_centred")
        s_sq = m.sem("p3_squared")
        s_var = m.sem("p3_square_sums")
        s_varV = m.sem("p3_variance")
        s_root = m.sem("p3_inverse_root")
        s_n = m.sem("p3_conv_normed")
        s_sig = m.sem("p3_conv_sigmoid")
        s_u = m.sem("p3_conv_out")
        s_y = m.sem("p3_rwkv_out")
        s_p = m.sem("p3_projected")
        s_pV = m.sem("p3_projected_taken")
        s_o = m.sem("p3_out_projected")
        s_oA = m.sem("p3_out_squares")
        s_r = m.sem("p3_rstd")
        s_x1 = m.sem("p3_x1")
        s_x1A = m.sem("p3_x1_squares")
        s_h2 = m.sem("p3_h2")
        s_st = m.sem("p3_stored")
        s_v, s_a = m.sem("p3_vector_chain"), m.sem("p3_scalar_chain")
        block = stack.enter_context(nc.Block())

        def h2(t):
            return p_conv[:, t, :]

        def vcol(name, i=0):
            return vec[:, VEC_AT[name] + i:VEC_AT[name] + i + 1]

        @block.sync
        def _(sp):
            sp.dma_start(p_conv[:, :, :], w["p_conv"][0].rearrange("(k p) n -> p k n", p=P)).then_inc(s_pc, 16)
            sp.dma_start(p_rwkv[:, :, :], w["p_rwkv"][0].rearrange("(k p) n -> p k n", p=P)).then_inc(s_pr, 16)
            sp.dma_start(w_o[:, :, :], w["w_o"][0].rearrange("(k p) n -> p k n", p=P)).then_inc(s_wo, 16)
            sp.dma_start(x[:, :, :], w["x"][0].rearrange("(t p) d -> p t d", p=P)).then_inc(s_x, 16)
            for t in range(NT):
                sp.wait_ge(s_x1, t + 1)
                sp.dma_start(keep.x1_dram[t * P:(t + 1) * P, :], x[:, t, :]).then_inc(s_st, 16)
            for t in range(NT):
                sp.wait_ge(s_h2, t + 1)
                sp.dma_start(keep.h2_dram[t * P:(t + 1) * P, :], h2(t)).then_inc(s_st, 16)
            sp.wait_ge(s_st, 16 * 2 * NT)

        @block.gpsimd
        def _(pool):
            pool.memset(headones[:, :], 0.0).then_inc(s_g, 1)
            for q in range(2):
                pool.wait_ge(s_g, 1 + q)
                pool.memset(headones[HD * q:HD * q + HD, HD * q:HD * q + HD], 1.0).then_inc(s_g, 1)
            pool.wait_ge(s_g, 3)
            for j in range(2 * NT):
                kind, t = j % 2, j // 2
                pool.wait_ge(s_oA, j + 1)
                pool.tensor_tensor(rstd[:, kind, t:t + 1], mean_sq[:, kind, t:t + 1], keep.power[:, 0:1],
                                   ALU.pow).then_inc(s_r, 1)

        @block.scalar
        def _(act):
            link = Link(act, s_a)
            for r in range(RT_):
                act.wait_ge(s_d, r + 1)
                act.activation(sq[:, r, :], co[:, r, :], ACT.Square).then_inc(s_sq, 1)
            act.wait_ge(s_var, 1)
            for r in range(RT_):
                act.wait_ge(s_d, RT_ + r + 1)
                act.activation(sq[:, r, :], y[:, r, :], ACT.Square).then_inc(s_sq, 1)
            act.wait_ge(s_varV, 1)
            logs = [link.sign(act.activation(stat[:, :], stat[:, :], ACT.Ln))]
            for r in range(RT_):
                act.wait_ge(s_varV, 2 + r)
                logs.append(link.sign(act.activation(sq[:, r, :], sq[:, r, :], ACT.Ln)))
            link.wait(logs[0])
            act.activation(stat[:, :], stat[:, :], ACT.Exp, scale=-0.5).then_inc(s_root, 1)
            for r in range(RT_):
                link.wait(logs[1 + r])
                act.activation(sq[:, r, :], sq[:, r, :], ACT.Exp, scale=-0.5).then_inc(s_root, 1)
            for r in range(RT_):
                act.wait_ge(s_n, r + 1)
                if r >= 3:
                    act.wait_ge(s_u, r - 2)
                act.activation(sig[:, r % 3, :], co[:, r, :], ACT.Sigmoid, bias=vcol("conv_ln_b", r),
                               scale=vcol("conv_ln_g", r)).then_inc(s_sig, 1)
            for t in range(NT):
                act.wait_ge(s_o, 2 * t + 2)
                for half in range(2):
                    act.wait_ge(s_y, RT_)
                    if t or half:
                        link.wait()
                    link.sign(act.activation(stat[:, :], bank[(2 * t + half) % 4][:, :], ACT.Square,
                                             accum_out=sums[:, 0, t, half:half + 1]))
                link.wait()
                link(act.activation(mean_sq[:, 0, t:t + 1], sums[:, 0, t, 0:1], ACT.Identity, bias=sums[:, 0, t, 1:2]))
                act.activation(mean_sq[:, 0, t:t + 1], mean_sq[:, 0, t:t + 1], ACT.Copy, scale=1.0 / D,
                               bias=RMS_EPS).then_inc(s_oA, 1)
                act.wait_ge(s_x1, t + 1)
                for half in range(2):
                    link.sign(act.activation(stat[:, :], x[:, t, half * N:half * N + N], ACT.Square,
                                             accum_out=sums[:, 1, t, half:half + 1]))
                    link.wait()
                link(act.activation(mean_sq[:, 1, t:t + 1], sums[:, 1, t, 0:1], ACT.Identity, bias=sums[:, 1, t, 1:2]))
                act.activation(mean_sq[:, 1, t:t + 1], mean_sq[:, 1, t:t + 1], ACT.Copy, scale=1.0 / D,
                               bias=RMS_EPS).then_inc(s_oA, 1)

        @block.tensor
        def _(pe):
            for r in range(RT_):
                mm = pe.matmul(bank[0][:, :], keep.ones[:, :], co[:, r, :], start=(r == 0), stop=(r == RT_ - 1))
            mm.then_inc(s_mu, 1)
            pe.wait_ge(s_g, 3)
            for r in range(RT_):
                pe.matmul(bank[1 + r][:, :], headones[:, :], y[:, r, :], start=True, stop=True).then_inc(s_mu, 1)
            pe.wait_ge(s_sq, RT_)
            for r in range(RT_):
                mm = pe.matmul(bank[5][:, :], keep.ones[:, :], sq[:, r, :], start=(r == 0), stop=(r == RT_ - 1))
            mm.then_inc(s_var, 1)
            for r in range(RT_):
                pe.wait_ge(s_sq, RT_ + r + 1)
                pe.matmul(bank[1 + r][:, :], headones[:, :], sq[:, r, :], start=True, stop=True).then_inc(s_var, 1)
            for j, (p_w, src, s_in, s_ready) in enumerate(((p_conv, co, s_pc, s_u), (p_rwkv, y, s_pr, s_y))):
                pe.wait_ge(s_in, 16)
                pe.wait_ge(s_ready, RT_)
                for dt in range(KD):
                    n = j * KD + dt
                    if n < 3:
                        pe.wait_ge(s_varV, 1 + RT_)
                    else:
                        pe.wait_ge(s_pV, n - 2)
                    for r in range(RT_):
                        mm = pe.matmul(bank[5 + n % 3][:, :], p_w[:, r, dt * P:(dt + 1) * P], src[:, r, :],
                                       start=(r == 0), stop=(r == RT_ - 1))
                    mm.then_inc(s_p, 1)
            pe.wait_ge(s_wo, 16)
            pe.wait_ge(s_pV, 2 * KD)
            for t in range(NT):
                for half in range(2):
                    if t >= 2:
                        pe.wait_ge(s_x1, t - 1)
                    for k in range(KD):
                        mm = pe.matmul(bank[(2 * t + half) % 4][:, :], gates[:, k, t * P:(t + 1) * P],
                                       w_o[:, k, half * N:half * N + N], start=(k == 0), stop=(k == KD - 1))
                    mm.then_inc(s_o, 1)

        @block.vector
        def _(dve):
            link = Link(dve, s_v)
            V = nc.vector
            dve.wait_ge(s_mu, 1)
            link(V.tensor_scalar(stat[:, :], bank[0][:, :], 1.0 / CW, None, ALU.mult))
            for r in range(RT_):
                V.tensor_tensor(co[:, r, :], co[:, r, :], stat[:, :], ALU.subtract).then_inc(s_d, 1)
            for r in range(RT_):
                dve.wait_ge(s_mu, 2 + r)
                V.scalar_tensor_tensor(out=y[:, r, :], in0=bank[1 + r][:, :], scalar=-1.0 / HD, in1=y[:, r, :],
                                       op0=ALU.mult, op1=ALU.add).then_inc(s_d, 1)
            dve.wait_ge(s_var, 1)
            dve.wait_ge(s_d, RT_)
            V.tensor_scalar(stat[:, :], bank[5][:, :], CW * LN_EPS, None, ALU.add).then_inc(s_varV, 1)
            for r in range(RT_):
                dve.wait_ge(s_var, 2 + r)
                V.tensor_scalar(sq[:, r, :], bank[1 + r][:, :], HD * GN_EPS, None, ALU.add).then_inc(s_varV, 1)
            dve.wait_ge(s_root, 1)
            for r in range(RT_):
                V.scalar_tensor_tensor(out=co[:, r, :], in0=co[:, r, :], scalar=CW ** 0.5, in1=stat[:, :],
                                       op0=ALU.mult, op1=ALU.mult).then_inc(s_n, 1)
            dve.wait_ge(s_n, RT_)
            for r in range(RT_):
                dve.wait_ge(s_sig, r + 1)
                link(V.tensor_scalar(co[:, r, :], co[:, r, :], vcol("conv_ln_g", r), vcol("conv_ln_b", r), ALU.mult, ALU.add))
                V.tensor_tensor(co[:, r, :], co[:, r, :], sig[:, r % 3, :], ALU.mult).then_inc(s_u, 1)
            for r in range(RT_):
                dve.wait_ge(s_root, 2 + r)
                link(V.scalar_tensor_tensor(out=y[:, r, :], in0=y[:, r, :], scalar=HD ** 0.5, in1=sq[:, r, :],
                                            op0=ALU.mult, op1=ALU.mult))
                link(V.tensor_scalar(y[:, r, :], y[:, r, :], vcol("gn_g", r), vcol("gn_b", r), ALU.mult, ALU.add))
                link(V.tensor_tensor(y[:, r, :], y[:, r, :], mix.bonus[:, r, :], ALU.add))
                V.tensor_tensor(y[:, r, :], y[:, r, :], mix.gate_r[:, r, :], ALU.mult).then_inc(s_y, 1)
            for n in range(2 * KD):
                dve.wait_ge(s_p, n + 1)
                gated = V.tensor_tensor(gates[:, n, :], gates[:, n, :], bank[5 + n % 3][:, :], ALU.mult)
                if n < KD:
                    gated.then_inc(s_pV, 1)
                else:
                    link(gated)
                    dve.wait_ge(s_pV, n - KD + 1)
                    V.tensor_tensor(gates[:, n - KD, :], gates[:, n - KD, :], gates[:, n, :], ALU.add).then_inc(s_pV, 1)
            dve.wait_ge(s_x, 16)
            for t in range(NT):
                dve.wait_ge(s_r, 2 * t + 1)
                gt, g2row, shift = keep.mod[:, 2 * D:3 * D], keep.mod[:, 4 * D:5 * D], keep.mod[:, 3 * D:4 * D]
                for half in range(2):
                    cs = slice(half * N, half * N + N)
                    link.sign(V.scalar_tensor_tensor(out=h2(t)[:, cs], in0=bank[(2 * t + half) % 4][:, :],
                                                     scalar=rstd[:, 0, t:t + 1], in1=gt[:, cs], op0=ALU.mult, op1=ALU.mult))
                link.wait()
                V.tensor_tensor(x[:, t, :], x[:, t, :], h2(t), ALU.add).then_inc(s_x1, 1)
                dve.wait_ge(s_r, 2 * t + 2)
                dve.wait_ge(s_x1, t + 1)
                link(V.scalar_tensor_tensor(out=h2(t), in0=x[:, t, :], scalar=rstd[:, 1, t:t + 1], in1=g2row,
                                            op0=ALU.mult, op1=ALU.mult))
                V.tensor_tensor(h2(t), h2(t), shift, ALU.add).then_inc(s_h2, 1)


MAXB = NE + S * TOPK // P - 1
NO_TOKEN, NO_ROW = 8 * S, 16 * S * TOPK
BIG = 1e30


def route(nc, w, keep, moe):
    with ExitStack() as stack:
        m = Memory(nc, stack)
        spare = [0]

        def old(*shape):
            size = 1
            for n in shape:
                size *= n
            spare[0] += size
            assert spare[0] <= 5 * D
            flat = keep.mod[:, spare[0] - size:spare[0]]
            names = "abc"[:len(shape)]
            if len(shape) == 1:
                return flat
            return flat.rearrange("p (%s) -> p %s" % (" ".join(names), " ".join(names)), **dict(zip(names, shape)))

        h2 = moe.xg
        h2T = m.sb("h2T", [P, KD, S])
        br = m.sb("b_router", [P, NE])
        ws = m.sb("ws", [P, 2, KD, DE])
        sig, gu = m.sb("sig4", [P, 2, DE]), m.sb("gu4", [P, 2, DE])
        hT = m.sb("hT4", [P, 2, 2, P])
        E = [P, NT, NE]
        wsd, wr, g8 = old(2, D), old(KD, NE), old(NT, NG, 8)
        scores, biased, sel, gated, left, rank, resets = (old(NT, NE) for _ in range(7))
        gs, top4, top8 = (m.sb(n, [P, NT, 8]) for n in ("gs", "top4", "top8"))
        gleft = m.sb("gleft", [P, NT, NG])
        gmask = m.sb("gmask", [P, NT, NG])
        total, over = m.sb("total", [P, NT]), m.sb("over", [P, NT])
        toki, tokf, pi, pf = m.sb("toki", [P, NT], I32), m.sb("tokf", [P, 3, NT]), m.sb("pi", [P, 1], I32), m.sb("pf", [P, 1])
        iota_i = m.sb("iota_i", [P, S], I32)
        colf, before = m.sb("colf4", [P, P]), m.sb("before", [P, P])
        cnt, more, ends, done_, part = (m.sb(n, [P, NE]) for n in ("cnt", "more", "ends", "done_", "part"))
        bf = m.sb("bf", [P, 4])
        bank = [m.bank(f"d{i}") for i in range(8)]
        table = moe.table

        s_h, s_wr, s_ws = [m.sem(f"p4_h2_{t}_in") for t in range(NT)], m.sem("p4_router_in"), m.sem("p4_shared_in")
        s_io = m.sem("p4_iotas")
        s_t, s_tA, s_tV = m.sem("p4_h2_turned"), m.sem("p4_h2T_by_scalar"), m.sem("p4_h2T_by_vector")
        s_lg, s_sc = m.sem("p4_logits"), m.sem("p4_scores")
        s_sel, s_tri = m.sem("p4_selected"), m.sem("p4_before_mask")
        s_pos, s_blk, s_blkp = m.sem("p4_places"), m.sem("p4_blocks"), m.sem("p4_blocks_turned")
        s_s, s_sA, s_sV = m.sem("p4_shared_up"), m.sem("p4_shared_sigmoid"), m.sem("p4_shared_hidden")
        s_ht, s_htA = m.sem("p4_hidden_turned"), m.sem("p4_hiddenT")
        s_dn, s_dnA = m.sem("p4_shared_down"), m.sem("p4_shared_out")
        s_v = m.sem("p4_vector_chain")
        block = stack.enter_context(nc.Block())

        @block.sync
        def _(sp):
            for t in range(NT):
                sp.dma_start(h2[:, t, :], keep.h2_dram[t * P:(t + 1) * P, :]).then_inc(s_h[t], 16)
            sp.dma_start(wr[:, :, :], w["w_router"][0].rearrange("(k p) n -> p k n", p=P)).then_inc(s_wr, 16)
            sp.dma_start(br[:, :], w["b_router"][0].rearrange("(a n) -> a n", a=1).to_broadcast([P, NE])).then_inc(s_wr, 16)
            for j, name in enumerate(("ws_gate", "ws_up")):
                sp.dma_start(ws[:, j, :, :], w[name][0].rearrange("(k p) n -> p k n", p=P)).then_inc(s_ws, 16)
            sp.dma_start(wsd[:, :, :], w["ws_down"][0].rearrange("(k p) n -> p k n", p=P)).then_inc(s_ws, 16)
            for b in range(moe.RING):
                moe.load(sp, b, b)

        @block.gpsimd
        def _(pool):
            pool.iota(toki[:, :], [[P, NT]], base=0, channel_multiplier=1).then_inc(s_io, 1)
            pool.iota(pi[:, :], [[0, 1]], base=0, channel_multiplier=1).then_inc(s_io, 1)
            pool.iota(iota_i[:, :], [[1, S]], base=0, channel_multiplier=0).then_inc(s_io, 1)
            pool.memset(resets[:, :, :], 1.0).then_inc(s_io, 1)
            pool.memset(moe.offsets[:, 0:1], float(NO_TOKEN)).then_inc(s_io, 1)
            pool.memset(moe.offsets[:, 1:2], float(NO_ROW)).then_inc(s_io, 1)
            pool.wait_ge(s_io, 6)
            pool.memset(resets[:, :, 0:1], 0.0).then_inc(s_io, 1)

        @block.scalar
        def _(act):
            for t in range(NT):
                act.wait_ge(s_t, 2 * t + 1)
                act.activation(h2T[:, 0:4, t * P:(t + 1) * P], bank[0][:, :].rearrange("p (k s) -> p k s", k=4),
                               ACT.Copy).then_inc(s_tA, 1)
            act.wait_ge(s_lg, 1)
            act.activation(scores[:, :, :], bank[2][:, 0:NT * NE].rearrange("p (t e) -> p t e", t=NT),
                           ACT.Sigmoid).then_inc(s_sc, 1)

            def sigmoid(t):
                act.wait_ge(s_s, t + 1)
                if t >= 2:
                    act.wait_ge(s_sV, t - 1)
                act.activation(sig[:, t % 2, :], bank[4 + t % 2][:, 0:DE], ACT.Sigmoid).then_inc(s_sA, 1)

            sigmoid(0)
            for t in range(NT):
                if t < NT - 1:
                    sigmoid(t + 1)
                act.wait_ge(s_ht, t + 1)
                if t >= 2:
                    act.wait_ge(s_dn, t - 1)
                act.activation(hT[:, t % 2, :, :], bank[3][:, 0:2 * P].rearrange("p (k s) -> p k s", k=2),
                               ACT.Copy).then_inc(s_htA, 1)
                act.wait_ge(s_dn, t + 1)
                for half in range(2):
                    act.activation(moe.shared[:, t, half * N:half * N + N], bank[6 + half][:, :], ACT.Copy).then_inc(s_dnA, 1)

        @block.tensor
        def _(pe):
            for t in range(NT):
                pe.wait_ge(s_h[t], 16)
                for half in range(2):
                    if t:
                        pe.wait_ge((s_tA, s_tV)[half], t)
                    for k in range(4):
                        c0 = (half * 4 + k) * P
                        mm = pe.transpose(bank[half][:, k * P:(k + 1) * P], h2[:, t, c0:c0 + P], keep.ident[:, :])
                    mm.then_inc(s_t, 1)
            pe.wait_ge(s_wr, 32)
            pe.wait_ge(s_tA, NT)
            pe.wait_ge(s_tV, NT)
            for t in range(NT):
                for k in range(KD):
                    mm = pe.matmul(bank[2][:, t * NE:(t + 1) * NE], h2T[:, k, t * P:(t + 1) * P], wr[:, k, :],
                                   start=(k == 0), stop=(k == KD - 1))
            mm.then_inc(s_lg, 1)
            pe.wait_ge(s_ws, 48)

            def shared_up(t):
                if t >= 2:
                    pe.wait_ge(s_sV, t - 1)
                for k in range(KD):
                    mm = pe.matmul(bank[4 + t % 2][:, :], h2T[:, k, t * P:(t + 1) * P], ws[:, :, k, :],
                                   start=(k == 0), stop=(k == KD - 1))
                mm.then_inc(s_s, 1)

            def shared_down(t):
                pe.wait_ge(s_sV, t + 1)
                if t:
                    pe.wait_ge(s_htA, t)
                for k in range(2):
                    mm = pe.transpose(bank[3][:, k * P:(k + 1) * P], gu[:, t % 2, k * P:(k + 1) * P], keep.ident[:, :])
                mm.then_inc(s_ht, 1)
                pe.wait_ge(s_htA, t + 1)
                if t:
                    pe.wait_ge(s_dnA, 2 * t)
                for half in range(2):
                    for k in range(2):
                        mm = pe.matmul(bank[6 + half][:, :], hT[:, t % 2, k, :], wsd[:, k, half * N:half * N + N],
                                       start=(k == 0), stop=(k == 1))
                mm.then_inc(s_dn, 1)

            def places():
                pe.wait_ge(s_sel, 1)
                pe.wait_ge(s_tri, 1)
                for t in range(NT):
                    for u in range(t + 1):
                        pe.matmul(bank[0][:, t * NE:(t + 1) * NE], before[:, :] if u == t else keep.ones[:, :], sel[:, u, :],
                                  start=(u == 0), stop=(u == t))
                for u in range(NT):
                    mm = pe.matmul(bank[1][:, 0:NE], keep.ones[:, :], sel[:, u, :], start=(u == 0), stop=(u == NT - 1))
                mm.then_inc(s_pos, 1)

            shared_up(0)
            shared_up(1)
            shared_down(0)
            shared_up(2)
            shared_down(1)
            places()
            shared_up(3)
            shared_down(2)
            shared_down(3)
            pe.wait_ge(s_blk, 1)
            for j in range(2):
                mm = pe.matmul(bank[2][0:1, j * P:(j + 1) * P], bf[:, j:j + 1], keep.ident[:, :], start=True, stop=True)
            mm.then_inc(s_blkp, 1)

        @block.vector
        def _(dve):
            link = Link(dve, s_v)
            V = nc.vector

            def hidden(t):
                dve.wait_ge(s_sA, t + 1)
                link(V.tensor_tensor(sig[:, t % 2, :], sig[:, t % 2, :], bank[4 + t % 2][:, 0:DE], ALU.mult))
                if t >= 2:
                    dve.wait_ge(s_ht, t - 1)
                V.tensor_tensor(gu[:, t % 2, :], sig[:, t % 2, :], bank[4 + t % 2][:, DE:2 * DE], ALU.mult).then_inc(s_sV, 1)

            dve.wait_ge(s_io, 7)
            link.sign(V.tensor_copy(tokf[:, 0, :], toki[:, :]))
            link.sign(V.tensor_copy(pf[:, :], pi[:, :]))
            link.sign(V.tensor_copy(moe.iota[:, :], iota_i[:, :]))
            link(V.tensor_copy(colf[:, :], iota_i[:, 0:P]))
            V.tensor_scalar(before[:, :], colf[:, :], pf[:, 0:1], None, ALU.is_gt).then_inc(s_tri, 1)
            link.sign(V.tensor_scalar(tokf[:, 1, :], tokf[:, 0, :], float(-NO_TOKEN), None, ALU.add))
            link.sign(V.tensor_scalar(tokf[:, 2, :], tokf[:, 0, :], float(TOPK), float(-NO_ROW), ALU.mult, ALU.add))
            for t in range(NT):
                dve.wait_ge(s_t, 2 * t + 2)
                V.tensor_copy(h2T[:, 4:8, t * P:(t + 1) * P],
                              bank[1][:, :].rearrange("p (k s) -> p k s", k=4)).then_inc(s_tV, 1)
            dve.wait_ge(s_sc, 1)
            dve.wait_ge(s_wr, 32)
            link(V.tensor_tensor(biased[:, :, :], scores[:, :, :], br[:, :].unsqueeze(1).to_broadcast(E), ALU.add))
            hidden(0)
            for t in range(NT):
                for g in range(NG):
                    link.sign(V.max(g8[:, t, g, :], biased[:, t, g * PER:(g + 1) * PER]))
            link.wait()
            link(V.tensor_tensor(gs[:, :, :], g8[:, :, :, 0], g8[:, :, :, 1], ALU.add))
            for t in range(NT):
                link.sign(V.max(top4[:, t, :], gs[:, t, :]))
            link.wait()
            hidden(1)
            link(V.tensor_scalar(top4[:, :, TOPG:], top4[:, :, TOPG:], 0.0, -4.0 * BIG, ALU.mult, ALU.add))
            for t in range(NT):
                link.sign(V.match_replace(out=gleft[:, t, :], in_to_replace=top4[:, t, :], in_values=gs[:, t, :],
                                          imm_value=-2.0 * BIG))
            link.wait()
            link(V.tensor_tensor(gmask[:, :, :], gleft[:, :, :], gs[:, :, :], ALU.is_lt))
            link(V.tensor_scalar(gmask[:, :, :], gmask[:, :, :], -1.0, BIG, ALU.add, ALU.mult))
            for t in range(NT):
                link.sign(V.tensor_tensor(biased[:, t, :].rearrange("p (g m) -> p g m", g=NG),
                                          biased[:, t, :].rearrange("p (g m) -> p g m", g=NG),
                                          gmask[:, t, :].unsqueeze(2).to_broadcast([P, NG, PER]), ALU.add))
            link.wait()
            for t in range(NT):
                link.sign(V.max(top8[:, t, :], biased[:, t, :]))
            link.wait()
            for t in range(NT):
                link.sign(V.match_replace(out=left[:, t, :], in_to_replace=top8[:, t, :], in_values=biased[:, t, :],
                                          imm_value=-2.0 * BIG))
            link.wait()
            V.tensor_tensor(sel[:, :, :], left[:, :, :], biased[:, :, :], ALU.is_lt).then_inc(s_sel, 1)
            dve.wait_ge(s_sel, 1)
            link(V.tensor_tensor(gated[:, :, :], scores[:, :, :], sel[:, :, :], ALU.mult))
            link(V.tensor_reduce(total[:, :], gated[:, :, :], AX.X, ALU.add))
            hidden(2)
            link(V.reciprocal(over[:, :], total[:, :]))
            for t in range(NT):
                link.sign(V.tensor_scalar(table[:, t, :, 0], gated[:, t, :], over[:, t:t + 1], SCALE, ALU.mult, ALU.mult))
                link.sign(V.tensor_scalar(table[:, t, :, 1], sel[:, t, :], 0.0, tokf[:, 1, t:t + 1], ALU.mult, ALU.add))
            link(V.tensor_tensor_scan(rank[:, :, :].rearrange("p t e -> p (t e)"), resets[:, :, :].rearrange("p t e -> p (t e)"),
                                      sel[:, :, :].rearrange("p t e -> p (t e)"), 0.0, ALU.mult, ALU.add))
            link(V.tensor_tensor(rank[:, :, :], rank[:, :, :], sel[:, :, :], ALU.subtract))
            for t in range(NT):
                link.sign(V.tensor_scalar(table[:, t, :, 2], rank[:, t, :], tokf[:, 2, t:t + 1], None, ALU.add))
            hidden(3)
            dve.wait_ge(s_pos, 1)
            link(V.tensor_scalar(left[:, :, :], sel[:, :, :], -1.0, 4.0 * S, ALU.add, ALU.mult))
            link.sign(V.tensor_tensor(table[:, :, :, 3], left[:, :, :],
                                      bank[0][:, 0:NT * NE].rearrange("p (t e) -> p t e", t=NT), ALU.add))
            link(V.tensor_copy(cnt[:, :], bank[1][:, 0:NE]))
            link(V.tensor_scalar(more[:, :], cnt[:, :], float(P), None, ALU.is_gt))
            for j in range(2, NT):
                link(V.tensor_scalar(part[:, :], cnt[:, :], float(j * P), None, ALU.is_gt))
                link(V.tensor_tensor(more[:, :], more[:, :], part[:, :], ALU.add))
            link(V.tensor_tensor_scan(ends[:, :], keep.ones[:, 0:NE], more[:, :], float(NE), ALU.mult, ALU.add))
            link(V.tensor_copy(moe.n_blocks[0:1, :], ends[0:1, NE - 1:NE]))
            link(V.tensor_scalar(done_[:, :], ends[:, :], pf[:, 0:1], None, ALU.is_le))
            link(V.tensor_tensor(part[:, :], done_[:, :], more[:, :], ALU.mult))
            link(V.tensor_reduce(bf[:, 2:3], done_[:, :], AX.X, ALU.add))
            link(V.tensor_reduce(bf[:, 3:4], part[:, :], AX.X, ALU.add))
            link(V.tensor_scalar(bf[:, 3:4], bf[:, 3:4], -1.0, pf[:, 0:1], ALU.mult, ALU.add))
            link(V.tensor_scalar(bf[:, 3:4], bf[:, 3:4], float(1 - NE), float(P), ALU.add, ALU.mult))
            link(V.tensor_scalar(bf[:, 2:3], bf[:, 2:3], float(NE - 1), None, ALU.min))
            link(V.tensor_scalar(part[:, 0:1], pf[:, :], float(NE), None, ALU.is_lt))
            link(V.tensor_scalar(bf[:, 3:4], bf[:, 3:4], 0.0, float(S - P), ALU.max, ALU.min))
            link(V.tensor_scalar(part[:, 1:2], part[:, 0:1], -1.0, 1.0, ALU.mult, ALU.add))
            link(V.tensor_tensor(bf[:, 1:2], bf[:, 3:4], part[:, 1:2], ALU.mult))
            link(V.tensor_tensor(bf[:, 2:3], bf[:, 2:3], part[:, 1:2], ALU.mult))
            link(V.tensor_tensor(part[:, 2:3], pf[:, :], part[:, 0:1], ALU.mult))
            V.tensor_tensor(bf[:, 0:1], bf[:, 2:3], part[:, 2:3], ALU.add).then_inc(s_blk, 1)
            dve.wait_ge(s_blkp, 1)
            link(V.tensor_copy(moe.blocks[0:1, :, :].rearrange("p a b -> p (a b)"), bank[2][0:1, 0:2 * P]))


def plan_experts(nc, m, w, keep, moe):
    moe.RING = 4
    moe.ring = m.sb("expert_ring", [P, moe.RING, 3 * KD * DE])
    moe.table = m.sb("table", [P, NT, NE, 4])
    moe.iota = m.sb("iota", [P, S])
    moe.xg = m.sb("xg", [P, 4, D])
    moe.blocks = m.sb("blocks", [1, 2, P], I32)
    moe.n_blocks = m.sb("n_blocks", [1, 1], I32)
    moe.offsets = m.sb("offsets", [P, 2])
    moe.s_ring = [m.sem(f"expert_slot{i}_in") for i in range(moe.RING)]
    moe.rows = nc.dram_tensor("expert_rows", (S * TOPK, D), F32, kind="Internal").ap()
    width = KD * DE
    parts = [w["we_gate"][0].rearrange("e (p k) n -> e p (k n)", k=KD),
             w["we_up"][0].rearrange("e (p k) n -> e p (k n)", k=KD),
             w["we_down"][0].rearrange("e (p k) n -> e p (k n)", k=2)]

    def load(engine, expert, slot):
        for j, part in enumerate(parts):
            source = part[expert] if isinstance(expert, int) else part[bass.ds(expert, 1)].rearrange("a p n -> (a p) n")
            engine.dma_start(moe.ring[:, slot, j * width:(j + 1) * width], source).then_inc(moe.s_ring[slot], 16)

    moe.load = load


def experts(nc, w, keep, moe):
    with ExitStack() as stack:
        m = Memory(nc, stack)
        RING = moe.RING
        hot = m.sb("hot", [P, 2, NT, P])
        column = m.sb("column", [P, 2, NT, 4])
        gate = m.sb("gate", [P, 4, 1])
        tokens = m.sb("tokens", [P, 4, 1], U32)
        rowf = m.sb("row_float", [P, 4, 1])
        row_ids = m.sb("row_ids", [P, 4, 1], U32)
        xT = m.sb("xT", [P, 2, KD, P])
        sig = m.sb("sig5", [P, 2, DE])
        hid = m.sb("hid", [P, 2, DE])
        hT = m.sb("hT5", [P, 2, 2, P])
        y = m.sb("y5", [P, 4, D])
        carrier = m.sb("carrier", [1, 2])
        px = [m.bank(f"px{i}") for i in range(2)]
        pg, pu = m.bank("p_gate", [P, DE]), m.bank("p_up", [P, DE])
        py = [m.bank(f"py{i}") for i in range(2)]
        ph, pid = m.bank("ph"), m.bank("pid")

        s_gather, s_scatter = m.sem("p5_gather_may_start"), m.sem("p5_scatter_may_start")
        s_col, s_hot = m.sem("p5_column"), m.sem("p5_one_hot")
        s_id = m.sem("p5_numbers_product")
        s_num, s_rows = m.sem("p5_token_numbers"), m.sem("p5_row_numbers")
        s_xg = [m.sem(f"p5_gathered{i}") for i in range(4)]
        s_x = m.sem("p5_x_turned")
        s_xA, s_xV = m.sem("p5_xT_by_scalar"), m.sem("p5_xT_by_vector")
        s_pg, s_gu = m.sem("p5_gate_product"), m.sem("p5_up")
        s_sig, s_t, s_hid = m.sem("p5_sigmoid"), m.sem("p5_silu"), m.sem("p5_hidden")
        s_h, s_hA = m.sem("p5_hidden_turned"), m.sem("p5_hiddenT")
        s_y, s_yA, s_yV = m.sem("p5_down"), m.sem("p5_y_by_scalar"), m.sem("p5_y_by_vector")
        s_out = [m.sem(f"p5_scattered{i}") for i in range(4)]
        block = stack.enter_context(nc.Block())
        MAIN = NE - 4
        STEPS = (MAXB + 3) // 4 * 4

        def steps(engine, stages, last=None):
            most = max(lead for lead, _ in stages)
            for i in range(-most, 4):
                for lead, code in stages:
                    if i + lead >= 0 and (i >= 0 or i + lead < lead):
                        code(i + lead, i + lead, True)
            with engine.Fori(1, MAIN // 4) as turn:
                for u in range(4):
                    for lead, code in stages:
                        code(4 * turn + (u + lead), u + lead, True)
            count = engine.value_load(moe.n_blocks[0:1, 0:1], min_val=NE, max_val=MAXB)
            with engine.Fori(MAIN // 4, STEPS // 4) as turn:
                with engine.If(4 * turn < count):
                    for u in range(4):
                        for lead, code in stages:
                            with engine.If(4 * turn + (u + lead) < count):
                                code(4 * turn + (u + lead), u + lead, False)
                                if last is not None and lead == 0:
                                    last(4 * turn + u, u)

        def taken(engine, semaphore, b, back):
            if isinstance(b, int) and b < back:
                return
            engine.wait_ge(semaphore, b - back + 1)

        def slot_done(engine, semaphores, b, u, per):
            if isinstance(b, int):
                engine.wait_ge(semaphores[b % 4], per * (b // 4 + 1))
            else:
                engine.wait_ge(semaphores[u % 4], per // 4 * b + (per - per // 4 * (u % 4)))

        def left(engine, b, u):
            if isinstance(b, int) and b < 4:
                return
            slot_done(engine, s_out, b - 4, u % 4, 16)

        @block.sync
        def _(sp):
            with sp.Fori(1, NE // RING) as turn:
                for u in range(RING):
                    sp.wait_ge(s_y, RING * turn + (u - RING + 1))
                    moe.load(sp, RING * turn + u, u)
            count = sp.value_load(moe.n_blocks[0:1, 0:1], min_val=NE, max_val=MAXB)
            with sp.Fori(NE // RING, STEPS // RING) as turn:
                with sp.If(RING * turn < count):
                    for u in range(RING):
                        with sp.If(RING * turn + u < count):
                            sp.wait_ge(s_y, RING * turn + (u - RING + 1))
                            expert = sp.value_load(moe.blocks[0:1, 0, bass.ds(RING * turn + u, 1)], min_val=0, max_val=NE - 1)
                            moe.load(sp, expert, u)

        @block.gpsimd
        def _(pool):
            last_token, last_row = pool.to_reg(S - 1), pool.to_reg(S * TOPK - 1)

            def carry_wait(semaphore, b, place):
                taken(pool, semaphore, b, 1)
                nc.gpsimd.tensor_tensor(carrier[0:1, place:place + 1], moe.offsets[0:1, 0:1], moe.offsets[0:1, 0:1],
                                        ALU.add).then_inc(semaphore, 1)

            def gather(b, u, first):
                pool.wait_ge(s_num, b + 1)
                taken(pool, s_x, b, 4)
                carry_wait(s_gather, b, 0)
                pool.indirect_dma_start(moe.xg[:, u % 4, :], None, keep.h2_dram,
                                        bass.IndirectOffsetOnAxis(tokens[:, u % 4, 0:1], 0),
                                        bounds_check=last_token, oob_is_err=False).then_inc(s_xg[u % 4], 16)

            def scatter(b, u, first):
                pool.wait_ge(s_rows, b + 1)
                pool.wait_ge(s_yA, b + 1)
                pool.wait_ge(s_yV, b + 1)
                carry_wait(s_scatter, b, 1)
                pool.indirect_dma_start(moe.rows, bass.IndirectOffsetOnAxis(row_ids[:, u % 4, 0:1], 0), y[:, u % 4, :], None,
                                        bounds_check=last_row, oob_is_err=False).then_inc(s_out[u % 4], 16)

            steps(pool, [(3, gather), (0, scatter)], lambda b, u: slot_done(pool, s_out, b, u, 16))

        @block.scalar
        def _(act):
            def sigmoid(b, u, first):
                act.wait_ge(s_pg, b + 1)
                taken(act, s_hid, b, 2)
                act.activation(sig[:, u % 2, :], pg[:, :], ACT.Sigmoid).then_inc(s_sig, 1)

            def xT_half(b, u, first):
                act.wait_ge(s_x, b + 1)
                taken(act, s_gu, b, 2)
                act.activation(xT[:, u % 2, 0:4, :], px[0][:, :].rearrange("p (k s) -> p k s", k=4), ACT.Copy).then_inc(s_xA, 1)

            def hiddenT(b, u, first):
                act.wait_ge(s_h, b + 1)
                taken(act, s_y, b, 2)
                act.activation(hT[:, u % 2, :, :], ph[:, 0:2 * P].rearrange("p (k s) -> p k s", k=2), ACT.Copy).then_inc(s_hA, 1)

            def y_half(b, u, first):
                act.wait_ge(s_y, b + 1)
                left(act, b, u)
                act.activation(y[:, u % 4, 0:N], py[0][:, :], ACT.Copy).then_inc(s_yA, 1)

            steps(act, [(0, sigmoid), (1, xT_half), (0, hiddenT), (0, y_half)])

        @block.tensor
        def _(pe):
            def up(b, u, first):
                slot_done(pe, moe.s_ring, b, u, 48)
                pe.wait_ge(s_xA, b + 1)
                pe.wait_ge(s_xV, b + 1)
                weights = moe.ring[:, u % RING, 0:2 * KD * DE].rearrange("p (j k n) -> p j k n", j=2, k=KD)
                for j, (bank, read, done) in enumerate(((pg, s_t, s_pg), (pu, s_hid, s_gu))):
                    taken(pe, read, b, 1)
                    for k in range(KD):
                        mm = pe.matmul(bank[:, :], xT[:, u % 2, k, :], weights[:, j, k, :], start=(k == 0), stop=(k == KD - 1))
                    mm.then_inc(done, 1)

            def turn_x(b, u, first):
                slot_done(pe, s_xg, b, u, 16)
                taken(pe, s_xA, b, 1)
                taken(pe, s_xV, b, 1)
                rows = moe.xg[:, u % 4, :].rearrange("p (d k) -> p k d", k=KD)
                for k in range(KD):
                    mm = pe.transpose(px[k // 4][:, (k % 4) * P:(k % 4 + 1) * P], rows[:, k, :], keep.ident[:, :])
                mm.then_inc(s_x, 1)

            def turn_hidden(b, u, first):
                pe.wait_ge(s_hid, b + 1)
                taken(pe, s_hA, b, 1)
                rows = hid[:, u % 2, :].rearrange("p (d k) -> p k d", k=2)
                for k in range(2):
                    mm = pe.transpose(ph[:, k * P:(k + 1) * P], rows[:, k, :], keep.ident[:, :])
                mm.then_inc(s_h, 1)

            def numbers(b, u, first):
                pe.wait_ge(s_hot, b + 1)
                taken(pe, s_num, b, 1)
                for t in range(NT):
                    mm = pe.matmul(pid[:, 0:4], hot[:, u % 2, t, :], column[:, u % 2, t, :], start=(t == 0), stop=(t == NT - 1))
                mm.then_inc(s_id, 1)

            def down(b, u, first):
                pe.wait_ge(s_hA, b + 1)
                taken(pe, s_yA, b, 1)
                taken(pe, s_yV, b, 1)
                weights = moe.ring[:, u % RING, 2 * KD * DE:3 * KD * DE].rearrange("p (k n) -> p k n", k=2)
                for half in range(2):
                    for k in range(2):
                        mm = pe.matmul(py[half][:, :], hT[:, u % 2, k, :], weights[:, k, half * N:half * N + N],
                                       start=(k == 0), stop=(k == 1))
                mm.then_inc(s_y, 1)

            steps(pe, [(0, up), (1, turn_x), (0, turn_hidden), (3, numbers), (0, down)])

        @block.vector
        def _(dve):
            V = nc.vector

            def silu(b, u, first):
                dve.wait_ge(s_sig, b + 1)
                V.scalar_tensor_tensor(out=sig[:, u % 2, :], in0=pg[:, :], scalar=gate[:, u % 4, :], in1=sig[:, u % 2, :],
                                       op0=ALU.mult, op1=ALU.mult).then_inc(s_t, 1)

            def hidden(b, u, first):
                dve.wait_ge(s_gu, b + 1)
                dve.wait_ge(s_t, b + 1)
                taken(dve, s_h, b, 2)
                V.tensor_tensor(hid[:, u % 2, :], sig[:, u % 2, :], pu[:, :], ALU.mult).then_inc(s_hid, 1)

            def xT_half(b, u, first):
                dve.wait_ge(s_x, b + 1)
                taken(dve, s_gu, b, 2)
                V.tensor_copy(xT[:, u % 2, 4:8, :], px[1][:, :].rearrange("p (k s) -> p k s", k=4)).then_inc(s_xV, 1)

            def numbers(b, u, first):
                dve.wait_ge(s_id, b + 1)
                taken(dve, s_x, b, 4)
                V.tensor_copy(gate[:, u % 4, :], pid[:, 0:1])
                V.tensor_copy(rowf[:, u % 4, :], pid[:, 2:3])
                V.tensor_tensor(tokens[:, u % 4, :], pid[:, 1:2], moe.offsets[:, 0:1], ALU.add).then_inc(s_num, 1)

            def row_numbers(b, u, first):
                dve.wait_ge(s_num, b + 1)
                left(dve, b, u)
                V.tensor_tensor(row_ids[:, u % 4, :], rowf[:, u % 4, :], moe.offsets[:, 1:2], ALU.add).then_inc(s_rows, 1)

            def places(b, u, first):
                expert, start = b, 0
                if not first:
                    expert = dve.value_load(moe.blocks[0:1, 0, bass.ds(b, 1)], min_val=0, max_val=NE - 1)
                    start = dve.value_load(moe.blocks[0:1, 1, bass.ds(b, 1)], min_val=0, max_val=S - P)
                taken(dve, s_id, b, 2)
                V.tensor_copy(column[:, u % 2, :, :].unsqueeze(2), moe.table[:, :, bass.ds(expert, 1), :]).then_inc(s_col, 1)
                dve.wait_ge(s_col, b + 1)
                for t in range(NT):
                    last = V.tensor_scalar(hot[:, u % 2, t, :], moe.iota[:, bass.ds(start, P)], column[:, u % 2, t, 3:4], None,
                                           ALU.is_equal)
                last.then_inc(s_hot, 1)

            def y_half(b, u, first):
                dve.wait_ge(s_y, b + 1)
                left(dve, b, u)
                V.tensor_copy(y[:, u % 4, N:2 * N], py[1][:, :]).then_inc(s_yV, 1)

            steps(dve, [(0, silu), (0, hidden), (1, xT_half), (3, numbers), (1, row_numbers), (4, places), (0, y_half)])


def combine(nc, w, keep, moe, out):
    with ExitStack() as stack:
        m = Memory(nc, stack)
        rows = m.sb("rows6", [P, 2, TOPK * D])
        x1 = m.sb("x6", [P, NT, D])
        y = m.sb("y6", [P, 2, D])
        sq = m.sb("sq6", [P, D])
        sums, mean_sq, rstd = m.sb("sums6", [P, NT]), m.sb("mean_sq6", [P, NT]), m.sb("rstd6", [P, NT])
        s_in, s_x = m.sem("p6_rows_in"), m.sem("p6_x1_in")
        s_red, s_y, s_sq, s_r, s_o, s_st = (m.sem(f"p6_{n}") for n in ("reduced", "y", "squares", "rstd", "out", "stored"))
        s_v, s_a = m.sem("p6_vector_chain"), m.sem("p6_scalar_chain")
        s_in = [m.sem(f"p6_rows{i}_in") for i in range(2)]
        block = stack.enter_context(nc.Block())
        expert_rows = moe.rows.rearrange("(t p j) d -> t p (j d)", p=P, j=TOPK)

        @block.sync
        def _(sp):
            for t in range(NT):
                if t >= 2:
                    sp.wait_ge(s_red, t - 1)
                sp.dma_start(rows[:, t % 2, :], expert_rows[t]).then_inc(s_in[t % 2], 16)
                if t == 0:
                    sp.dma_start(x1[:, :, :], keep.x1_dram.rearrange("(t p) d -> p t d", p=P)).then_inc(s_x, 16)
            for t in range(NT):
                sp.wait_ge(s_o, t + 1)
                sp.dma_start(out[0, t * P:(t + 1) * P, :], x1[:, t, :]).then_inc(s_st, 16)
            sp.wait_ge(s_st, 16 * NT)

        @block.gpsimd
        def _(pool):
            for t in range(NT):
                pool.wait_ge(s_sq, t + 1)
                pool.tensor_tensor(rstd[:, t:t + 1], mean_sq[:, t:t + 1], keep.power[:, 0:1], ALU.pow).then_inc(s_r, 1)

        @block.scalar
        def _(act):
            link = Link(act, s_a)
            for t in range(NT):
                act.wait_ge(s_y, t + 1)
                link(act.activation(sq[:, :], y[:, t % 2, :], ACT.Square, accum_out=sums[:, t:t + 1]))
                act.activation(mean_sq[:, t:t + 1], sums[:, t:t + 1], ACT.Copy, scale=1.0 / D, bias=RMS_EPS).then_inc(s_sq, 1)

        @block.vector
        def _(dve):
            link = Link(dve, s_v)
            V = nc.vector
            gt = keep.mod[:, 5 * D:6 * D]

            def finish(t):
                dve.wait_ge(s_r, t + 1)
                dve.wait_ge(s_x, 16)
                link(V.scalar_tensor_tensor(out=y[:, t % 2, :], in0=y[:, t % 2, :], scalar=rstd[:, t:t + 1], in1=gt,
                                            op0=ALU.mult, op1=ALU.mult))
                V.tensor_tensor(x1[:, t, :], x1[:, t, :], y[:, t % 2, :], ALU.add).then_inc(s_o, 1)

            for t in range(NT):
                dve.wait_ge(s_in[t % 2], 16 * (t // 2 + 1))
                if t >= 2:
                    dve.wait_ge(s_o, t - 1)
                V.tensor_reduce(y[:, t % 2, :], rows[:, t % 2, :].rearrange("p (j d) -> p d j", j=TOPK), AX.X,
                                ALU.add).then_inc(s_red, 1)
                dve.wait_ge(s_red, t + 1)
                V.tensor_tensor(y[:, t % 2, :], y[:, t % 2, :], moe.shared[:, t, :], ALU.add).then_inc(s_y, 1)
                if t:
                    finish(t - 1)
            finish(NT - 1)


class Names:
    pass


def layer(nc, w, out):
    with ExitStack() as stack:
        m = Memory(nc, stack)
        keep = Names()
        keep.mod = m.sb("mod", [P, 6 * D])
        keep.ident = m.sb("ident", [P, P])
        keep.ones = m.sb("ones", [P, P])
        keep.power = m.sb("power", [P, 8])
        keep.vec = m.sb("vec", [P, N_VEC])
        keep.one_minus_mu = m.sb("one_minus_mu", [P, NZ_RWKV])
        keep.silu_c = m.sb("silu_c", [P, KD])
        keep.x1_dram = nc.dram_tensor("x1_rows", (S, D), F32, kind="Internal").ap()
        keep.h2_dram = nc.dram_tensor("h2_rows", (S, D), F32, kind="Internal").ap()
        with ExitStack() as mix_stack:
            mm = Memory(nc, mix_stack)
            mix = Names()
            mix.gates = mm.sb("gates", [P, NZ_GATE, S])
            mix.zr = mm.sb("zr", [P, NZ_RWKV, S])
            mix.co = mm.sb("co", [P, RT_, S])
            mix.taps = mm.sb("taps", [P, N_TAP])
            project(nc, w, keep, mix)
            mix.gate_r = mm.sb("gate_r", [P, RT_, S])
            mix.bonus = mm.sb("bonus", [P, RT_, S])
            rwkv(nc, w, keep, mix)
            merge(nc, w, keep, mix)
        moe = Names()
        moe.shared = m.sb("shared", [P, NT, D])
        with ExitStack() as moe_stack:
            me = Memory(nc, moe_stack)
            plan_experts(nc, me, w, keep, moe)
            route(nc, w, keep, moe)
            experts(nc, w, keep, moe)
        combine(nc, w, keep, moe, out)


_INS = ["x", "c", "w_ada", "b_ada", "norm_mix_pre", "norm_mix_post", "norm_ffn_pre", "norm_ffn_post", "w_in",
        "mu_shift", "conv_w", "conv_b", "conv_ln_g", "conv_ln_b", "p_conv", "w0", "w2", "a0", "a2", "g2", "k_k",
        "k_a", "r_k", "gn_g", "gn_b", "p_rwkv", "w_o", "w_router", "b_router", "we_gate", "we_up", "we_down",
        "ws_gate", "ws_up", "ws_down"]


def kernel(**inputs):
    import numpy as np
    import concourse.bacc as bacc
    from concourse.bass_utils import run_bass_kernel_spmd

    nc = bacc.Bacc("TRN2", target_bir_lowering=False, num_devices=1)
    arrays, w = {}, {}
    for name in _INS:
        a = np.ascontiguousarray(inputs[name])
        arrays[f"in_{name}"] = a
        w[name] = nc.dram_tensor(f"in_{name}", a.shape, mybir.dt.from_np(a.dtype), kind="ExternalInput").ap()
    out = nc.dram_tensor("out_rows", (1, S, D), F32, kind="ExternalOutput").ap()
    layer(nc, w, out)
    result = run_bass_kernel_spmd(nc, [arrays], core_ids=[0])
    return result.results[0]["out_rows"]
```

```python
from contextlib import ExitStack

import concourse.bass as bass
from concourse import mybir

F32 = mybir.dt.float32
F32R = mybir.dt.float32r
BF16 = mybir.dt.bfloat16
I32 = mybir.dt.int32
U32 = mybir.dt.uint32
ALU = mybir.AluOpType
ACT = mybir.ActivationFunctionType
AX = mybir.AxisListType

P = 128
D = 1024
S = 512
KD = D // P
NT = S // P
CW = 512
CK = 31
RW = 512
RT_ = RW // P
HEADS, HD = 8, 64
LORA_W, LORA_A, LORA_G = 64, 64, 128
COL_CONV = 2 * CW
COL_RWKV = 3 * RW + LORA_W + LORA_A + LORA_G
COL_GATE = 2 * D
NE, NG, PER, TOPK, TOPG = 64, 8, 8, 8, 4
DE = 256
SCALE = 2.5
RMS_EPS, LN_EPS, GN_EPS = 1e-6, 1e-5, 64e-5
DECAY = float(0.6065306597126334)
N = 512


class Link:

    def __init__(self, engine, semaphore):
        self.engine, self.semaphore, self.count = engine, semaphore, 0

    def sign(self, instruction):
        self.count += 1
        instruction.then_inc(self.semaphore, 1)
        return self.count

    def wait(self, count=None):
        self.engine.wait_ge(self.semaphore, self.count if count is None else count)

    def __call__(self, instruction):
        self.sign(instruction)
        self.wait()


class Memory:

    def __init__(self, nc, stack):
        self.nc, self.stack, self.semaphores = nc, stack, []

    def sb(self, name, shape, dtype=F32):
        return self.stack.enter_context(self.nc.sbuf_tensor(name, shape, dtype))

    def bank(self, name, shape=None):
        return self.stack.enter_context(self.nc.psum_tensor(name, shape or [P, N], F32))

    def sem(self, name):
        self.semaphores.append(self.nc.alloc_semaphore(name=name))
        return self.semaphores[-1]

    def reset_semaphores(self):
        self.nc.clear_and_free_semaphores(self.semaphores)
        self.nc.all_engine_barrier()




VEC_ROWS = [("mu_shift", COL_RWKV // P), ("conv_b", 4), ("conv_ln_g", 4), ("conv_ln_b", 4), ("w0", 4),
            ("a0", 4), ("k_k", 4), ("k_a", 4), ("r_k", 4), ("gn_g", 4), ("gn_b", 4)]
VEC_AT = {}
_row = 0
for _name, _count in VEC_ROWS:
    VEC_AT[_name] = _row
    _row += _count
N_VEC = _row
N_TAP = CK * (CW // P)
GAINS = ["norm_mix_pre", "norm_mix_post", "norm_ffn_pre", "norm_ffn_post"]
ADA = 6 * D // N
N_WIDE = ADA + 2 * len(GAINS)

IN_SLICES = ([(o, N) for o in range(0, COL_CONV, N)]
             + [(COL_CONV + o, N) for o in range(0, 3 * RW, N)]
             + [(COL_CONV + COL_RWKV + o, N) for o in range(0, COL_GATE, N)]
             + [(COL_CONV + 3 * RW, COL_RWKV - 3 * RW)])
STREAM = [("ada", i) for i in range(4)]
_ada = 4
for _i in range(len(IN_SLICES)):
    STREAM.append(("in", _i))
    if _i >= 1 and _ada < ADA:
        STREAM.append(("ada", _ada))
        _ada += 1
while _ada < ADA:
    STREAM.append(("ada", _ada))
    _ada += 1
STREAM_AT = {item: n for n, item in enumerate(STREAM)}
RING1 = 3
PAIR = 2 * P
FIRST = 4
DIRECT = 2
Z_TILES = [(s, t) for s, (_, w) in enumerate(IN_SLICES) for t in range(w // P)]
NZ_RWKV, NZ_CONV, NZ_GATE = COL_RWKV // P, COL_CONV // P, COL_GATE // P
Z_KINDS = ([("value", i) for i in range(NZ_CONV // 2)] + [("sigmoid", i) for i in range(NZ_CONV // 2)]
           + [("rwkv", i) for i in range(3 * RW // P)] + [("gate", i) for i in range(NZ_GATE)]
           + [("rwkv", i) for i in range(3 * RW // P, NZ_RWKV)])
TAPS_A_TILE = 6
TAPS = CK * (CW // P)


def project(nc, w, keep, mix):
    with ExitStack() as stack:
        m = Memory(nc, stack)
        with ExitStack() as first_use:
            mf = Memory(nc, first_use)
            ring = mf.sb("ring1", [P, RING1, KD, N])
            x = mf.sb("x1", [P, NT, D])
            hT = mf.sb("hT", [P, KD, S])
        ring_lo = m.sb("ring_lo", [P, RING1, KD, N], F32R)
        h_hi = m.sb("h_hi", [P, KD, S], F32R)
        h_lo = m.sb("h_lo", [P, KD, S], F32R)
        w_hi = m.sb("w_hi", [P, 2, KD, PAIR], F32R)
        glu = mix.gates[:, NZ_GATE - 2:, :]
        upad = m.sb("upad", [P, RT_, CK - 1 + S])
        acc = m.sb("ada_acc", [P, 2, N])
        crow = m.sb("crow", [KD, P])
        modcol = m.sb("modcol", [P, 2 * KD])
        vrows = m.sb("vrows", [N_VEC, P])
        trows = m.sb("trows", [N_TAP, P])
        wide = m.sb("wide", [N_WIDE, N])
        mean_sq = m.sb("mean_sq", [P, NT])
        rstd = m.sb("rstd1", [P, NT])
        sums = m.sb("sums1", [P, NT])
        pz = [m.bank(f"pz{i}") for i in range(3)]
        pt = [m.bank(f"pt{i}") for i in range(2)]
        pm, pg = [m.bank(f"pm{i}") for i in range(2)], m.bank("pg")
        vec, taps = keep.vec, mix.taps

        s_const = m.sem("p1_const")
        s_crow, s_wide, s_vrows, s_x = m.sem("p1_c_in"), m.sem("p1_wide_in"), m.sem("p1_vrows_in"), m.sem("p1_x_in")
        s_slot = [m.sem(f"p1_slot{i}_in") for i in range(RING1)]
        s_cT, s_sig, s_silu = m.sem("p1_c_turned"), m.sem("p1_c_sigmoid"), m.sem("p1_silu_c")
        s_vecT, s_vec = m.sem("p1_vec_turned"), m.sem("p1_vec_ready")
        s_sq, s_rstd = m.sem("p1_squares"), m.sem("p1_rstd")
        s_xA, s_xV = m.sem("p1_x_scaled_by_scalar"), m.sem("p1_x_scaled_by_vector")
        s_ada, s_adam = m.sem("p1_ada_partial"), m.sem("p1_ada_summed")
        s_gain, s_adag = m.sem("p1_gain_row"), m.sem("p1_gain_copied")
        s_mod = m.sem("p1_mod_row")
        s_col, s_colV = m.sem("p1_mod_columns"), m.sem("p1_mod_columns_taken")
        s_ht, s_hA = m.sem("p1_x_turned"), m.sem("p1_xT_taken")
        s_mod_h, s_hlo = m.sem("p1_hT"), m.sem("p1_h_lo")
        s_whi, s_wlo = m.sem("p1_w_hi"), m.sem("p1_w_lo")
        s_hhi = m.sem("p1_h_hi")
        s_z = m.sem("p1_z")
        s_zA, s_zV = m.sem("p1_z_taken_by_scalar"), m.sem("p1_z_taken_by_vector")
        s_v, s_a = m.sem("p1_vector_chain"), m.sem("p1_scalar_chain")
        s_glu = m.sem("p1_glu")
        block = stack.enter_context(nc.Block())

        def vcol(name, i=0):
            return vec[:, VEC_AT[name] + i:VEC_AT[name] + i + 1]

        def slot_wait(engine, item):
            n = STREAM_AT[item]
            engine.wait_ge(s_slot[n % RING1], 16 * (n // RING1 + 1))

        z_end, total = [], 0
        for _, width in IN_SLICES:
            total += width // P
            z_end.append(total)

        def free_wait(engine, item):
            kind, i = item
            if kind == "ada":
                engine.wait_ge(s_adam, i + 1)
            else:
                engine.wait_ge(s_z, z_end[i])

        def exact(ap):
            return ap.bitcast(F32)

        def pair(buffer, b):
            s, t = Z_TILES[2 * b]
            return buffer[:, STREAM_AT[("in", s)] % RING1, :, t * P:t * P + PAIR]

        def has_gain(i):
            return (i // 2) % 3 > 0

        def gains_to(i):
            return sum(has_gain(j) for j in range(i))

        @block.sync
        def _(sp):
            sp.dma_start(crow[:, :], w["c"][0].rearrange("(r n) -> r n", n=P)).then_inc(s_crow, 16)
            sp.dma_start(wide[0:ADA, :], w["b_ada"][0].rearrange("(r n) -> r n", n=N)).then_inc(s_wide, 16)
            for g, name in enumerate(GAINS):
                sp.dma_start(wide[ADA + 2 * g:ADA + 2 * g + 2, :],
                              w[name][0].rearrange("(r n) -> r n", n=N)).then_inc(s_wide, 16)
            sp.dma_start(x[:, :, :], w["x"][0].rearrange("(t p) d -> p t d", p=P)).then_inc(s_x, 16)
            for n, (kind, i) in enumerate(STREAM):
                if n >= RING1:
                    free_wait(sp, STREAM[n - RING1])
                if kind == "ada":
                    at, width, source = i * N, N, w["w_ada"][0]
                else:
                    (at, width), source = IN_SLICES[i], w["w_in"][0]
                sp.dma_start(ring[:, n % RING1, :, 0:width],
                             source[:, at:at + width].rearrange("(k p) n -> p k n", p=P)).then_inc(
                                 s_slot[n % RING1], 16)

        @block.gpsimd
        def _(pool):
            pool.memset(keep.ident[:, :], 0.0).then_inc(s_const, 1)
            pool.memset(keep.ones[:, :], 1.0).then_inc(s_const, 1)
            pool.memset(keep.power[:, :], -0.5).then_inc(s_const, 1)
            pool.memset(upad[:, :, 0:CK - 1], 0.0).then_inc(s_const, 1)
            pool.wait_ge(s_const, 4)
            pool.affine_select(out=keep.ident[:, :], in_=keep.ident[:, :], compare_op=ALU.not_equal, fill=1.0,
                               base=0, pattern=[[-1, P]], channel_multiplier=1).then_inc(s_const, 1)
            pool.wait_ge(s_sq, 1)
            pool.tensor_tensor(rstd[:, :], mean_sq[:, :], keep.power[:, 0:NT], ALU.pow).then_inc(s_rstd, 1)
            for b in range(len(Z_TILES) // 2):
                pool.wait_ge(s_whi, b + 1)
                pool.tensor_tensor(pair(ring_lo, b), pair(ring, b), exact(w_hi[:, b % 2, :, :]), ALU.subtract).then_inc(s_wlo, 1)

        @block.scalar
        def _(act):
            link = Link(act, s_a)
            for name, count in VEC_ROWS:
                r = VEC_AT[name]
                src = w[name][0]
                if name == "r_k":
                    src = src.rearrange("h d -> (h d)")
                act.dma_start(vrows[r:r + count, :], src.rearrange("(r n) -> r n", n=P)).then_inc(s_vrows, 16)
            act.dma_start(trows[:, :], w["conv_w"][0].rearrange("k (r n) -> (k r) n", n=P)).then_inc(s_vrows, 16)
            act.wait_ge(s_cT, 1)
            act.activation(keep.silu_c[:, :], pg[:, 0:KD], ACT.Sigmoid).then_inc(s_sig, 1)
            act.wait_ge(s_x, 16)
            for t in range(NT):
                sq = act.activation(hT[:, 2 * t:2 * t + 2, :], x[:, t, :].rearrange("p (a b) -> p a b", b=S), ACT.Square, accum_out=sums[:, t:t + 1])
                link.sign(sq)
            link.wait()
            act.activation(mean_sq[:, :], sums[:, :], ACT.Copy, scale=1.0 / D, bias=RMS_EPS).then_inc(s_sq, 1)
            act.wait_ge(s_rstd, 1)
            for t in range(0, NT, 2):
                act.activation(x[:, t, :], x[:, t, :], ACT.Copy, scale=rstd[:, t:t + 1]).then_inc(s_xA, 1)

            def gain_copy(i):
                if has_gain(i):
                    act.wait_ge(s_gain, gains_to(i) + 1)
                    act.activation(keep.mod[:, i * N:i * N + N], pg[:, :], ACT.Copy).then_inc(s_adag, 1)

            for i in range(FIRST):
                gain_copy(i)
                for k in range(2 * i, 2 * i + 2):
                    act.wait_ge(s_ht, k + 1)
                    act.activation(hT[:, k, :], pt[k % 2][:, :], ACT.Copy).then_inc(s_hA, 1)

            def split(b):
                slot_wait(act, ("in", Z_TILES[2 * b][0]))
                if b >= 2:
                    act.wait_ge(s_z, 2 * b - 2)
                act.activation(w_hi[:, b % 2, :, :], pair(ring, b), ACT.Copy).then_inc(s_whi, 1)

            split(0)
            act.wait_ge(s_colV, 1)
            for k in range(KD):
                act.activation(h_hi[:, k, :], hT[:, k, :], ACT.Identity, scale=modcol[:, KD + k:KD + k + 1],
                               bias=modcol[:, k:k + 1]).then_inc(s_hhi, 1)
            split(1)
            act.wait_ge(s_vec, 2)
            for n, (s, t) in enumerate(Z_TILES):
                act.wait_ge(s_z, n + 1)
                z = pz[n % 3]
                kind, i = Z_KINDS[n]
                if kind == "rwkv":
                    act.activation(mix.zr[:, i, :], z[:, :], ACT.Copy,
                                   scale=keep.one_minus_mu[:, i:i + 1]).then_inc(s_zA, 1)
                elif kind == "value":
                    act.activation(upad[:, i, CK - 1:], z[:, :], ACT.Copy).then_inc(s_zA, 1)
                elif kind == "sigmoid":
                    if i >= 2:
                        act.wait_ge(s_glu, i - 1)
                    act.activation(glu[:, i % 2, :], z[:, :], ACT.Sigmoid).then_inc(s_zA, 1)
                else:
                    if i == NZ_GATE - 2:
                        act.wait_ge(s_glu, RT_)
                    act.activation(mix.gates[:, i, :], z[:, :], ACT.Sigmoid).then_inc(s_zA, 1)
                if n % 2 and n // 2 + 2 < len(Z_TILES) // 2:
                    split(n // 2 + 2)
                if t == 3 and 1 <= s <= ADA - 4:
                    gain_copy(s + 3)

        @block.tensor
        def _(pe):
            pe.wait_ge(s_const, 5)
            pe.wait_ge(s_crow, 16)
            pe.transpose(pg[:, 0:KD], crow[:, :], keep.ident[0:KD, 0:KD]).then_inc(s_cT, 1)

            def gain_row(i):
                if has_gain(i):
                    if gains_to(i):
                        pe.wait_ge(s_adag, gains_to(i))
                    row = ADA + 2 * {1: 0, 2: 1, 4: 2, 5: 3}[i // 2] + i % 2
                    pe.matmul(pg[:, :], keep.ident[0:N_WIDE, row:row + 1].to_broadcast([N_WIDE, P]),
                              wide[:, :], start=True, stop=True).then_inc(s_gain, 1)

            def ada_direct(i):
                out = pm[i % 2]
                if i >= 2:
                    pe.wait_ge(s_mod, i - 1)
                if i < FIRST:
                    slot_wait(pe, ("ada", i))
                    slot = STREAM_AT[("ada", i)] % RING1
                    for k in range(DIRECT):
                        pe.matmul(out[:, :], keep.silu_c[:, k:k + 1].to_broadcast([P, P]), ring[:, slot, k, :],
                                  start=(k == 0), stop=False)

            def ada_sum(i):
                out = pm[i % 2]
                pe.wait_ge(s_ada, i + 1)
                pe.matmul(out[:, :], keep.ones[:, :], acc[:, i % 2, :], start=(i >= FIRST), stop=False)
                pe.matmul(out[:, :], keep.ident[0:N_WIDE, i:i + 1].to_broadcast([N_WIDE, P]), wide[:, :],
                          start=False, stop=True).then_inc(s_adam, 1)

            def mod_columns(i):
                pe.wait_ge(s_mod, i + 1)
                for j in range(i * N // P, (i + 1) * N // P):
                    last = pe.matmul(pt[1][:, j:j + 1], keep.mod[0:1, j * P:(j + 1) * P], keep.ones[0:1, 0:1],
                                     start=True, stop=True)
                last.then_inc(s_col, 1)

            pe.wait_ge(s_silu, 1)
            pe.wait_ge(s_wide, 16 * (1 + len(GAINS)))
            gain_row(2)
            ada_direct(0)
            pe.wait_ge(s_xA, NT // 2)
            pe.wait_ge(s_xV, NT // 2)
            for k in range(KD):
                if k >= 2:
                    pe.wait_ge(s_hA, k - 1)
                for t in range(NT):
                    last = pe.transpose(pt[k % 2][:, t * P:(t + 1) * P], x[:, t, k * P:(k + 1) * P], keep.ident[:, :])
                last.then_inc(s_ht, 1)
            ada_sum(0)
            gain_row(3)
            ada_direct(1)
            ada_sum(1)
            pe.wait_ge(s_hA, KD)
            mod_columns(0)
            pe.wait_ge(s_vrows, 16 * (len(VEC_ROWS) + 1))
            pe.transpose(pt[0][:, 0:N_VEC], vrows[:, :], keep.ident[0:N_VEC, 0:N_VEC])
            pe.transpose(pt[0][:, P:P + N_TAP], trows[:, :], keep.ident[0:N_TAP, 0:N_TAP]).then_inc(s_vecT, 1)
            mod_columns(1)
            for i in (2, 3):
                ada_direct(i)
                ada_sum(i)
            mod_columns(2)
            mod_columns(3)
            for n, (s, t) in enumerate(Z_TILES):
                if t == 0:
                    slot_wait(pe, ("in", s))
                if n >= 3:
                    pe.wait_ge(s_zA, n - 2)
                    kind, i = Z_KINDS[n - 3]
                    if kind == "rwkv":
                        pe.wait_ge(s_zV, i + 1)
                pe.wait_ge(s_wlo, n // 2 + 1)
                w_lo = pair(ring_lo, n // 2)
                cs = slice(n % 2 * P, n % 2 * P + P)
                for k in range(KD):
                    if n == 0:
                        pe.wait_ge(s_hhi, k + 1)
                        pe.wait_ge(s_hlo, k + 1)
                    for i, (weights, h) in enumerate(((w_hi[:, n // 2 % 2, k, cs], h_hi), (w_hi[:, n // 2 % 2, k, cs], h_lo),
                                                      (w_lo[:, k, cs], h_hi))):
                        last = pe.matmul(pz[n % 3][:, :], weights, h[:, k, :],
                                         start=(k == 0 and i == 0), stop=(k == KD - 1 and i == 2))
                last.then_inc(s_z, 1)
                if t == 3 and 1 <= s <= ADA - 4:
                    gain_row(s + 3)
                    ada_direct(s + 3)
                    ada_sum(s + 3)

        @block.vector
        def _(dve):
            link = Link(dve, s_v)
            dve.wait_ge(s_sig, 1)
            nc.vector.tensor_tensor(keep.silu_c[:, :], keep.silu_c[:, :], pg[:, 0:KD], ALU.mult).then_inc(s_silu, 1)
            dve.wait_ge(s_rstd, 1)
            for t in range(1, NT, 2):
                nc.vector.tensor_scalar(x[:, t, :], x[:, t, :], rstd[:, t:t + 1], None, ALU.mult).then_inc(s_xV, 1)
            dve.wait_ge(s_silu, 1)

            def ada_partial(i):
                slot_wait(dve, ("ada", i))
                if i >= 2:
                    dve.wait_ge(s_adam, i - 1)
                slot = STREAM_AT[("ada", i)] % RING1
                first = DIRECT if i < FIRST else 0
                for k in range(first, KD):
                    c_k = keep.silu_c[:, k:k + 1]
                    if k == first:
                        last = nc.vector.tensor_scalar(acc[:, i % 2, :], ring[:, slot, k, :], c_k, None, ALU.mult)
                    else:
                        last = nc.vector.scalar_tensor_tensor(out=acc[:, i % 2, :], in0=ring[:, slot, k, :], scalar=c_k,
                                                              in1=acc[:, i % 2, :], op0=ALU.mult, op1=ALU.add)
                    if k < KD - 1:
                        link(last)
                last.then_inc(s_ada, 1)

            def mod_row(i):
                dve.wait_ge(s_adam, i + 1)
                row = keep.mod[:, i * N:i * N + N]
                kind = (i // 2) % 3
                if kind == 0:
                    nc.vector.tensor_copy(row, pm[i % 2][:, :]).then_inc(s_mod, 1)
                    return
                dve.wait_ge(s_adag, gains_to(i) + 1)
                nc.vector.scalar_tensor_tensor(out=row, in0=pm[i % 2][:, :], scalar=1.0 if kind == 1 else 0.0, in1=row,
                                               op0=ALU.add, op1=ALU.mult).then_inc(s_mod, 1)

            for i in range(FIRST):
                ada_partial(i)
                if i:
                    mod_row(i - 1)
            dve.wait_ge(s_vecT, 1)
            nc.vector.tensor_copy(taps[:, :], pt[0][:, P:P + N_TAP])
            nc.vector.tensor_copy(vec[:, :], pt[0][:, 0:N_VEC]).then_inc(s_vec, 1)
            dve.wait_ge(s_vec, 1)
            nc.vector.tensor_scalar(keep.one_minus_mu[:, :], vec[:, 0:NZ_RWKV], -1.0, 1.0, ALU.mult,
                                    ALU.add).then_inc(s_vec, 1)
            mod_row(FIRST - 1)
            dve.wait_ge(s_col, FIRST)
            nc.vector.tensor_copy(modcol[:, :], pt[1][:, 0:2 * KD]).then_inc(s_colV, 1)
            dve.wait_ge(s_colV, 1)
            dve.wait_ge(s_hA, KD)
            for k in range(KD):
                dve.wait_ge(s_hhi, k + 1)
                nc.vector.tensor_scalar(hT[:, k, :], hT[:, k, :], modcol[:, KD + k:KD + k + 1], modcol[:, k:k + 1],
                                        ALU.mult, ALU.add).then_inc(s_mod_h, 1)
                dve.wait_ge(s_mod_h, k + 1)
                nc.vector.tensor_tensor(h_lo[:, k, :], hT[:, k, :], exact(h_hi[:, k, :]), ALU.subtract).then_inc(s_hlo, 1)

            def conv_taps(first, end):
                for product in range(first, end):
                    k, r = product // RT_, product % RT_
                    tap = taps[:, k * RT_ + r:k * RT_ + r + 1]
                    u = upad[:, r, k:k + S]
                    if k == 0:
                        done[r] = link.sign(nc.vector.tensor_scalar(mix.co[:, r, :], u, tap, vcol("conv_b", r),
                                                                    ALU.mult, ALU.add))
                    else:
                        link.wait(done[r])
                        done[r] = link.sign(nc.vector.scalar_tensor_tensor(
                            out=mix.co[:, r, :], in0=u, scalar=tap, in1=mix.co[:, r, :], op0=ALU.mult, op1=ALU.add))

            done, made = {}, 0
            for n, (s, t) in enumerate(Z_TILES):
                kind, i = Z_KINDS[n]
                dve.wait_ge(s_zA, n + 1)
                if kind == "rwkv":
                    nc.vector.scalar_tensor_tensor(out=mix.zr[:, i, 1:], in0=pz[n % 3][:, 0:S - 1], scalar=vec[:, i:i + 1],
                                                   in1=mix.zr[:, i, 1:], op0=ALU.mult, op1=ALU.add).then_inc(s_zV, 1)
                elif kind == "sigmoid":
                    nc.vector.tensor_tensor(upad[:, i, CK - 1:], upad[:, i, CK - 1:], glu[:, i % 2, :],
                                            ALU.mult).then_inc(s_glu, 1)
                if t == 0 and 1 <= s <= ADA - 4:
                    ada_partial(s + 3)
                elif t == 3 and 1 <= s <= ADA - 4:
                    mod_row(s + 3)
                if n + 1 == NZ_CONV:
                    dve.wait_ge(s_const, 5)
                    dve.wait_ge(s_glu, RT_)
                elif n + 1 > NZ_CONV and t:
                    conv_taps(made, min(TAPS, made + TAPS_A_TILE))
                    made = min(TAPS, made + TAPS_A_TILE)
            assert made == TAPS


def rwkv(nc, w, keep, mix):
    with ExitStack() as stack:
        m = Memory(nc, stack)
        T4 = [P, RT_, S]
        cum, sg, aB, A = m.sb("cum", T4), m.sb("sg", T4), m.sb("aB", T4), m.sb("A_T", T4)
        reset = m.sb("reset", [P, S])
        loras = m.sb("loras", [P, RW])
        g2 = m.sb("g2", [P, RW])
        headones = m.sb("headones", [P, P])
        ka1 = m.sb("one_minus_ka", [P, RT_])
        mid = m.sb("mid", [P, RT_, NT])
        last = m.sb("last", [P, RT_, NT])
        mid_e = m.sb("mid_e", [P, RT_, NT])
        hop = m.sb("hop", [P, RT_, NT])
        LV = 7
        masks = m.sb("level_masks", [P, LV, P])
        low1 = m.sb("low1", [P, P])
        tri = m.sb("tri", [P, 2, P])
        col_i, row_i = m.sb("col_i", [P, P], I32), m.sb("row_i", [P, P], I32)
        colf, rowf, xorf, ge = m.sb("colf", [P, P]), m.sb("rowf", [P, P]), m.sb("xorf", [P, 2, P]), m.sb("ge", [P, 2, P])
        tok = m.sb("tok", [P, 2, 3, RW])
        AB = m.sb("AB", [P, HEADS, 2 * P])
        AK = m.sb("AK", [P, HEADS, 2 * P])
        factor, ep = (ap[:, :, :].rearrange("p (r h) t -> p r (h t)", r=RT_) for ap in (AB, AK))
        X, XT = m.sb("X", [P, HEADS, P]), m.sb("XT", [P, HEADS, P])
        Z = sg[:, :, :].rearrange("p (b a) (h t) -> p b (a h) t", b=2, t=P)
        TM = cum[:, :, :].rearrange("p (b a) (h t) -> p b (a h) t", b=2, t=P)
        G, U = m.sb("G", [P, 2, RT_, HD]), m.sb("U", [P, RT_, 2, HD])
        M = m.sb("M", [P, RT_, HD])
        co, conv_tmp = mix.co, m.sb("conv_tmp", [P, RT_, S])
        conv_stat = loras
        bank = [m.bank(f"b{i}") for i in range(8)]
        zr, vec, gate_r, bonus = mix.zr, keep.vec, mix.gate_r, mix.bonus
        r_, k_, v_ = zr[:, 0:4, :], zr[:, 4:8, :], zr[:, 8:12, :]

        s_w = m.sem("p2_weights_in")
        s_io = m.sem("p2_iotas")
        s_mask = m.sem("p2_masks")
        s_act = m.sem("p2_lora_activated")
        s_lora = m.sem("p2_lora_products")
        s_loraA = m.sem("p2_lora_taken")
        s_kk = m.sem("p2_kk")
        s_kksq = m.sem("p2_kk_squared")
        s_kksum = m.sem("p2_kk_sums")
        s_kkmax, s_kkroot = m.sem("p2_kk_max"), m.sem("p2_kk_inverse_norm")
        s_rk = m.sem("p2_rk")
        s_rksum = m.sem("p2_rk_sums")
        s_bonus = m.sem("p2_bonus")
        s_cc = m.sem("p2_centred")
        s_e1, s_e2, s_e3 = m.sem("p2_exp_plus"), m.sem("p2_exp_minus"), m.sem("p2_exp_before")
        s_kop = m.sem("p2_k_and_b_operands")
        s_cm, s_cmV, s_cd, s_csq = (m.sem(f"p2_conv_{n}") for n in ("sums", "mean", "centred", "squared"))
        s_cvar, s_cvarV, s_croot = (m.sem(f"p2_conv_{n}") for n in ("square_sums", "variance", "inverse_root"))
        s_cn, s_csig = m.sem("p2_conv_normed"), m.sem("p2_conv_sigmoid")
        s_mid = m.sem("p2_mid_exp")
        s_v, s_a, s_g = m.sem("p2_vector_chain"), m.sem("p2_scalar_chain"), m.sem("p2_pool_chain")
        s_tokp, s_tok = m.sem("p2_tok_turned"), m.sem("p2_tok_ready")
        s_pair, s_pairV = m.sem("p2_pair_products"), m.sem("p2_pair_masked")
        s_x2, s_x2p = m.sem("p2_x_start"), m.sem("p2_xt_start")
        s_tm = m.sem("p2_level_T")
        s_z, s_zA = m.sem("p2_Z"), m.sem("p2_Z_taken")
        s_xz, s_xV, s_xzV = m.sem("p2_XZ"), m.sem("p2_X_added"), m.sem("p2_XT_added")
        s_G, s_GA = m.sem("p2_G"), m.sem("p2_G_taken")
        s_U, s_UV = m.sem("p2_U"), m.sem("p2_U_taken")
        s_M, s_MV = m.sem("p2_M"), m.sem("p2_M_taken")
        s_Y, s_YA = m.sem("p2_Y"), m.sem("p2_Y_taken")
        block = stack.enter_context(nc.Block())
        STEPS = LV - 1
        LAST_C = NT - 1

        def vcol(name, i=0):
            return vec[:, VEC_AT[name] + i:VEC_AT[name] + i + 1]

        def wide(ap, shape):
            return ap.to_broadcast(shape)

        def unit(u):
            g, q = u // 2, u % 2
            return slice(4 * g + q, 4 * g + q + 3, 2), q

        TM_COUNT = 4 + STEPS - 1

        def at(h):
            return h // 2, slice(HD * (h % 2), HD * (h % 2) + HD)

        @block.sync
        def _(sp):
            sp.dma_start(loras[0:LORA_W, :], w["w2"][0]).then_inc(s_w, 16)
            sp.dma_start(loras[LORA_W:P, :], w["a2"][0]).then_inc(s_w, 16)
            sp.dma_start(g2[:, :], w["g2"][0]).then_inc(s_w, 16)

        @block.gpsimd
        def _(pool):
            link = Link(pool, s_g)
            link.sign(pool.memset(headones[:, :], 0.0))
            link.sign(pool.memset(reset[:, :], 1.0))
            pool.iota(col_i[:, :], [[1, P]], base=0, channel_multiplier=0).then_inc(s_io, 1)
            pool.iota(row_i[:, :], [[0, P]], base=0, channel_multiplier=1).then_inc(s_io, 1)
            link.wait()
            for q in range(2):
                pool.wait_ge(s_io, 2 + q)
                pool.memset(headones[HD * q:HD * q + HD, HD * q:HD * q + HD], 1.0).then_inc(s_io, 1)
            pool.wait_ge(s_io, 4)
            pool.memset(reset[:, :].rearrange("p (c t) -> p c t", c=NT)[:, :, 0:1], 0.0).then_inc(s_io, 1)
            pool.wait_ge(s_rk, RT_)
            for r in range(RT_):
                pool.wait_ge(s_e2, r + 1)
                for operand in (k_, aB):
                    pool.tensor_tensor(operand[:, r, :], operand[:, r, :], cum[:, r, :], ALU.mult).then_inc(s_kop, 1)
            pool.wait_ge(s_mask, 1)
            pool.wait_ge(s_kop, 2 * RT_)
            for c in range(NT):
                for u in range(4):
                    heads, _ = unit(u)
                    if c:
                        pool.wait_ge(s_z, 2 * (c * STEPS - 1))
                    pool.wait_ge(s_pairV, 4 * c + u + 1)
                    pool.tensor_tensor(TM[:, (c * STEPS) % 2, heads, :], AB[:, heads, 0:P], wide(masks[:, 1:2, :], [P, 2, P]),
                                       ALU.mult).then_inc(s_tm, 1)
                for lv in range(1, STEPS):
                    n = c * STEPS + lv
                    if n >= 2:
                        pool.wait_ge(s_z, 2 * (n - 1))
                    pool.tensor_tensor(TM[:, n % 2, :, :], AB[:, :, 0:P], wide(masks[:, lv + 1:lv + 2, :], [P, HEADS, P]),
                                       ALU.mult).then_inc(s_tm, 1)

        @block.scalar
        def _(act):
            link = Link(act, s_a)
            act.activation(zr[0:LORA_W, 12, :], zr[0:LORA_W, 12, :], ACT.Tanh).then_inc(s_act, 1)
            act.activation(zr[:, 13, :], zr[:, 13, :], ACT.Sigmoid).then_inc(s_act, 1)
            for j, (dst, bias) in enumerate(((sg, "w0"), (aB, "a0"), (gate_r, None))):
                for r in range(RT_):
                    act.wait_ge(s_lora, RT_ * j + r + 1)
                    if bias:
                        act.activation(dst[:, r, :], bank[r][:, :], ACT.Sigmoid, bias=vcol(bias, r)).then_inc(s_loraA, 1)
                    else:
                        act.activation(dst[:, r, :], bank[r][:, :], ACT.Copy).then_inc(s_loraA, 1)
                if j == 0:
                    for r in range(RT_):
                        act.wait_ge(s_kk, r + 1)
                        act.activation(bonus[:, r, :], A[:, r, :], ACT.Square).then_inc(s_kksq, 1)
            for r in range(RT_):
                act.wait_ge(s_kkmax, r + 1)
                link.sign(act.activation(bonus[:, r, :], bonus[:, r, :], ACT.Ln))
            for r in range(RT_):
                link.wait(r + 1)
                act.activation(bonus[:, r, :], bonus[:, r, :], ACT.Exp, scale=-0.5).then_inc(s_kkroot, 1)
            for r in range(RT_):
                act.wait_ge(s_cc, r + 1)
                if r == 0:
                    act.activation(mid_e[:, :, :], mid[:, :, :], ACT.Exp, scale=-DECAY).then_inc(s_mid, 1)
                act.activation(ep[:, r, :], cum[:, r, :], ACT.Exp, scale=-DECAY).then_inc(s_e1, 1)
                act.activation(sg[:, r, :], sg[:, r, :], ACT.Exp, scale=-DECAY).then_inc(s_e3, 1)
                act.wait_ge(s_e1, r + 1)
                act.activation(cum[:, r, :], cum[:, r, :], ACT.Exp, scale=DECAY).then_inc(s_e2, 1)

            def tokens(c, i):
                act.wait_ge(s_tokp, 3 * c + i + 1)
                if c >= 2:
                    act.wait_ge(s_Y, c - 1)
                act.activation(tok[:, c % 2, i, :], bank[(6, 7, 6)[i]][:, :], ACT.Copy).then_inc(s_tok, 1)

            def conv_root():
                act.wait_ge(s_cvarV, 1)
                count = link.sign(act.activation(conv_stat[:, :], conv_stat[:, :], ACT.Ln))
                link.wait(count)
                act.activation(conv_stat[:, :], conv_stat[:, :], ACT.Exp, scale=-0.5).then_inc(s_croot, 1)

            for i in range(3):
                tokens(0, i)
            for c in range(NT):
                for lv in range(STEPS):
                    for g in range(2):
                        n = (c * STEPS + lv) * 2 + g
                        act.wait_ge(s_z, n + 1)
                        if n >= 2:
                            act.wait_ge(s_xz, n - 1)
                        act.activation(Z[:, lv % 2, 4 * g:4 * g + 4, :], bank[g][:, :].rearrange("p (h t) -> p h t", h=4),
                                       ACT.Copy).then_inc(s_zA, 1)
                        if lv == 0 and g == 0:
                            act.wait_ge(s_G, c + 1)
                            if c:
                                act.wait_ge(s_U, c)
                            if c == 1:
                                conv_root()
                            for q in range(2):
                                act.activation(G[:, q, :, :], bank[6 + q][:, 0:RT_ * HD].rearrange("p (r v) -> p r v", r=RT_),
                                               ACT.Copy).then_inc(s_GA, 1)
                    if c == 0 and 1 <= lv <= RT_:
                        act.wait_ge(s_cd, lv)
                        act.activation(conv_tmp[:, lv - 1, :], co[:, lv - 1, :], ACT.Square).then_inc(s_csq, 1)
                    elif c == 2 and lv < RT_:
                        act.wait_ge(s_cn, lv + 1)
                        act.wait_ge(s_cvar, 1)
                        act.activation(conv_tmp[:, lv, :], co[:, lv, :], ACT.Sigmoid, bias=vcol("conv_ln_b", lv),
                                       scale=vcol("conv_ln_g", lv)).then_inc(s_csig, 1)
                if c < LAST_C:
                    for i in range(2):
                        tokens(c + 1, i)
                act.wait_ge(s_Y, c + 1)
                for q in range(2):
                    act.activation(zr[HD * q:HD * q + HD, 0:4, c * P:(c + 1) * P],
                                   bank[2 + q][HD * q:HD * q + HD, :].rearrange("p (r t) -> p r t", r=RT_),
                                   ACT.Copy).then_inc(s_YA, 1)
                if c < LAST_C:
                    tokens(c + 1, 2)

        @block.tensor
        def _(pe):
            pe.wait_ge(s_w, 48)
            pe.wait_ge(s_act, 2)
            for j, (weights, inputs) in enumerate(((loras[0:LORA_W, :], zr[0:LORA_W, 12, :]), (loras[LORA_W:P, :], zr[LORA_W:P, 12, :]),
                                                   (g2[:, :], zr[:, 13, :]))):
                for r in range(RT_):
                    if j:
                        pe.wait_ge(s_loraA, RT_ * (j - 1) + r + 1)
                    pe.matmul(bank[r][:, :], weights[:, r * P:(r + 1) * P], inputs, start=True, stop=True).then_inc(s_lora, 1)
                if j == 0:
                    pe.wait_ge(s_io, 5)
                    for r in range(RT_):
                        pe.wait_ge(s_kksq, r + 1)
                        pe.matmul(bank[4 + r][:, :], headones[:, :], bonus[:, r, :], start=True, stop=True).then_inc(s_kksum, 1)
            pe.wait_ge(s_kkmax, RT_)
            for r in range(RT_):
                pe.wait_ge(s_rk, r + 1)
                pe.matmul(bank[4 + r][:, :], headones[:, :], bonus[:, r, :], start=True, stop=True).then_inc(s_rksum, 1)
            pe.wait_ge(s_loraA, 2 * RT_ + 1)
            for r in range(RT_):
                mm = pe.matmul(bank[0][:, :], keep.ones[:, :], co[:, r, :], start=(r == 0), stop=(r == RT_ - 1))
            mm.then_inc(s_cm, 1)
            pe.wait_ge(s_bonus, RT_)
            pe.wait_ge(s_kop, 2 * RT_)

            def turn(c, i):
                if c and i == 0:
                    pe.wait_ge(s_GA, 2 * c)
                if i == 2:
                    pe.wait_ge(s_tok, 3 * c + 1)
                for r in range(RT_):
                    mm = pe.transpose(bank[(6, 7, 6)[i]][:, r * P:(r + 1) * P], (aB, k_, v_)[i][:, r, c * P:(c + 1) * P],
                                      keep.ident[:, :])
                mm.then_inc(s_tokp, 1)

            def start_values(c):
                pe.wait_ge(s_tok, 3 * c + 3)
                pe.wait_ge(s_pairV, 4 * c + 4)
                if c:
                    pe.wait_ge(s_MV, c)
                for h in range(HEADS):
                    r, ps = at(h)
                    dst = bank[6 + h % 2][:, r * HD:(r + 1) * HD]
                    if c:
                        pe.matmul(dst, A[ps, r, c * P:(c + 1) * P], M[ps, r, :], start=True, stop=False)
                    mm = pe.matmul(dst, AK[:, h, 0:P], tok[:, c % 2, 2, h * HD:(h + 1) * HD], start=(c == 0), stop=True)
                mm.then_inc(s_G, 1)

            for i in range(3):
                turn(0, i)
            for c in range(NT):
                ts = slice(c * P, (c + 1) * P)
                B_tok, K_tok, V_tok = (tok[:, c % 2, i, :] for i in range(3))
                for u in range(4):
                    _, q = unit(u)
                    if u == 0 and c < 2:
                        pe.wait_ge((s_cmV, s_cvarV)[c], 1)
                    if u >= 2:
                        pe.wait_ge(s_pairV, 4 * c + u - 1)
                        pe.wait_ge(s_x2, 4 * c + u - 1)
                    elif c:
                        pe.wait_ge(s_YA, 2 * c - 1 + q)
                        if q == 0:
                            pe.wait_ge(s_UV, c)
                        else:
                            pe.wait_ge(s_MV, c)
                    for j in range(2):
                        r, ps = at(4 * (u // 2) + 2 * j + q)
                        for dst, lhs in ((bank[q], aB), (bank[2 + q], k_)):
                            pe.matmul(dst[:, j * 2 * P:j * 2 * P + P], lhs[ps, r, ts], A[ps, r, ts], start=True, stop=True)
                            pe.matmul(dst[:, j * 2 * P + P:(j + 1) * 2 * P], lhs[ps, r, ts], r_[ps, r, ts],
                                      start=True, stop=True)
                        mm = pe.matmul(bank[4 + q][:, j * P:(j + 1) * P], A[ps, r, ts], aB[ps, r, ts], start=True, stop=True)
                    mm.then_inc(s_pair, 1)
                for lv in range(STEPS):
                    n = c * STEPS + lv
                    for g in range(2):
                        if lv:
                            pe.wait_ge(s_tm, TM_COUNT * c + 4 + lv)
                            pe.wait_ge(s_xV, 2 * (c * (STEPS - 1) + lv - 1) + g + 1)
                        else:
                            pe.wait_ge(s_tm, TM_COUNT * c + 2 * g + 2)
                            pe.wait_ge(s_x2, 4 * c + 2 * g + 2)
                            pe.wait_ge(s_pairV, 4 * c + 3 + g)
                        for h in range(4 * g, 4 * g + 4):
                            cs = slice((h % 4) * P, (h % 4 + 1) * P)
                            mm = pe.matmul(bank[g][:, cs], TM[:, n % 2, h, :], X[:, h, :], start=True, stop=True)
                        mm.then_inc(s_z, 1)
                        if lv == 0 and g == 0:
                            start_values(c)
                    for g in range(2):
                        pe.wait_ge(s_zA, 2 * n + g + 1)
                        if lv:
                            pe.wait_ge(s_xzV, 2 * (n - 1) + g + 1)
                        if lv == 0:
                            pe.wait_ge(s_x2, 4 * c + 3 + g)
                            pe.wait_ge(s_x2p, 4 * c + 2 * g + 2)
                        for h in range(4 * g, 4 * g + 4):
                            cs = slice((h % 4) * P, (h % 4 + 1) * P)
                            if lv < STEPS - 1:
                                pe.matmul(bank[2 + g][:, cs], XT[:, h, :], Z[:, lv % 2, h, :], start=True, stop=True)
                            mm = pe.matmul(bank[4 + g][:, cs], Z[:, lv % 2, h, :], XT[:, h, :], start=True, stop=True)
                        mm.then_inc(s_xz, 1)
                pe.wait_ge(s_xzV, 2 * STEPS * (c + 1))
                pe.wait_ge(s_GA, 2 * c + 2)
                for h in range(HEADS):
                    mm = pe.matmul(bank[4][:, h * HD:(h + 1) * HD], XT[:, h, :], G[:, h % 2, h // 2, :], start=True, stop=True)
                mm.then_inc(s_U, 1)
                if c < LAST_C:
                    turn(c + 1, 0)
                    turn(c + 1, 1)
                pe.wait_ge(s_UV, c + 1)
                if c < LAST_C:
                    for r in range(RT_):
                        cs = slice(r * P, (r + 1) * P)
                        pe.matmul(bank[5][:, cs], B_tok[:, cs], U[:, r, :, :].rearrange("p q v -> p (q v)"), start=True, stop=False)
                        mm = pe.matmul(bank[5][:, cs], K_tok[:, cs], V_tok[:, cs], start=False, stop=True)
                    mm.then_inc(s_M, 1)
                for h in range(HEADS):
                    r, ps = at(h)
                    dst = bank[2 + h % 2][ps, r * P:(r + 1) * P]
                    if c:
                        pe.matmul(dst, M[ps, r, :], r_[ps, r, ts], start=True, stop=False)
                    pe.matmul(dst, U[:, r, h % 2, :], AB[:, h, P:2 * P], start=(c == 0), stop=False)
                    mm = pe.matmul(dst, V_tok[:, h * HD:(h + 1) * HD], AK[:, h, P:2 * P], start=False, stop=True)
                mm.then_inc(s_Y, 1)
                if c == 0:
                    pe.wait_ge(s_csq, RT_)
                    for r in range(RT_):
                        mm = pe.matmul(bank[0][:, :], keep.ones[:, :], conv_tmp[:, r, :], start=(r == 0), stop=(r == RT_ - 1))
                    mm.then_inc(s_cvar, 1)
                if c < LAST_C:
                    turn(c + 1, 2)

        @block.vector
        def _(dve):
            link = Link(dve, s_v)
            V = nc.vector
            for r in range(RT_):
                V.tensor_scalar(A[:, r, :], k_[:, r, :], vcol("k_k", r), None, ALU.mult).then_inc(s_kk, 1)
            dve.wait_ge(s_io, 2)
            a = link.sign(V.tensor_copy(colf[:, :], col_i[:, :]))
            b = link.sign(V.tensor_copy(rowf[:, :], row_i[:, :]))
            link(V.tensor_tensor(col_i[:, :], col_i[:, :], row_i[:, :], ALU.bitwise_xor))
            link(V.tensor_copy(xorf[:, 0, :], col_i[:, :]))
            link.sign(V.tensor_tensor(tri[:, 1, :], colf[:, :], rowf[:, :], ALU.is_ge))
            link.sign(V.tensor_tensor(ge[:, 0, :], colf[:, :], rowf[:, :], ALU.is_lt))
            link(V.tensor_tensor(tri[:, 0, :], colf[:, :], rowf[:, :], ALU.is_gt))
            link.sign(V.tensor_tensor(xorf[:, 1, :], xorf[:, 0, :], ge[:, 0, :], ALU.mult))
            link(V.tensor_tensor(xorf[:, 0, :], xorf[:, 0, :], tri[:, 0, :], ALU.mult))
            link.sign(V.tensor_scalar(low1[:, :], xorf[:, 1, :], 1.0, None, ALU.is_equal))
            for lv in range(LV):
                link(V.tensor_scalar(ge[:, 0, :], xorf[:, 0, :], float(2 ** lv), None, ALU.is_ge))
                link(V.tensor_scalar(ge[:, 1, :], xorf[:, 0, :], float(2 ** (lv + 1)), None, ALU.is_lt))
                link(V.tensor_tensor(masks[:, lv, :], ge[:, 0, :], ge[:, 1, :], ALU.mult))
            V.tensor_scalar(ka1[:, :], vec[:, VEC_AT["k_a"]:VEC_AT["k_a"] + RT_], -1.0, 1.0, ALU.mult,
                            ALU.add).then_inc(s_mask, 1)
            dve.wait_ge(s_io, 5)
            done = []
            for r in range(RT_):
                dve.wait_ge(s_loraA, r + 1)
                done.append(link.sign(V.tensor_tensor_scan(cum[:, r, :], reset[:, :], sg[:, r, :], 0.0, ALU.mult, ALU.add)))
            for r in range(RT_):
                link.wait(done[r])
                done[r] = link.sign(V.tensor_copy(mid[:, r, :], cum[:, r, P // 2 - 1::P]))
            for r in range(RT_):
                link.wait(done[r])
                chunks = cum[:, r, :].rearrange("p (c t) -> p c t", c=NT)
                done[r] = link.sign(V.tensor_tensor(chunks, chunks, wide(mid[:, r, :].unsqueeze(2), [P, NT, P]), ALU.subtract))
            for r in range(RT_):
                link.wait(done[r])
                V.tensor_tensor(sg[:, r, :], cum[:, r, :], sg[:, r, :], ALU.subtract).then_inc(s_cc, 1)
            for r in range(RT_):
                dve.wait_ge(s_kksum, r + 1)
                V.tensor_scalar(bonus[:, r, :], bank[4 + r][:, :], 1e-24, None, ALU.max).then_inc(s_kkmax, 1)
            dve.wait_ge(s_mask, 1)
            for r in range(RT_):
                dve.wait_ge(s_loraA, RT_ + r + 1)
                done[r] = link.sign(V.tensor_scalar(factor[:, r, :], aB[:, r, :], vcol("k_a", r), ka1[:, r:r + 1], ALU.mult, ALU.add))
            for r in range(RT_):
                link.wait(done[r])
                dve.wait_ge(s_kk, r + 1)
                done[r] = link.sign(V.tensor_tensor(k_[:, r, :], k_[:, r, :], factor[:, r, :], ALU.mult))
            for r in range(RT_):
                dve.wait_ge(s_kkroot, r + 1)
                done[r] = link.sign(V.tensor_tensor(A[:, r, :], A[:, r, :], bonus[:, r, :], ALU.mult))
            for r in range(RT_):
                link.wait(done[r])
                done[r] = link.sign(V.tensor_tensor(aB[:, r, :], aB[:, r, :], A[:, r, :], ALU.mult))
            for r in range(RT_):
                link.wait(done[r])
                V.scalar_tensor_tensor(out=bonus[:, r, :], in0=k_[:, r, :], scalar=vcol("r_k", r), in1=r_[:, r, :],
                                       op0=ALU.mult, op1=ALU.mult).then_inc(s_rk, 1)
            link.wait()
            dve.wait_ge(s_rk, RT_)
            for r in range(RT_):
                dve.wait_ge(s_e1, r + 1)
                link.sign(V.tensor_tensor(r_[:, r, :], r_[:, r, :], ep[:, r, :], ALU.mult))
                link.sign(V.tensor_copy(last[:, r, :], ep[:, r, P - 1::P]))
                dve.wait_ge(s_e3, r + 1)
                link.sign(V.scalar_tensor_tensor(out=A[:, r, :], in0=A[:, r, :], scalar=-1.0, in1=sg[:, r, :], op0=ALU.mult,
                                                 op1=ALU.mult))
                dve.wait_ge(s_rksum, r + 1)
                V.tensor_tensor(bonus[:, r, :], bank[4 + r][:, :], v_[:, r, :], ALU.mult).then_inc(s_bonus, 1)
            link.wait()
            dve.wait_ge(s_cm, 1)
            V.tensor_scalar(conv_stat[:, :], bank[0][:, :], 1.0 / CW, None, ALU.mult).then_inc(s_cmV, 1)
            dve.wait_ge(s_mid, 1)
            link(V.tensor_tensor(hop[:, :, 0:NT - 1], last[:, :, 0:NT - 1], mid_e[:, :, 1:NT], ALU.mult))
            for c in range(NT):
                for u in range(4):
                    heads, q = unit(u)
                    dve.wait_ge(s_pair, 4 * c + u + 1)
                    if c and u == 0:
                        dve.wait_ge(s_Y, c)
                    m2 = wide(tri[:, :, :].rearrange("p a t -> p (a t)").unsqueeze(1), [P, 2, 2 * P])
                    products = bank[q][:, :].rearrange("p (h t) -> p h t", h=2)
                    V.tensor_tensor(AB[:, heads, :], products, m2, ALU.mult)
                    first = link.sign(V.tensor_tensor(X[:, heads, :], bank[4 + q][:, 0:2 * P].rearrange("p (h t) -> p h t", h=2),
                                                      wide(low1[:, :].unsqueeze(1), [P, 2, P]), ALU.mult))
                    second = link.sign(V.tensor_tensor(XT[:, heads, :], products[:, :, 0:P], wide(masks[:, 0:1, :], [P, 2, P]),
                                                       ALU.mult))
                    V.tensor_tensor(AK[:, heads, :], bank[2 + q][:, :].rearrange("p (h t) -> p h t", h=2),
                                    m2, ALU.mult).then_inc(s_pairV, 1)
                    one = wide(keep.ident[:, :].unsqueeze(1), [P, 2, P])
                    link.wait(first)
                    V.tensor_tensor(X[:, heads, :], X[:, heads, :], one, ALU.add).then_inc(s_x2, 1)
                    link.wait(second)
                    V.tensor_tensor(XT[:, heads, :], XT[:, heads, :], one, ALU.add).then_inc(s_x2p, 1)
                for lv in range(STEPS):
                    for g in range(2):
                        n = (c * STEPS + lv) * 2 + g
                        dve.wait_ge(s_xz, n + 1)
                        if lv == 0:
                            dve.wait_ge(s_x2p, 4 * c + 4)
                            dve.wait_ge(s_x2, 4 * c + 4)
                        if n >= 2:
                            dve.wait_ge(s_xzV, n - 1)
                        hs = slice(4 * g, 4 * g + 4)
                        if lv < STEPS - 1:
                            V.tensor_tensor(X[:, hs, :], X[:, hs, :], bank[2 + g][:, :].rearrange("p (h t) -> p h t", h=4),
                                            ALU.add).then_inc(s_xV, 1)
                        V.tensor_tensor(XT[:, hs, :], XT[:, hs, :], bank[4 + g][:, :].rearrange("p (h t) -> p h t", h=4),
                                        ALU.add).then_inc(s_xzV, 1)
                    if c == 0 and lv < RT_:
                        dve.wait_ge(s_cmV, 1)
                        V.tensor_tensor(co[:, lv, :], co[:, lv, :], conv_stat[:, :], ALU.subtract).then_inc(s_cd, 1)
                    elif c == 1 and 1 <= lv <= RT_:
                        dve.wait_ge(s_croot, 1)
                        V.scalar_tensor_tensor(out=co[:, lv - 1, :], in0=co[:, lv - 1, :], scalar=CW ** 0.5, in1=conv_stat[:, :],
                                               op0=ALU.mult, op1=ALU.mult).then_inc(s_cn, 1)
                    elif c == 2 and 1 <= lv <= RT_:
                        r = lv - 1
                        dve.wait_ge(s_csig, r + 1)
                        link(V.tensor_scalar(co[:, r, :], co[:, r, :], vcol("conv_ln_g", r), vcol("conv_ln_b", r), ALU.mult, ALU.add))
                        link.sign(V.tensor_tensor(co[:, r, :], co[:, r, :], conv_tmp[:, r, :], ALU.mult))
                dve.wait_ge(s_U, c + 1)
                V.tensor_copy(U[:, :, :, :].rearrange("p r q v -> p (r q v)"), bank[4][:, :]).then_inc(s_UV, 1)
                if c == LAST_C:
                    continue
                dve.wait_ge(s_M, c + 1)
                if c:
                    dve.wait_ge(s_Y, c + 1)
                for q in range(2):
                    ps = slice(HD * q, HD * q + HD)
                    new = bank[5][ps, :].rearrange("p (r v) -> p r v", r=RT_)[:, :, HD * q:HD * q + HD]
                    if c:
                        link.sign(V.tensor_tensor(M[ps, :, :], M[ps, :, :], new, ALU.add))
                    else:
                        link.sign(V.tensor_copy(M[ps, :, :], new))
                link.wait()
                if c == 0:
                    dve.wait_ge(s_cvar, 1)
                    dve.wait_ge(s_cd, RT_)
                    V.tensor_scalar(conv_stat[:, :], bank[0][:, :], CW * LN_EPS, None, ALU.add).then_inc(s_cvarV, 1)
                V.tensor_tensor(M[:, :, :], M[:, :, :], wide(hop[:, :, c:c + 1], [P, RT_, HD]), ALU.mult).then_inc(s_MV, 1)

    m.reset_semaphores()


def merge(nc, w, keep, mix):
    with ExitStack() as stack:
        m = Memory(nc, stack)
        p_conv, p_rwkv = m.sb("p_conv", [P, RT_, D]), m.sb("p_rwkv", [P, RT_, D])
        w_o = m.sb("w_o", [P, KD, D])
        x = m.sb("x3", [P, NT, D])
        sq = m.sb("sq3", [P, RT_, S])
        stat = m.sb("stat3", [P, S])
        headones = m.sb("headones3", [P, P])
        sums = m.sb("sums3", [P, 2, NT, 2])
        mean_sq, rstd = m.sb("mean_sq3", [P, 2, NT]), m.sb("rstd3", [P, 2, NT])
        bank = [m.bank(f"c{i}") for i in range(8)]
        co, y, gates, vec = mix.co, mix.zr[:, 0:4, :], mix.gates, keep.vec

        s_pc, s_pr, s_wo, s_x = (m.sem(f"p3_{n}_in") for n in ("p_conv", "p_rwkv", "w_o", "x"))
        s_g = m.sem("p3_head_ones")
        s_mu = m.sem("p3_sums")
        s_d = m.sem("p3_centred")
        s_sq = m.sem("p3_squared")
        s_var = m.sem("p3_square_sums")
        s_varV = m.sem("p3_variance")
        s_root = m.sem("p3_inverse_root")
        s_y = m.sem("p3_rwkv_out")
        s_p = m.sem("p3_projected")
        s_pV = m.sem("p3_projected_taken")
        s_o = m.sem("p3_out_projected")
        s_oA = m.sem("p3_out_squares")
        s_r = m.sem("p3_rstd")
        s_x1 = m.sem("p3_x1")
        s_h2 = m.sem("p3_h2")
        s_st = m.sem("p3_stored")
        s_v, s_a = m.sem("p3_vector_chain"), m.sem("p3_scalar_chain")
        block = stack.enter_context(nc.Block())

        def h2(t):
            return p_conv[:, t, :]

        def vcol(name, i=0):
            return vec[:, VEC_AT[name] + i:VEC_AT[name] + i + 1]

        @block.sync
        def _(sp):
            sp.dma_start(p_conv[:, :, :], w["p_conv"][0].rearrange("(k p) n -> p k n", p=P)).then_inc(s_pc, 16)
            sp.dma_start(p_rwkv[:, :, :], w["p_rwkv"][0].rearrange("(k p) n -> p k n", p=P)).then_inc(s_pr, 16)
            sp.dma_start(w_o[:, :, :], w["w_o"][0].rearrange("(k p) n -> p k n", p=P)).then_inc(s_wo, 16)
            sp.dma_start(x[:, :, :], w["x"][0].rearrange("(t p) d -> p t d", p=P)).then_inc(s_x, 16)
            for t in range(NT):
                sp.wait_ge(s_x1, t + 1)
                sp.dma_start(keep.x1_dram[t * P:(t + 1) * P, :], x[:, t, :]).then_inc(s_st, 16)
            for t in range(NT):
                sp.wait_ge(s_h2, t + 1)
                sp.dma_start(keep.h2_dram[t * P:(t + 1) * P, :], h2(t)).then_inc(s_st, 16)
            sp.wait_ge(s_st, 16 * 2 * NT)

        @block.gpsimd
        def _(pool):
            pool.memset(headones[:, :], 0.0).then_inc(s_g, 1)
            for q in range(2):
                pool.wait_ge(s_g, 1 + q)
                pool.memset(headones[HD * q:HD * q + HD, HD * q:HD * q + HD], 1.0).then_inc(s_g, 1)
            pool.wait_ge(s_g, 3)
            for j in range(2 * NT):
                kind, t = j % 2, j // 2
                pool.wait_ge(s_oA, j + 1)
                pool.tensor_tensor(rstd[:, kind, t:t + 1], mean_sq[:, kind, t:t + 1], keep.power[:, 0:1],
                                   ALU.pow).then_inc(s_r, 1)

        @block.scalar
        def _(act):
            link = Link(act, s_a)
            for r in range(RT_):
                act.wait_ge(s_d, r + 1)
                act.activation(sq[:, r, :], y[:, r, :], ACT.Square).then_inc(s_sq, 1)
            logs = []
            for r in range(RT_):
                act.wait_ge(s_varV, r + 1)
                logs.append(link.sign(act.activation(sq[:, r, :], sq[:, r, :], ACT.Ln)))
            for r in range(RT_):
                link.wait(logs[r])
                act.activation(sq[:, r, :], sq[:, r, :], ACT.Exp, scale=-0.5).then_inc(s_root, 1)
            for t in range(NT):
                act.wait_ge(s_o, 2 * t + 2)
                for half in range(2):
                    act.wait_ge(s_y, RT_)
                    if t or half:
                        link.wait()
                    link.sign(act.activation(stat[:, :], bank[(2 * t + half) % 4][:, :], ACT.Square,
                                             accum_out=sums[:, 0, t, half:half + 1]))
                link.wait()
                link(act.activation(mean_sq[:, 0, t:t + 1], sums[:, 0, t, 0:1], ACT.Identity, bias=sums[:, 0, t, 1:2]))
                act.activation(mean_sq[:, 0, t:t + 1], mean_sq[:, 0, t:t + 1], ACT.Copy, scale=1.0 / D,
                               bias=RMS_EPS).then_inc(s_oA, 1)
                act.wait_ge(s_x1, t + 1)
                for half in range(2):
                    link.sign(act.activation(stat[:, :], x[:, t, half * N:half * N + N], ACT.Square,
                                             accum_out=sums[:, 1, t, half:half + 1]))
                    link.wait()
                link(act.activation(mean_sq[:, 1, t:t + 1], sums[:, 1, t, 0:1], ACT.Identity, bias=sums[:, 1, t, 1:2]))
                act.activation(mean_sq[:, 1, t:t + 1], mean_sq[:, 1, t:t + 1], ACT.Copy, scale=1.0 / D,
                               bias=RMS_EPS).then_inc(s_oA, 1)

        @block.tensor
        def _(pe):
            pe.wait_ge(s_g, 3)
            for r in range(RT_):
                pe.matmul(bank[r][:, :], headones[:, :], y[:, r, :], start=True, stop=True).then_inc(s_mu, 1)

            def square_sums():
                for r in range(RT_):
                    pe.wait_ge(s_sq, r + 1)
                    pe.matmul(bank[r][:, :], headones[:, :], sq[:, r, :], start=True, stop=True).then_inc(s_var, 1)

            for j, (p_w, src, s_in, s_ready) in enumerate(((p_conv, co, s_pc, None), (p_rwkv, y, s_pr, s_y))):
                pe.wait_ge(s_in, 16)
                if s_ready:
                    pe.wait_ge(s_ready, RT_)
                for dt in range(KD):
                    n = j * KD + dt
                    if n == 2:
                        square_sums()
                    if n >= 3:
                        pe.wait_ge(s_pV, n - 2)
                    for r in range(RT_):
                        mm = pe.matmul(bank[5 + n % 3][:, :], p_w[:, r, dt * P:(dt + 1) * P], src[:, r, :],
                                       start=(r == 0), stop=(r == RT_ - 1))
                    mm.then_inc(s_p, 1)
            pe.wait_ge(s_wo, 16)
            pe.wait_ge(s_pV, 2 * KD)
            pe.wait_ge(s_varV, RT_)
            for t in range(NT):
                for half in range(2):
                    if t >= 2:
                        pe.wait_ge(s_x1, t - 1)
                    for k in range(KD):
                        mm = pe.matmul(bank[(2 * t + half) % 4][:, :], gates[:, k, t * P:(t + 1) * P],
                                       w_o[:, k, half * N:half * N + N], start=(k == 0), stop=(k == KD - 1))
                    mm.then_inc(s_o, 1)

        @block.vector
        def _(dve):
            link = Link(dve, s_v)
            V = nc.vector
            for r in range(RT_):
                dve.wait_ge(s_mu, r + 1)
                V.scalar_tensor_tensor(out=y[:, r, :], in0=bank[r][:, :], scalar=-1.0 / HD, in1=y[:, r, :],
                                       op0=ALU.mult, op1=ALU.add).then_inc(s_d, 1)

            def gate_product(n):
                dve.wait_ge(s_p, n + 1)
                gated = V.tensor_tensor(gates[:, n, :], gates[:, n, :], bank[5 + n % 3][:, :], ALU.mult)
                if n < KD:
                    gated.then_inc(s_pV, 1)
                else:
                    link(gated)
                    dve.wait_ge(s_pV, n - KD + 1)
                    V.tensor_tensor(gates[:, n - KD, :], gates[:, n - KD, :], gates[:, n, :], ALU.add).then_inc(s_pV, 1)

            for r in range(RT_):
                dve.wait_ge(s_var, r + 1)
                V.tensor_scalar(sq[:, r, :], bank[r][:, :], HD * GN_EPS, None, ALU.add).then_inc(s_varV, 1)
                if r < 3:
                    gate_product(r)
            for r in range(RT_):
                dve.wait_ge(s_root, r + 1)
                link(V.scalar_tensor_tensor(out=y[:, r, :], in0=y[:, r, :], scalar=HD ** 0.5, in1=sq[:, r, :],
                                            op0=ALU.mult, op1=ALU.mult))
                link(V.tensor_scalar(y[:, r, :], y[:, r, :], vcol("gn_g", r), vcol("gn_b", r), ALU.mult, ALU.add))
                link(V.tensor_tensor(y[:, r, :], y[:, r, :], mix.bonus[:, r, :], ALU.add))
                V.tensor_tensor(y[:, r, :], y[:, r, :], mix.gate_r[:, r, :], ALU.mult).then_inc(s_y, 1)
                if r < 3:
                    gate_product(3 + r)
            for n in range(6, 2 * KD):
                gate_product(n)
            dve.wait_ge(s_x, 16)
            for t in range(NT):
                dve.wait_ge(s_r, 2 * t + 1)
                gt, g2row, shift = keep.mod[:, 2 * D:3 * D], keep.mod[:, 4 * D:5 * D], keep.mod[:, 3 * D:4 * D]
                for half in range(2):
                    cs = slice(half * N, half * N + N)
                    link.sign(V.scalar_tensor_tensor(out=h2(t)[:, cs], in0=bank[(2 * t + half) % 4][:, :],
                                                     scalar=rstd[:, 0, t:t + 1], in1=gt[:, cs], op0=ALU.mult, op1=ALU.mult))
                link.wait()
                V.tensor_tensor(x[:, t, :], x[:, t, :], h2(t), ALU.add).then_inc(s_x1, 1)
                dve.wait_ge(s_r, 2 * t + 2)
                dve.wait_ge(s_x1, t + 1)
                link(V.scalar_tensor_tensor(out=h2(t), in0=x[:, t, :], scalar=rstd[:, 1, t:t + 1], in1=g2row,
                                            op0=ALU.mult, op1=ALU.mult))
                V.tensor_tensor(h2(t), h2(t), shift, ALU.add).then_inc(s_h2, 1)


MAXB = NE + S * TOPK // P - 1
NO_TOKEN, NO_ROW = 8 * S, 16 * S * TOPK
BIG = 1e30


def route(nc, w, keep, moe):
    with ExitStack() as stack:
        m = Memory(nc, stack)
        spare = [0]

        def old(*shape):
            size = 1
            for n in shape:
                size *= n
            spare[0] += size
            assert spare[0] <= 5 * D
            flat = keep.mod[:, spare[0] - size:spare[0]]
            names = "abc"[:len(shape)]
            if len(shape) == 1:
                return flat
            return flat.rearrange("p (%s) -> p %s" % (" ".join(names), " ".join(names)), **dict(zip(names, shape)))

        h2 = moe.xg
        h2T = m.sb("h2T", [P, KD, S])
        br = m.sb("b_router", [P, NE])
        ws = m.sb("ws", [P, 2, KD, DE])
        sig, gu = m.sb("sig4", [P, 2, DE]), m.sb("gu4", [P, 2, DE])
        hT = m.sb("hT4", [P, 2, 2, P])
        E = [P, NT, NE]
        wsd, wr, g8 = old(2, D), old(KD, NE), old(NT, NG, 8)
        scores, biased, sel, gated, left, rank, resets = (old(NT, NE) for _ in range(7))
        gs, top4, top8 = (m.sb(n, [P, NT, 8]) for n in ("gs", "top4", "top8"))
        gleft = m.sb("gleft", [P, NT, NG])
        gmask = m.sb("gmask", [P, NT, NG])
        total, over = m.sb("total", [P, NT]), m.sb("over", [P, NT])
        toki, tokf, pi, pf = m.sb("toki", [P, NT], I32), m.sb("tokf", [P, 3, NT]), m.sb("pi", [P, 1], I32), m.sb("pf", [P, 1])
        iota_i = m.sb("iota_i", [P, S], I32)
        values = m.sb("table_values", [P, NT * NE, 3])
        colf, before = m.sb("colf4", [P, P]), m.sb("before", [P, P])
        cnt, more, ends, done_, part = (old(NE) for _ in range(5))
        bf = m.sb("bf", [P, 4])
        bank = [m.bank(f"d{i}") for i in range(8)]

        s_h, s_wr, s_ws = [m.sem(f"p4_h2_{t}_in") for t in range(NT)], m.sem("p4_router_in"), m.sem("p4_shared_in")
        s_io = m.sem("p4_iotas")
        s_t, s_tA, s_tV = m.sem("p4_h2_turned"), m.sem("p4_h2T_by_scalar"), m.sem("p4_h2T_by_vector")
        s_lg, s_sc = m.sem("p4_logits"), m.sem("p4_scores")
        s_sel, s_tri = m.sem("p4_selected"), m.sem("p4_before_mask")
        s_pos, s_blk, s_blkp = m.sem("p4_places"), m.sem("p4_blocks"), m.sem("p4_blocks_turned")
        s_s, s_sA, s_sV = m.sem("p4_shared_up"), m.sem("p4_shared_sigmoid"), m.sem("p4_shared_hidden")
        s_ht, s_htA = m.sem("p4_hidden_turned"), m.sem("p4_hiddenT")
        s_dn, s_dnA = m.sem("p4_shared_down"), m.sem("p4_shared_out")
        s_v = m.sem("p4_vector_chain")
        block = stack.enter_context(nc.Block())

        @block.sync
        def _(sp):
            for t in range(NT):
                sp.dma_start(h2[:, t, :], keep.h2_dram[t * P:(t + 1) * P, :]).then_inc(s_h[t], 16)
            sp.dma_start(wr[:, :, :], w["w_router"][0].rearrange("(k p) n -> p k n", p=P)).then_inc(s_wr, 16)
            sp.dma_start(br[:, :], w["b_router"][0].rearrange("(a n) -> a n", a=1).to_broadcast([P, NE])).then_inc(s_wr, 16)
            for j, name in enumerate(("ws_gate", "ws_up")):
                sp.dma_start(ws[:, j, :, :], w[name][0].rearrange("(k p) n -> p k n", p=P)).then_inc(s_ws, 16)
            sp.dma_start(wsd[:, :, :], w["ws_down"][0].rearrange("(k p) n -> p k n", p=P)).then_inc(s_ws, 16)
            for b in range(moe.RING):
                moe.load(sp, b, b, (0, 1, 2))

        @block.gpsimd
        def _(pool):
            pool.iota(toki[:, :], [[P, NT]], base=0, channel_multiplier=1).then_inc(s_io, 1)
            pool.iota(pi[:, :], [[0, 1]], base=0, channel_multiplier=1).then_inc(s_io, 1)
            pool.iota(iota_i[:, :], [[1, S]], base=0, channel_multiplier=0).then_inc(s_io, 1)
            pool.memset(resets[:, :, :], 1.0).then_inc(s_io, 1)
            pool.memset(moe.offsets[:, 0:1], float(NO_TOKEN)).then_inc(s_io, 1)
            pool.memset(moe.offsets[:, 1:2], float(NO_ROW)).then_inc(s_io, 1)
            pool.wait_ge(s_io, 6)
            pool.memset(resets[:, :, 0:1], 0.0).then_inc(s_io, 1)

        @block.scalar
        def _(act):
            for t in range(NT):
                act.wait_ge(s_t, 2 * t + 1)
                act.activation(h2T[:, 0:4, t * P:(t + 1) * P], bank[0][:, :].rearrange("p (k s) -> p k s", k=4),
                               ACT.Copy).then_inc(s_tA, 1)
            act.wait_ge(s_lg, 1)
            act.activation(scores[:, :, :], bank[2][:, 0:NT * NE].rearrange("p (t e) -> p t e", t=NT),
                           ACT.Sigmoid).then_inc(s_sc, 1)

            def sigmoid(t):
                act.wait_ge(s_s, t + 1)
                if t >= 2:
                    act.wait_ge(s_sV, t - 1)
                act.activation(sig[:, t % 2, :], bank[4 + t % 2][:, 0:DE], ACT.Sigmoid).then_inc(s_sA, 1)

            sigmoid(0)
            for t in range(NT):
                if t < NT - 1:
                    sigmoid(t + 1)
                act.wait_ge(s_ht, t + 1)
                if t >= 2:
                    act.wait_ge(s_dn, t - 1)
                act.activation(hT[:, t % 2, :, :], bank[3][:, 0:2 * P].rearrange("p (k s) -> p k s", k=2),
                               ACT.Copy).then_inc(s_htA, 1)
                act.wait_ge(s_dn, t + 1)
                for half in range(2):
                    act.activation(moe.shared[:, t, half * N:half * N + N], bank[6 + half][:, :], ACT.Copy).then_inc(s_dnA, 1)

        @block.tensor
        def _(pe):
            for t in range(NT):
                pe.wait_ge(s_h[t], 16)
                for half in range(2):
                    if t:
                        pe.wait_ge((s_tA, s_tV)[half], t)
                    for k in range(4):
                        c0 = (half * 4 + k) * P
                        mm = pe.transpose(bank[half][:, k * P:(k + 1) * P], h2[:, t, c0:c0 + P], keep.ident[:, :])
                    mm.then_inc(s_t, 1)
            pe.wait_ge(s_wr, 32)
            pe.wait_ge(s_tA, NT)
            pe.wait_ge(s_tV, NT)
            for t in range(NT):
                for k in range(KD):
                    mm = pe.matmul(bank[2][:, t * NE:(t + 1) * NE], h2T[:, k, t * P:(t + 1) * P], wr[:, k, :],
                                   start=(k == 0), stop=(k == KD - 1))
            mm.then_inc(s_lg, 1)
            pe.wait_ge(s_ws, 48)

            def shared_up(t):
                if t >= 2:
                    pe.wait_ge(s_sV, t - 1)
                for k in range(KD):
                    mm = pe.matmul(bank[4 + t % 2][:, :], h2T[:, k, t * P:(t + 1) * P], ws[:, :, k, :],
                                   start=(k == 0), stop=(k == KD - 1))
                mm.then_inc(s_s, 1)

            def shared_down(t):
                pe.wait_ge(s_sV, t + 1)
                if t:
                    pe.wait_ge(s_htA, t)
                for k in range(2):
                    mm = pe.transpose(bank[3][:, k * P:(k + 1) * P], gu[:, t % 2, k * P:(k + 1) * P], keep.ident[:, :])
                mm.then_inc(s_ht, 1)
                pe.wait_ge(s_htA, t + 1)
                if t:
                    pe.wait_ge(s_dnA, 2 * t)
                for half in range(2):
                    for k in range(2):
                        mm = pe.matmul(bank[6 + half][:, :], hT[:, t % 2, k, :], wsd[:, k, half * N:half * N + N],
                                       start=(k == 0), stop=(k == 1))
                mm.then_inc(s_dn, 1)

            def places():
                pe.wait_ge(s_sel, 1)
                pe.wait_ge(s_tri, 1)
                for t in range(NT):
                    for u in range(t + 1):
                        pe.matmul(bank[0][:, t * NE:(t + 1) * NE], before[:, :] if u == t else keep.ones[:, :], sel[:, u, :],
                                  start=(u == 0), stop=(u == t))
                for u in range(NT):
                    mm = pe.matmul(bank[1][:, 0:NE], keep.ones[:, :], sel[:, u, :], start=(u == 0), stop=(u == NT - 1))
                mm.then_inc(s_pos, 1)

            shared_up(0)
            shared_up(1)
            shared_down(0)
            shared_up(2)
            shared_down(1)
            places()
            shared_up(3)
            shared_down(2)
            shared_down(3)
            pe.wait_ge(s_blk, 1)
            for j in range(2):
                mm = pe.matmul(bank[2][0:1, j * P:(j + 1) * P], bf[:, j:j + 1], keep.ident[:, :], start=True, stop=True)
            mm.then_inc(s_blkp, 1)

        @block.vector
        def _(dve):
            link = Link(dve, s_v)
            V = nc.vector

            def hidden(t):
                dve.wait_ge(s_sA, t + 1)
                link(V.tensor_tensor(sig[:, t % 2, :], sig[:, t % 2, :], bank[4 + t % 2][:, 0:DE], ALU.mult))
                if t >= 2:
                    dve.wait_ge(s_ht, t - 1)
                V.tensor_tensor(gu[:, t % 2, :], sig[:, t % 2, :], bank[4 + t % 2][:, DE:2 * DE], ALU.mult).then_inc(s_sV, 1)

            dve.wait_ge(s_io, 7)
            link.sign(V.tensor_copy(tokf[:, 0, :], toki[:, :]))
            link.sign(V.tensor_copy(pf[:, :], pi[:, :]))
            link.sign(V.tensor_copy(moe.iota[:, :], iota_i[:, :]))
            link(V.tensor_copy(colf[:, :], iota_i[:, 0:P]))
            V.tensor_scalar(before[:, :], colf[:, :], pf[:, 0:1], None, ALU.is_gt).then_inc(s_tri, 1)
            link.sign(V.tensor_scalar(tokf[:, 1, :], tokf[:, 0, :], float(-NO_TOKEN), None, ALU.add))
            link.sign(V.tensor_scalar(tokf[:, 2, :], tokf[:, 0, :], float(TOPK), float(-NO_ROW), ALU.mult, ALU.add))
            for t in range(NT):
                dve.wait_ge(s_t, 2 * t + 2)
                V.tensor_copy(h2T[:, 4:8, t * P:(t + 1) * P],
                              bank[1][:, :].rearrange("p (k s) -> p k s", k=4)).then_inc(s_tV, 1)
            dve.wait_ge(s_sc, 1)
            dve.wait_ge(s_wr, 32)
            link(V.tensor_tensor(biased[:, :, :], scores[:, :, :], br[:, :].unsqueeze(1).to_broadcast(E), ALU.add))
            hidden(0)
            for t in range(NT):
                for g in range(NG):
                    link.sign(V.max(g8[:, t, g, :], biased[:, t, g * PER:(g + 1) * PER]))
            link.wait()
            link(V.tensor_tensor(gs[:, :, :], g8[:, :, :, 0], g8[:, :, :, 1], ALU.add))
            for t in range(NT):
                link.sign(V.max(top4[:, t, :], gs[:, t, :]))
            link.wait()
            hidden(1)
            link(V.tensor_scalar(top4[:, :, TOPG:], top4[:, :, TOPG:], 0.0, -4.0 * BIG, ALU.mult, ALU.add))
            for t in range(NT):
                link.sign(V.match_replace(out=gleft[:, t, :], in_to_replace=top4[:, t, :], in_values=gs[:, t, :],
                                          imm_value=-2.0 * BIG))
            link.wait()
            link(V.tensor_tensor(gmask[:, :, :], gleft[:, :, :], gs[:, :, :], ALU.is_lt))
            link(V.tensor_scalar(gmask[:, :, :], gmask[:, :, :], -1.0, BIG, ALU.add, ALU.mult))
            for t in range(NT):
                link.sign(V.tensor_tensor(biased[:, t, :].rearrange("p (g m) -> p g m", g=NG),
                                          biased[:, t, :].rearrange("p (g m) -> p g m", g=NG),
                                          gmask[:, t, :].unsqueeze(2).to_broadcast([P, NG, PER]), ALU.add))
            link.wait()
            for t in range(NT):
                link.sign(V.max(top8[:, t, :], biased[:, t, :]))
            link.wait()
            for t in range(NT):
                link.sign(V.match_replace(out=left[:, t, :], in_to_replace=top8[:, t, :], in_values=biased[:, t, :],
                                          imm_value=-2.0 * BIG))
            link.wait()
            V.tensor_tensor(sel[:, :, :], left[:, :, :], biased[:, :, :], ALU.is_lt).then_inc(s_sel, 1)
            dve.wait_ge(s_sel, 1)
            link(V.tensor_tensor(gated[:, :, :], scores[:, :, :], sel[:, :, :], ALU.mult))
            link(V.tensor_reduce(total[:, :], gated[:, :, :], AX.X, ALU.add))
            hidden(2)
            link(V.reciprocal(over[:, :], total[:, :]))
            for t in range(NT):
                link.sign(V.tensor_scalar(values[:, t * NE:(t + 1) * NE, 0], gated[:, t, :], over[:, t:t + 1], SCALE, ALU.mult, ALU.mult))
                link.sign(V.tensor_scalar(values[:, t * NE:(t + 1) * NE, 1], sel[:, t, :], 0.0, tokf[:, 1, t:t + 1], ALU.mult, ALU.add))
            link(V.tensor_tensor_scan(rank[:, :, :].rearrange("p t e -> p (t e)"), resets[:, :, :].rearrange("p t e -> p (t e)"),
                                      sel[:, :, :].rearrange("p t e -> p (t e)"), 0.0, ALU.mult, ALU.add))
            link(V.tensor_tensor(rank[:, :, :], rank[:, :, :], sel[:, :, :], ALU.subtract))
            for t in range(NT):
                link.sign(V.tensor_scalar(values[:, t * NE:(t + 1) * NE, 2], rank[:, t, :], tokf[:, 2, t:t + 1], None, ALU.add))
            link.wait()
            whole, parts = values[:, :, :], moe.parts[:, :, :, :, :].rearrange("p t e v j -> p (t e) v j")
            for j in range(3):
                link(V.tensor_copy(parts[:, :, :, j], whole))
                if j < 2:
                    link(V.tensor_tensor(whole, whole, parts[:, :, :, j], ALU.subtract))
            hidden(3)
            dve.wait_ge(s_pos, 1)
            link(V.tensor_scalar(left[:, :, :], sel[:, :, :], -1.0, 4.0 * S, ALU.add, ALU.mult))
            link.sign(V.tensor_tensor(moe.place[:, :, :], left[:, :, :],
                                      bank[0][:, 0:NT * NE].rearrange("p (t e) -> p t e", t=NT), ALU.add))
            link(V.tensor_copy(cnt[:, :], bank[1][:, 0:NE]))
            link(V.tensor_scalar(more[:, :], cnt[:, :], float(P), None, ALU.is_gt))
            for j in range(2, NT):
                link(V.tensor_scalar(part[:, :], cnt[:, :], float(j * P), None, ALU.is_gt))
                link(V.tensor_tensor(more[:, :], more[:, :], part[:, :], ALU.add))
            link(V.tensor_tensor_scan(ends[:, :], keep.ones[:, 0:NE], more[:, :], float(NE), ALU.mult, ALU.add))
            link(V.tensor_copy(moe.n_blocks[0:1, :], ends[0:1, NE - 1:NE]))
            link(V.tensor_scalar(done_[:, :], ends[:, :], pf[:, 0:1], None, ALU.is_le))
            link(V.tensor_tensor(part[:, :], done_[:, :], more[:, :], ALU.mult))
            link(V.tensor_reduce(bf[:, 2:3], done_[:, :], AX.X, ALU.add))
            link(V.tensor_reduce(bf[:, 3:4], part[:, :], AX.X, ALU.add))
            link(V.tensor_scalar(bf[:, 3:4], bf[:, 3:4], -1.0, pf[:, 0:1], ALU.mult, ALU.add))
            link(V.tensor_scalar(bf[:, 3:4], bf[:, 3:4], float(1 - NE), float(P), ALU.add, ALU.mult))
            link(V.tensor_scalar(bf[:, 2:3], bf[:, 2:3], float(NE - 1), None, ALU.min))
            link(V.tensor_scalar(part[:, 0:1], pf[:, :], float(NE), None, ALU.is_lt))
            link(V.tensor_scalar(bf[:, 3:4], bf[:, 3:4], 0.0, float(S - P), ALU.max, ALU.min))
            link(V.tensor_scalar(part[:, 1:2], part[:, 0:1], -1.0, 1.0, ALU.mult, ALU.add))
            link(V.tensor_tensor(bf[:, 1:2], bf[:, 3:4], part[:, 1:2], ALU.mult))
            link(V.tensor_tensor(bf[:, 2:3], bf[:, 2:3], part[:, 1:2], ALU.mult))
            link(V.tensor_tensor(part[:, 2:3], pf[:, :], part[:, 0:1], ALU.mult))
            V.tensor_tensor(bf[:, 0:1], bf[:, 2:3], part[:, 2:3], ALU.add).then_inc(s_blk, 1)
            dve.wait_ge(s_blkp, 1)
            link(V.tensor_copy(moe.blocks[0:1, :, :].rearrange("p a b -> p (a b)"), bank[2][0:1, 0:2 * P]))


def plan_experts(nc, m, w, keep, moe):
    moe.RING = 4
    moe.ring = m.sb("expert_ring", [P, moe.RING, 3 * KD * DE])
    moe.place = m.sb("place", [P, NT, NE])
    moe.parts = m.sb("table_parts", [P, NT, NE, 3, 3], BF16)
    moe.iota = m.sb("iota", [P, S])
    moe.xg = m.sb("xg", [P, 4, D])
    moe.blocks = m.sb("blocks", [1, 2, P], I32)
    moe.n_blocks = m.sb("n_blocks", [1, 1], I32)
    moe.offsets = m.sb("offsets", [P, 2])
    moe.s_up_in = [m.sem(f"expert_gate_up{i}_in") for i in range(moe.RING)]
    moe.s_down_in = [m.sem(f"expert_down{i}_in") for i in range(moe.RING)]
    moe.rows = nc.dram_tensor("expert_rows", (S * TOPK, D), F32, kind="Internal").ap()
    width = KD * DE
    parts = [w["we_gate"][0].rearrange("e (p k) n -> e p (k n)", k=KD),
             w["we_up"][0].rearrange("e (p k) n -> e p (k n)", k=KD),
             w["we_down"][0].rearrange("e (p k) n -> e p (k n)", k=2)]

    def load(engine, expert, slot, kinds):
        for j in kinds:
            source = parts[j][expert] if isinstance(expert, int) else parts[j][bass.ds(expert, 1)].rearrange("a p n -> (a p) n")
            done = (moe.s_up_in, moe.s_up_in, moe.s_down_in)[j][slot]
            engine.dma_start(moe.ring[:, slot, j * width:(j + 1) * width], source).then_inc(done, 16)

    moe.load = load


def experts(nc, w, keep, moe):
    with ExitStack() as stack:
        m = Memory(nc, stack)
        RING = moe.RING
        hot = m.sb("hot", [P, 2, NT, P], BF16)
        column = m.sb("column", [P, 2, NT, 9], BF16)
        place = m.sb("place_column", [P, 2, NT])
        number = m.sb("number", [P, 4, 3])
        tokens = m.sb("tokens", [P, 4, 1], U32)
        row_ids = m.sb("row_ids", [P, 4, 1], U32)
        xT = m.sb("xT", [P, 2, KD, P])
        sig = m.sb("sig5", [P, 2, DE])
        hid = m.sb("hid", [P, 2, DE])
        hT = m.sb("hT5", [P, 2, 2, P])
        y = m.sb("y5", [P, 4, D])
        carrier = m.sb("carrier", [1, 2])
        px = [m.bank(f"px{i}") for i in range(2)]
        pg, pu = m.bank("p_gate", [P, DE]), m.bank("p_up", [P, DE])
        py = [m.bank(f"py{i}") for i in range(2)]
        ph, pid = m.bank("ph"), m.bank("pid")

        s_gather, s_scatter = m.sem("p5_gather_may_start"), m.sem("p5_scatter_may_start")
        s_col, s_hot = m.sem("p5_column"), m.sem("p5_one_hot")
        s_id = m.sem("p5_numbers_product")
        s_sum = m.sem("p5_numbers_whole")
        s_num, s_rows = m.sem("p5_token_numbers"), m.sem("p5_row_numbers")
        s_xg = [m.sem(f"p5_gathered{i}") for i in range(4)]
        s_x = m.sem("p5_x_turned")
        s_xA, s_xV = m.sem("p5_xT_by_scalar"), m.sem("p5_xT_by_vector")
        s_pg, s_gu = m.sem("p5_gate_product"), m.sem("p5_up")
        s_sig, s_t, s_hid = m.sem("p5_sigmoid"), m.sem("p5_silu"), m.sem("p5_hidden")
        s_h, s_hA = m.sem("p5_hidden_turned"), m.sem("p5_hiddenT")
        s_y, s_yA, s_yV = m.sem("p5_down"), m.sem("p5_y_by_scalar"), m.sem("p5_y_by_vector")
        s_x1 = m.sem("p5_x1_in")
        s_out = [m.sem(f"p5_scattered{i}") for i in range(4)]
        block = stack.enter_context(nc.Block())
        MAIN = NE - 4
        STEPS = (MAXB + 3) // 4 * 4

        def steps(engine, stages, last=None):
            most = max(lead for lead, _ in stages)
            for i in range(-most, 4):
                for lead, code in stages:
                    if i + lead >= 0 and (i >= 0 or i + lead < lead):
                        code(i + lead, i + lead, True)
            with engine.Fori(1, MAIN // 4) as turn:
                for u in range(4):
                    for lead, code in stages:
                        code(4 * turn + (u + lead), u + lead, True)
            count = engine.value_load(moe.n_blocks[0:1, 0:1], min_val=NE, max_val=MAXB)
            with engine.Fori(MAIN // 4, STEPS // 4) as turn:
                with engine.If(4 * turn < count):
                    for u in range(4):
                        for lead, code in stages:
                            with engine.If(4 * turn + (u + lead) < count):
                                code(4 * turn + (u + lead), u + lead, False)
                                if last is not None and lead == 0:
                                    last(4 * turn + u, u)

        def taken(engine, semaphore, b, back):
            if isinstance(b, int) and b < back:
                return
            engine.wait_ge(semaphore, b - back + 1)

        def slot_done(engine, semaphores, b, u, per):
            if isinstance(b, int):
                engine.wait_ge(semaphores[b % 4], per * (b // 4 + 1))
            else:
                engine.wait_ge(semaphores[u % 4], per // 4 * b + (per - per // 4 * (u % 4)))

        def left(engine, b, u):
            if isinstance(b, int) and b < 4:
                return
            slot_done(engine, s_out, b - 4, u % 4, 16)

        @block.sync
        def _(sp):
            with sp.Fori(1, NE // RING) as turn:
                for u in range(RING):
                    sp.wait_ge(s_gu, RING * turn + (u - RING + 1))
                    moe.load(sp, RING * turn + u, u, (0, 1))
                    sp.wait_ge(s_y, RING * turn + (u - RING + 1))
                    moe.load(sp, RING * turn + u, u, (2,))
            count = sp.value_load(moe.n_blocks[0:1, 0:1], min_val=NE, max_val=MAXB)
            with sp.Fori(NE // RING, STEPS // RING) as turn:
                with sp.If(RING * turn < count):
                    for u in range(RING):
                        with sp.If(RING * turn + u < count):
                            expert = sp.value_load(moe.blocks[0:1, 0, bass.ds(RING * turn + u, 1)], min_val=0, max_val=NE - 1)
                            sp.wait_ge(s_gu, RING * turn + (u - RING + 1))
                            moe.load(sp, expert, u, (0, 1))
                            sp.wait_ge(s_y, RING * turn + (u - RING + 1))
                            moe.load(sp, expert, u, (2,))
            sp.dma_start(moe.x1[:, :, :], keep.x1_dram.rearrange("(t p) d -> p t d", p=P)).then_inc(s_x1, 16)
            sp.wait_ge(s_x1, 16)

        @block.gpsimd
        def _(pool):
            last_token, last_row = pool.to_reg(S - 1), pool.to_reg(S * TOPK - 1)

            def carry_wait(semaphore, b, place):
                taken(pool, semaphore, b, 1)
                nc.gpsimd.tensor_tensor(carrier[0:1, place:place + 1], moe.offsets[0:1, 0:1], moe.offsets[0:1, 0:1],
                                        ALU.add).then_inc(semaphore, 1)

            def gather(b, u, first):
                pool.wait_ge(s_num, b + 1)
                taken(pool, s_x, b, 4)
                carry_wait(s_gather, b, 0)
                pool.indirect_dma_start(moe.xg[:, u % 4, :], None, keep.h2_dram,
                                        bass.IndirectOffsetOnAxis(tokens[:, u % 4, 0:1], 0),
                                        bounds_check=last_token, oob_is_err=False).then_inc(s_xg[u % 4], 16)

            def scatter(b, u, first):
                pool.wait_ge(s_rows, b + 1)
                pool.wait_ge(s_yA, b + 1)
                pool.wait_ge(s_yV, b + 1)
                carry_wait(s_scatter, b, 1)
                pool.indirect_dma_start(moe.rows, bass.IndirectOffsetOnAxis(row_ids[:, u % 4, 0:1], 0), y[:, u % 4, :], None,
                                        bounds_check=last_row, oob_is_err=False).then_inc(s_out[u % 4], 16)

            steps(pool, [(4, gather), (0, scatter)], lambda b, u: slot_done(pool, s_out, b, u, 16))

        @block.scalar
        def _(act):
            def sigmoid(b, u, first):
                act.wait_ge(s_pg, b + 1)
                taken(act, s_hid, b, 2)
                act.activation(sig[:, u % 2, :], pg[:, :], ACT.Sigmoid).then_inc(s_sig, 1)

            def xT_half(b, u, first):
                act.wait_ge(s_x, b + 1)
                taken(act, s_gu, b, 2)
                act.activation(xT[:, u % 2, 0:4, :], px[0][:, :].rearrange("p (k s) -> p k s", k=4), ACT.Copy).then_inc(s_xA, 1)

            def hiddenT(b, u, first):
                act.wait_ge(s_h, b + 1)
                taken(act, s_y, b, 2)
                act.activation(hT[:, u % 2, :, :], ph[:, 0:2 * P].rearrange("p (k s) -> p k s", k=2), ACT.Copy).then_inc(s_hA, 1)

            def y_half(b, u, first):
                act.wait_ge(s_y, b + 1)
                left(act, b, u)
                act.activation(y[:, u % 4, 0:N], py[0][:, :], ACT.Copy).then_inc(s_yA, 1)

            steps(act, [(1, sigmoid), (0, hiddenT), (2, xT_half), (0, y_half)])

        @block.tensor
        def _(pe):
            def gate_up(j):
                bank, read, done = ((pg, s_t, s_pg), (pu, s_hid, s_gu))[j]

                def code(b, u, first):
                    if j == 0:
                        slot_done(pe, moe.s_up_in, b, u, 32)
                        pe.wait_ge(s_xA, b + 1)
                        pe.wait_ge(s_xV, b + 1)
                    taken(pe, read, b, 1)
                    weights = moe.ring[:, u % RING, 0:2 * KD * DE].rearrange("p (j k n) -> p j k n", j=2, k=KD)
                    for k in range(KD):
                        mm = pe.matmul(bank[:, :], xT[:, u % 2, k, :], weights[:, j, k, :], start=(k == 0), stop=(k == KD - 1))
                    mm.then_inc(done, 1)

                return code

            def turn_x(b, u, first):
                slot_done(pe, s_xg, b, u, 16)
                taken(pe, s_xA, b, 1)
                taken(pe, s_xV, b, 1)
                rows = moe.xg[:, u % 4, :].rearrange("p (d k) -> p k d", k=KD)
                for k in range(KD):
                    mm = pe.transpose(px[k // 4][:, (k % 4) * P:(k % 4 + 1) * P], rows[:, k, :], keep.ident[:, :])
                mm.then_inc(s_x, 1)

            def turn_hidden(b, u, first):
                pe.wait_ge(s_hid, b + 1)
                taken(pe, s_hA, b, 1)
                rows = hid[:, u % 2, :].rearrange("p (d k) -> p k d", k=2)
                for k in range(2):
                    mm = pe.transpose(ph[:, k * P:(k + 1) * P], rows[:, k, :], keep.ident[:, :])
                mm.then_inc(s_h, 1)

            def numbers(b, u, first):
                pe.wait_ge(s_hot, b + 1)
                taken(pe, s_num, b, 1)
                for t in range(NT):
                    mm = pe.matmul(pid[:, 0:9], hot[:, u % 2, t, :], column[:, u % 2, t, :], start=(t == 0), stop=(t == NT - 1))
                mm.then_inc(s_id, 1)

            def down(b, u, first):
                slot_done(pe, moe.s_down_in, b, u, 16)
                pe.wait_ge(s_hA, b + 1)
                taken(pe, s_yA, b, 1)
                taken(pe, s_yV, b, 1)
                weights = moe.ring[:, u % RING, 2 * KD * DE:3 * KD * DE].rearrange("p (k n) -> p k n", k=2)
                for half in range(2):
                    for k in range(2):
                        mm = pe.matmul(py[half][:, :], hT[:, u % 2, k, :], weights[:, k, half * N:half * N + N],
                                       start=(k == 0), stop=(k == 1))
                mm.then_inc(s_y, 1)

            steps(pe, [(1, gate_up(0)), (0, turn_hidden), (1, gate_up(1)), (2, turn_x), (4, numbers), (0, down)])

        @block.vector
        def _(dve):
            V = nc.vector

            def silu(b, u, first):
                dve.wait_ge(s_sig, b + 1)
                V.scalar_tensor_tensor(out=sig[:, u % 2, :], in0=pg[:, :], scalar=number[:, u % 4, 0:1], in1=sig[:, u % 2, :],
                                       op0=ALU.mult, op1=ALU.mult).then_inc(s_t, 1)

            def hidden(b, u, first):
                dve.wait_ge(s_gu, b + 1)
                dve.wait_ge(s_t, b + 1)
                taken(dve, s_h, b, 2)
                V.tensor_tensor(hid[:, u % 2, :], sig[:, u % 2, :], pu[:, :], ALU.mult).then_inc(s_hid, 1)

            def xT_half(b, u, first):
                dve.wait_ge(s_x, b + 1)
                taken(dve, s_gu, b, 2)
                V.tensor_copy(xT[:, u % 2, 4:8, :], px[1][:, :].rearrange("p (k s) -> p k s", k=4)).then_inc(s_xV, 1)

            def numbers(b, u, first):
                dve.wait_ge(s_id, b + 1)
                taken(dve, s_x, b, 4)
                V.tensor_reduce(number[:, u % 4, :], pid[:, 0:9].rearrange("p (v j) -> p v j", j=3), AX.X, ALU.add).then_inc(s_sum, 1)
                dve.wait_ge(s_sum, b + 1)
                V.tensor_tensor(tokens[:, u % 4, :], number[:, u % 4, 1:2], moe.offsets[:, 0:1], ALU.add).then_inc(s_num, 1)

            def row_numbers(b, u, first):
                dve.wait_ge(s_num, b + 1)
                left(dve, b, u)
                V.tensor_tensor(row_ids[:, u % 4, :], number[:, u % 4, 2:3], moe.offsets[:, 1:2], ALU.add).then_inc(s_rows, 1)

            def places(b, u, first):
                expert, start = b, 0
                if not first:
                    expert = dve.value_load(moe.blocks[0:1, 0, bass.ds(b, 1)], min_val=0, max_val=NE - 1)
                    start = dve.value_load(moe.blocks[0:1, 1, bass.ds(b, 1)], min_val=0, max_val=S - P)
                taken(dve, s_id, b, 2)
                V.tensor_copy(place[:, u % 2, :].unsqueeze(2), moe.place[:, :, bass.ds(expert, 1)]).then_inc(s_col, 1)
                V.tensor_copy(column[:, u % 2, :, :].unsqueeze(2),
                              moe.parts[:, :, bass.ds(expert, 1), :, :].rearrange("p t e v j -> p t e (v j)"))
                dve.wait_ge(s_col, b + 1)
                for t in range(NT):
                    last = V.tensor_scalar(hot[:, u % 2, t, :], moe.iota[:, bass.ds(start, P)], place[:, u % 2, t:t + 1], None,
                                           ALU.is_equal)
                last.then_inc(s_hot, 1)

            def y_half(b, u, first):
                dve.wait_ge(s_y, b + 1)
                left(dve, b, u)
                V.tensor_copy(y[:, u % 4, N:2 * N], py[1][:, :]).then_inc(s_yV, 1)

            steps(dve, [(1, silu), (4, places), (1, hidden), (2, xT_half), (4, numbers), (1, row_numbers), (0, y_half)])


def combine(nc, w, keep, moe, out):
    with ExitStack() as stack:
        m = Memory(nc, stack)
        rows = m.sb("rows6", [P, 4, TOPK, N])
        x1 = moe.x1
        y = m.sb("y6", [P, 2, D])
        sq = m.sb("sq6", [P, D])
        sums, mean_sq, rstd = m.sb("sums6", [P, NT]), m.sb("mean_sq6", [P, NT]), m.sb("rstd6", [P, NT])
        s_red, s_y, s_sq, s_r, s_o, s_st = (m.sem(f"p6_{n}") for n in ("reduced", "y", "squares", "rstd", "out", "stored"))
        s_v, s_a = m.sem("p6_vector_chain"), m.sem("p6_scalar_chain")
        s_in = [m.sem(f"p6_rows{i}_in") for i in range(4)]
        block = stack.enter_context(nc.Block())
        expert_rows = moe.rows.rearrange("(t p j) d -> t p j d", p=P, j=TOPK)

        @block.sync
        def _(sp):
            for n in range(2 * NT):
                t, half = n // 2, n % 2
                if n >= 4:
                    sp.wait_ge(s_red, n - 3)
                sp.dma_start(rows[:, n % 4, :, :], expert_rows[t][:, :, half * N:half * N + N]).then_inc(s_in[n % 4], 16)
            for t in range(NT):
                sp.wait_ge(s_o, t + 1)
                sp.dma_start(out[0, t * P:(t + 1) * P, :], x1[:, t, :]).then_inc(s_st, 16)
            sp.wait_ge(s_st, 16 * NT)

        @block.gpsimd
        def _(pool):
            for t in range(NT):
                pool.wait_ge(s_sq, t + 1)
                pool.tensor_tensor(rstd[:, t:t + 1], mean_sq[:, t:t + 1], keep.power[:, 0:1], ALU.pow).then_inc(s_r, 1)

        @block.scalar
        def _(act):
            link = Link(act, s_a)
            for t in range(NT):
                act.wait_ge(s_y, t + 1)
                link(act.activation(sq[:, :], y[:, t % 2, :], ACT.Square, accum_out=sums[:, t:t + 1]))
                act.activation(mean_sq[:, t:t + 1], sums[:, t:t + 1], ACT.Copy, scale=1.0 / D, bias=RMS_EPS).then_inc(s_sq, 1)

        @block.vector
        def _(dve):
            link = Link(dve, s_v)
            V = nc.vector
            gt = keep.mod[:, 5 * D:6 * D]

            def finish(t):
                dve.wait_ge(s_r, t + 1)
                link(V.scalar_tensor_tensor(out=y[:, t % 2, :], in0=y[:, t % 2, :], scalar=rstd[:, t:t + 1], in1=gt,
                                            op0=ALU.mult, op1=ALU.mult))
                V.tensor_tensor(x1[:, t, :], x1[:, t, :], y[:, t % 2, :], ALU.add).then_inc(s_o, 1)

            for t in range(NT):
                if t >= 2:
                    dve.wait_ge(s_o, t - 1)
                for n in (2 * t, 2 * t + 1):
                    dve.wait_ge(s_in[n % 4], 16 * (n // 4 + 1))
                    V.tensor_reduce(y[:, t % 2, n % 2 * N:(n % 2 + 1) * N], rows[:, n % 4, :, :].rearrange("p j d -> p d j"),
                                    AX.X, ALU.add).then_inc(s_red, 1)
                dve.wait_ge(s_red, 2 * t + 2)
                V.tensor_tensor(y[:, t % 2, :], y[:, t % 2, :], moe.shared[:, t, :], ALU.add).then_inc(s_y, 1)
                if t:
                    finish(t - 1)
            finish(NT - 1)


class Names:
    pass


def layer(nc, w, out):
    with ExitStack() as stack:
        m = Memory(nc, stack)
        keep = Names()
        keep.mod = m.sb("mod", [P, 6 * D])
        keep.ident = m.sb("ident", [P, P])
        keep.ones = m.sb("ones", [P, P])
        keep.power = m.sb("power", [P, 8])
        keep.vec = m.sb("vec", [P, N_VEC])
        keep.one_minus_mu = m.sb("one_minus_mu", [P, NZ_RWKV])
        keep.silu_c = m.sb("silu_c", [P, KD])
        keep.x1_dram = nc.dram_tensor("x1_rows", (S, D), F32, kind="Internal").ap()
        keep.h2_dram = nc.dram_tensor("h2_rows", (S, D), F32, kind="Internal").ap()
        with ExitStack() as mix_stack:
            mm = Memory(nc, mix_stack)
            mix = Names()
            mix.gates = mm.sb("gates", [P, NZ_GATE, S])
            mix.zr = mm.sb("zr", [P, NZ_RWKV, S])
            mix.co = mm.sb("co", [P, RT_, S])
            mix.taps = mm.sb("taps", [P, N_TAP])
            project(nc, w, keep, mix)
            mix.gate_r = mm.sb("gate_r", [P, RT_, S])
            mix.bonus = mm.sb("bonus", [P, RT_, S])
            rwkv(nc, w, keep, mix)
            merge(nc, w, keep, mix)
        moe = Names()
        moe.shared = m.sb("shared", [P, NT, D])
        moe.x1 = keep.mod[:, 0:4 * D].rearrange("p (t d) -> p t d", t=NT)
        with ExitStack() as moe_stack:
            me = Memory(nc, moe_stack)
            plan_experts(nc, me, w, keep, moe)
            route(nc, w, keep, moe)
            experts(nc, w, keep, moe)
        combine(nc, w, keep, moe, out)


_INS = ["x", "c", "w_ada", "b_ada", "norm_mix_pre", "norm_mix_post", "norm_ffn_pre", "norm_ffn_post", "w_in",
        "mu_shift", "conv_w", "conv_b", "conv_ln_g", "conv_ln_b", "p_conv", "w0", "w2", "a0", "a2", "g2", "k_k",
        "k_a", "r_k", "gn_g", "gn_b", "p_rwkv", "w_o", "w_router", "b_router", "we_gate", "we_up", "we_down",
        "ws_gate", "ws_up", "ws_down"]


def kernel(**inputs):
    import numpy as np
    import concourse.bacc as bacc
    from concourse.bass_utils import run_bass_kernel_spmd

    nc = bacc.Bacc("TRN2", target_bir_lowering=False, num_devices=1)
    arrays, w = {}, {}
    for name in _INS:
        a = np.ascontiguousarray(inputs[name])
        arrays[f"in_{name}"] = a
        w[name] = nc.dram_tensor(f"in_{name}", a.shape, mybir.dt.from_np(a.dtype), kind="ExternalInput").ap()
    out = nc.dram_tensor("out_rows", (1, S, D), F32, kind="ExternalOutput").ap()
    layer(nc, w, out)
    result = run_bass_kernel_spmd(nc, [arrays], core_ids=[0])
    return result.results[0]["out_rows"]
```
